# Optimizing a Trainium2 kernel written in Bass

```python
import jax, jax.numpy as jnp
from jax import lax
import numpy as np

D_MODEL = 1024
BATCH = 1
SEQ = 512
DEPTH = 1

N_META = 16
GRID_W = 64
NA_WIN_ROWS = 8
NA_WIN_COLS = 16
NA_HEADS = 8
NA_HEAD_DIM = 64
NA_WIDTH = NA_HEADS * NA_HEAD_DIM
GLA_HEADS = 4
GLA_DK = 64
GLA_DV = 128
GLA_KW = GLA_HEADS * GLA_DK
GLA_VW = GLA_HEADS * GLA_DV
GLA_GATE_RANK = 16
GLA_GATE_TAU = 16.0
GLA_CHUNK = 64
MIX_WIDTH = NA_WIDTH + GLA_VW
IN_COLS = 3 * NA_WIDTH + 2 * GLA_KW + 2 * GLA_VW + 2 * GLA_GATE_RANK
D_FF = 2816
CONV_W = 3
RMS_EPS = 1e-6


def rmsnorm(x, g):
    xf = x.astype(jnp.float32)
    y = xf * lax.rsqrt(jnp.mean(xf * xf, axis=-1, keepdims=True) + RMS_EPS)
    return (y * g.astype(jnp.float32)).astype(x.dtype)

def neighbourhood_attention(q, k, v, rpb):
    B, L, H, dh = q.shape
    T = L - N_META
    W = GRID_W
    R = T // W
    kh = min(NA_WIN_ROWS, R)
    kw = NA_WIN_COLS
    q = q * (dh ** -0.5)
    qm, km, vm = q[:, :N_META], k[:, :N_META], v[:, :N_META]

    def grid(t):
        return t[:, N_META:].reshape(B, R, W, H, dh).transpose(0, 3, 1, 2, 4)

    qg, kg, vg = grid(q), grid(k), grid(v)
    rs = jnp.clip(jnp.arange(R) - kh // 2, 0, R - kh)
    row_idx = rs[:, None] + jnp.arange(kh)[None, :]
    k_rows = kg[:, :, row_idx]
    v_rows = vg[:, :, row_idx]
    cq = jnp.arange(W)
    cs = jnp.clip(cq - kw // 2, 0, W - kw)
    in_win = (cq[None, :] >= cs[:, None]) & (cq[None, :] < cs[:, None] + kw)
    dr = row_idx - jnp.arange(R)[:, None] + (NA_WIN_ROWS - 1)
    dc = jnp.clip(cq[None, :] - cq[:, None], -(kw - 1), kw - 1) + (NA_WIN_COLS - 1)
    bias = rpb[:, dr[:, None, :, None], dc[None, :, None, :]]

    s_loc = jnp.einsum('bhrcd,bhrikd->bhrcik', qg, k_rows).astype(jnp.float32) + bias.astype(jnp.float32)
    s_loc = jnp.where(in_win[:, None, :], s_loc, -jnp.inf)
    s_meta = jnp.einsum('bhrcd,bmhd->bhrcm', qg, km).astype(jnp.float32)
    s_all = jnp.concatenate([s_loc.reshape(B, H, R, W, kh * W), s_meta], axis=-1)
    p = jax.nn.softmax(s_all, axis=-1).astype(v.dtype)
    p_loc = p[..., :kh * W].reshape(B, H, R, W, kh, W)
    p_meta = p[..., kh * W:]
    og = (jnp.einsum('bhrcik,bhrikd->bhrcd', p_loc, v_rows)
          + jnp.einsum('bhrcm,bmhd->bhrcd', p_meta, vm))
    og = og.transpose(0, 2, 3, 1, 4).reshape(B, T, H * dh)
    sm = jnp.einsum('bqhd,bkhd->bhqk', qm, km).astype(jnp.float32)
    pm = jax.nn.softmax(sm, axis=-1).astype(v.dtype)
    om = jnp.einsum('bhqk,bkhd->bqhd', pm, vm).reshape(B, N_META, H * dh)
    return jnp.concatenate([om, og], axis=1)

def gla_chunked(q, k, v, log_a, strict):
    C = q.shape[-2]
    b = jnp.cumsum(log_a, axis=-2)
    b_last = b[..., -1:, :]
    q_dec = q * jnp.exp(b)
    k_inv = k * jnp.exp(-b)
    k_end = k * jnp.exp(b_last - b)
    mask = jnp.tril(jnp.ones((C, C), dtype=bool), k=-1 if strict else 0)
    a = jnp.where(mask, jnp.einsum('bhncd,bhnsd->bhncs', q_dec, k_inv), 0.0)
    o = jnp.einsum('bhncs,bhnse->bhnce', a, v)
    ds = jnp.einsum('bhncd,bhnce->nbhde', k_end, v)
    decay = jnp.exp(b_last[..., 0, :]).transpose(2, 0, 1, 3)

    def step(s, inp):
        dec, d = inp
        return dec[..., None] * s + d, s

    s0 = jnp.zeros(ds.shape[1:], ds.dtype)
    _, s_prev = lax.scan(step, s0, (decay, ds))
    return o + jnp.einsum('bhncd,nbhde->bhnce', q_dec, s_prev)

def gla_bidirectional(q, k, v, g, z, up_f, bias_f, up_b, bias_b, out_gain):
    B, L, _ = q.shape
    H, dk, dv, C = GLA_HEADS, GLA_DK, GLA_DV, GLA_CHUNK
    f32 = jnp.float32
    pad = (-N_META) % C
    Lp = L + pad
    N = Lp // C
    la_f = jax.nn.log_sigmoid((z[..., :GLA_GATE_RANK] @ up_f + bias_f).astype(f32)) / GLA_GATE_TAU
    la_b = jax.nn.log_sigmoid((z[..., GLA_GATE_RANK:] @ up_b + bias_b).astype(f32)) / GLA_GATE_TAU

    def pad_seq(t, d):
        return jnp.pad(t.astype(f32).reshape(B, L, H, d), ((0, 0), (pad, 0), (0, 0), (0, 0)))

    def chunk(t):
        return t.reshape(B, N, C, H, t.shape[-1]).transpose(0, 3, 1, 2, 4)

    def unchunk(t):
        return t.transpose(0, 2, 3, 1, 4).reshape(B, Lp, H, t.shape[-1])

    qp = pad_seq(q * (dk ** -0.5), dk)
    kp = pad_seq(k, dk)
    vp = pad_seq(v, dv)
    lfp = pad_seq(la_f, dk)
    lbp = pad_seq(la_b, dk)
    o_f = unchunk(gla_chunked(chunk(qp), chunk(kp), chunk(vp), chunk(lfp), False))
    rev = lambda t: t[:, ::-1]
    o_b = rev(unchunk(gla_chunked(chunk(rev(qp)), chunk(rev(kp)), chunk(rev(vp)), chunk(rev(lbp)), True)))
    o = (o_f + o_b)[:, pad:].astype(q.dtype)
    o = rmsnorm(o, out_gain) * jax.nn.silu(g.reshape(B, L, H, dv))
    return o.reshape(B, L, H * dv)

def hybrid_layer(h, norm_mix_pre, w_in, rpb, na_gain, up_f, bias_f, up_b, bias_b, gla_gain,
                 w_o, norm_mix_post, norm_ffn_pre, w_ffn_in, conv_w, conv_b, w_ffn_out, norm_ffn_post):
    B, L, _ = h.shape
    u = rmsnorm(h, norm_mix_pre)
    proj = u @ w_in
    sizes = [NA_WIDTH, NA_WIDTH, NA_WIDTH, GLA_KW, GLA_KW, GLA_VW, GLA_VW, 2 * GLA_GATE_RANK]
    offs = np.cumsum([0] + sizes)
    parts = [proj[..., int(offs[i]):int(offs[i + 1])] for i in range(len(sizes))]
    q_na, k_na, v_na, q_gl, k_gl, v_gl, g_gl, z_gl = parts
    shp = (B, L, NA_HEADS, NA_HEAD_DIM)
    o_na = neighbourhood_attention(q_na.reshape(shp), k_na.reshape(shp), v_na.reshape(shp), rpb)
    o_na = rmsnorm(o_na, na_gain)
    o_gl = gla_bidirectional(q_gl, k_gl, v_gl, g_gl, z_gl, up_f, bias_f, up_b, bias_b, gla_gain)
    mix = jnp.concatenate([o_na, o_gl], axis=-1) @ w_o
    h = h + rmsnorm(mix, norm_mix_post)
    a = rmsnorm(h, norm_ffn_pre) @ w_ffn_in
    half = CONV_W // 2
    ap = jnp.pad(a, ((0, 0), (half, half), (0, 0)))
    a = sum(ap[:, j:j + L] * conv_w[j] for j in range(CONV_W)) + conv_b
    val, gate = a[..., :D_FF], a[..., D_FF:]
    y = (jax.nn.gelu(gate, approximate=True) * val) @ w_ffn_out
    return h + rmsnorm(y, norm_ffn_post)

def first_inputs(seed: int = 0) -> dict:
    key = jax.random.key(seed)
    ks = jax.random.split(key, 20)
    f32 = jnp.float32

    def nrm(k, shape, scale):
        return jax.random.normal(k, shape, f32) * scale

    def gain(k, shape):
        return 1.0 + 0.1 * jax.random.normal(k, shape, f32)

    return {
        'x': nrm(ks[0], (BATCH, SEQ, D_MODEL), 1.0),
        'meta_tokens': nrm(ks[1], (N_META, D_MODEL), 1.0),
        'norm_mix_pre': gain(ks[2], (DEPTH, D_MODEL)),
        'w_in': nrm(ks[3], (DEPTH, D_MODEL, IN_COLS), D_MODEL ** -0.5),
        'na_rel_bias': nrm(ks[4], (DEPTH, NA_HEADS, 2 * NA_WIN_ROWS - 1, 2 * NA_WIN_COLS - 1), 0.5),
        'na_out_gain': gain(ks[5], (DEPTH, NA_WIDTH)),
        'gla_gate_up_fwd': nrm(ks[6], (DEPTH, GLA_GATE_RANK, GLA_KW), GLA_GATE_RANK ** -0.5),
        'gla_gate_bias_fwd': nrm(ks[7], (DEPTH, GLA_KW), 0.5),
        'gla_gate_up_bwd': nrm(ks[8], (DEPTH, GLA_GATE_RANK, GLA_KW), GLA_GATE_RANK ** -0.5),
        'gla_gate_bias_bwd': nrm(ks[9], (DEPTH, GLA_KW), 0.5),
        'gla_out_gain': gain(ks[10], (DEPTH, GLA_DV)),
        'w_o': nrm(ks[11], (DEPTH, MIX_WIDTH, D_MODEL), MIX_WIDTH ** -0.5),
        'norm_mix_post': gain(ks[12], (DEPTH, D_MODEL)),
        'norm_ffn_pre': gain(ks[13], (DEPTH, D_MODEL)),
        'w_ffn_in': nrm(ks[14], (DEPTH, D_MODEL, 2 * D_FF), D_MODEL ** -0.5),
        'ffn_conv_w': nrm(ks[15], (DEPTH, CONV_W, 2 * D_FF), CONV_W ** -0.5),
        'ffn_conv_b': nrm(ks[16], (DEPTH, 2 * D_FF), 0.02),
        'w_ffn_out': nrm(ks[17], (DEPTH, D_FF, D_MODEL), D_FF ** -0.5),
        'norm_ffn_post': gain(ks[18], (DEPTH, D_MODEL)),
    }

def first_block(x, meta_tokens, norm_mix_pre, w_in, na_rel_bias, na_out_gain, gla_gate_up_fwd,
              gla_gate_bias_fwd, gla_gate_up_bwd, gla_gate_bias_bwd, gla_out_gain, w_o, norm_mix_post,
              norm_ffn_pre, w_ffn_in, ffn_conv_w, ffn_conv_b, w_ffn_out, norm_ffn_post):
    B = x.shape[0]
    meta = jnp.broadcast_to(meta_tokens.astype(x.dtype)[None], (B, N_META, x.shape[-1]))
    h = jnp.concatenate([meta, x], axis=1)
    for l in range(DEPTH):
        h = hybrid_layer(h, norm_mix_pre[l], w_in[l], na_rel_bias[l], na_out_gain[l],
                         gla_gate_up_fwd[l], gla_gate_bias_fwd[l], gla_gate_up_bwd[l], gla_gate_bias_bwd[l],
                         gla_out_gain[l], w_o[l], norm_mix_post[l], norm_ffn_pre[l], w_ffn_in[l],
                         ffn_conv_w[l], ffn_conv_b[l], w_ffn_out[l], norm_ffn_post[l])
    return h[:, N_META:]


N_HEADS = 8
HEAD_DIM = 64
ATTN_WIDTH = N_HEADS * HEAD_DIM
IDX_HEADS = 8
IDX_DIM = 64
TOPK_MAX = 256
Q_BLOCK = 128
CONV_CH = 512
CONV_WIDTH = 31
D_FF_2 = -(-8 * D_MODEL // (3 * 256)) * 256
N_MOD = 6
EPS = 1e-6


def _in_split_sizes():
    return [ATTN_WIDTH, ATTN_WIDTH, ATTN_WIDTH,
            IDX_HEADS * IDX_DIM, IDX_DIM, IDX_HEADS,
            2 * CONV_CH, D_MODEL, D_MODEL]

def rmsnorm_2(x, g):
    xf = x.astype(jnp.float32)
    y = xf * lax.rsqrt(jnp.mean(xf * xf, axis=-1, keepdims=True) + EPS) * g.astype(jnp.float32)
    return y.astype(x.dtype)

def layernorm(x, g, b):
    xf = x.astype(jnp.float32)
    mu = jnp.mean(xf, axis=-1, keepdims=True)
    var = jnp.mean(jnp.square(xf - mu), axis=-1, keepdims=True)
    y = (xf - mu) * lax.rsqrt(var + EPS) * g.astype(jnp.float32) + b.astype(jnp.float32)
    return y.astype(x.dtype)

def modulate(h, shift, scale):
    return h * (1.0 + scale[:, None, :]) + shift[:, None, :]

def dsa_attention(q, k, v, q_idx, k_idx, w_idx):
    B, S = q.shape[0], q.shape[1]
    topk = min(TOPK_MAX, S // 4)
    n_blocks = S // Q_BLOCK
    f32 = jnp.float32
    slopes = jnp.exp2(-8.0 * jnp.arange(1, N_HEADS + 1, dtype=f32) / N_HEADS)
    key_pos = jnp.arange(S)
    k_idx32 = k_idx.astype(f32)
    gather = jax.vmap(lambda arr, ix: arr[ix])

    def one_block(i):
        start = i * Q_BLOCK
        qb = lax.dynamic_slice_in_dim(q, start, Q_BLOCK, axis=1).astype(f32)
        qib = lax.dynamic_slice_in_dim(q_idx, start, Q_BLOCK, axis=1).astype(f32)
        wb = lax.dynamic_slice_in_dim(w_idx, start, Q_BLOCK, axis=1).astype(f32)
        q_pos = start + jnp.arange(Q_BLOCK)
        idx_logits = jnp.einsum('btjd,bsd->btjs', qib, k_idx32) * (IDX_DIM ** -0.5)
        score = jnp.einsum('btj,btjs->bts', wb, jax.nn.relu(idx_logits))
        causal = key_pos[None, :] <= q_pos[:, None]
        score = jnp.where(causal[None], score, -jnp.inf)
        _, sel = lax.top_k(score, topk)
        k_sel = gather(k, sel).astype(f32)
        v_sel = gather(v, sel).astype(f32)
        s = jnp.einsum('bthd,btkhd->bhtk', qb, k_sel) * (HEAD_DIM ** -0.5)
        dist = (q_pos[None, :, None] - sel).astype(f32)
        s = s - slopes[None, :, None, None] * dist[:, None]
        valid = sel <= q_pos[None, :, None]
        s = jnp.where(valid[:, None], s, -jnp.inf)
        p = jax.nn.softmax(s, axis=-1)
        out = jnp.einsum('bhtk,btkhd->bthd', p, v_sel)
        return out.astype(q.dtype)

    outs = lax.map(one_block, jnp.arange(n_blocks))
    return jnp.transpose(outs, (1, 0, 2, 3, 4)).reshape(B, S, N_HEADS * HEAD_DIM)

def conformer_conv(u, w_dw, b_dw, ln_g, ln_b):
    a, g = jnp.split(u, 2, axis=-1)
    z = a * jax.nn.sigmoid(g)
    z = lax.conv_general_dilated(z, w_dw, window_strides=(1,), padding=[(CONV_WIDTH - 1, 0)],
                                 dimension_numbers=('NWC', 'WIO', 'NWC'),
                                 feature_group_count=CONV_CH) + b_dw
    z = layernorm(z, ln_g, ln_b)
    return jax.nn.silu(z)

def second_inputs(seed: int = 0) -> dict:
    key = jax.random.key(seed)
    ks = jax.random.split(key, 20)
    n_in = sum(_in_split_sizes())

    def nrm(k, shape, fan_in, gain=1.0):
        return jax.random.normal(k, shape, jnp.float32) * (gain * fan_in ** -0.5)

    def gain_vec(k, shape):
        return 1.0 + 0.02 * jax.random.normal(k, shape, jnp.float32)

    def small(k, shape):
        return 0.02 * jax.random.normal(k, shape, jnp.float32)

    return {
        "x": jax.random.normal(ks[0], (BATCH, SEQ, D_MODEL), jnp.float32),
        "c": jax.random.normal(ks[1], (BATCH, D_MODEL), jnp.float32),
        "norm_mix_g": gain_vec(ks[2], (DEPTH, D_MODEL)),
        "w_in": nrm(ks[3], (DEPTH, D_MODEL, n_in), D_MODEL),
        "w_dw": nrm(ks[4], (DEPTH, CONV_WIDTH, 1, CONV_CH), CONV_WIDTH),
        "b_dw": small(ks[5], (DEPTH, CONV_CH)),
        "conv_ln_g": gain_vec(ks[6], (DEPTH, CONV_CH)),
        "conv_ln_b": small(ks[7], (DEPTH, CONV_CH)),
        "w_attn_proj": nrm(ks[8], (DEPTH, ATTN_WIDTH, D_MODEL), ATTN_WIDTH),
        "w_conv_proj": nrm(ks[9], (DEPTH, CONV_CH, D_MODEL), CONV_CH),
        "w_out": nrm(ks[10], (DEPTH, D_MODEL, D_MODEL), D_MODEL),
        "norm_ffn_g": gain_vec(ks[11], (DEPTH, D_MODEL)),
        "w_ffn_in": nrm(ks[12], (DEPTH, D_MODEL, 2 * D_FF_2), D_MODEL),
        "w_ffn_out": nrm(ks[13], (DEPTH, D_FF_2, D_MODEL), D_FF_2),
        "w_ada": nrm(ks[14], (DEPTH, D_MODEL, N_MOD * D_MODEL), D_MODEL, 0.5),
        "b_ada": small(ks[15], (DEPTH, N_MOD * D_MODEL)),
        "norm_final_g": gain_vec(ks[16], (D_MODEL,)),
    }

def second_block(x, c, norm_mix_g, w_in, w_dw, b_dw, conv_ln_g, conv_ln_b, w_attn_proj,
              w_conv_proj, w_out, norm_ffn_g, w_ffn_in, w_ffn_out, w_ada, b_ada, norm_final_g):
    B, S, _ = x.shape
    split_at = list(np.cumsum(_in_split_sizes())[:-1])
    c_act = jax.nn.silu(c)
    for l in range(DEPTH):
        mod = c_act @ w_ada[l] + b_ada[l]
        sh_m, sc_m, g_m, sh_f, sc_f, g_f = jnp.split(mod, N_MOD, axis=-1)

        h = modulate(rmsnorm_2(x, norm_mix_g[l]), sh_m, sc_m)
        proj = h @ w_in[l]
        q, k, v, qi, ki, wi, u, ga, gb = jnp.split(proj, split_at, axis=-1)
        q = q.reshape(B, S, N_HEADS, HEAD_DIM)
        k = k.reshape(B, S, N_HEADS, HEAD_DIM)
        v = v.reshape(B, S, N_HEADS, HEAD_DIM)
        qi = qi.reshape(B, S, IDX_HEADS, IDX_DIM)
        wi = wi * (IDX_HEADS ** -0.5)
        y_attn = dsa_attention(q, k, v, qi, ki, wi) @ w_attn_proj[l]
        y_conv = conformer_conv(u, w_dw[l], b_dw[l], conv_ln_g[l], conv_ln_b[l]) @ w_conv_proj[l]
        merged = jax.nn.sigmoid(ga) * y_attn + jax.nn.sigmoid(gb) * y_conv
        x = x + g_m[:, None, :] * (merged @ w_out[l])

        h = modulate(rmsnorm_2(x, norm_ffn_g[l]), sh_f, sc_f)
        a, b = jnp.split(h @ w_ffn_in[l], 2, axis=-1)
        x = x + g_f[:, None, :] * ((jax.nn.silu(a) * b) @ w_ffn_out[l])
    return rmsnorm_2(x, norm_final_g)


def setup_inputs(seed=0):
    out = dict(first_inputs(seed))
    for name, value in second_inputs(seed + 1).items():
        if name != "x":
            out[name + "_2"] = value
    return out


def reference(
    x, meta_tokens, norm_mix_pre, w_in, na_rel_bias, na_out_gain, gla_gate_up_fwd,
    gla_gate_bias_fwd, gla_gate_up_bwd, gla_gate_bias_bwd, gla_out_gain, w_o, norm_mix_post,
    norm_ffn_pre, w_ffn_in, ffn_conv_w, ffn_conv_b, w_ffn_out, norm_ffn_post, c_2, norm_mix_g_2,
    w_in_2, w_dw_2, b_dw_2, conv_ln_g_2, conv_ln_b_2, w_attn_proj_2, w_conv_proj_2, w_out_2,
    norm_ffn_g_2, w_ffn_in_2, w_ffn_out_2, w_ada_2, b_ada_2, norm_final_g_2,
):
    x = first_block(
        x, meta_tokens, norm_mix_pre, w_in, na_rel_bias, na_out_gain, gla_gate_up_fwd,
        gla_gate_bias_fwd, gla_gate_up_bwd, gla_gate_bias_bwd, gla_out_gain, w_o, norm_mix_post,
        norm_ffn_pre, w_ffn_in, ffn_conv_w, ffn_conv_b, w_ffn_out, norm_ffn_post,
    )
    return second_block(
        x, c_2, norm_mix_g_2, w_in_2, w_dw_2, b_dw_2, conv_ln_g_2, conv_ln_b_2, w_attn_proj_2,
        w_conv_proj_2, w_out_2, norm_ffn_g_2, w_ffn_in_2, w_ffn_out_2, w_ada_2, b_ada_2,
        norm_final_g_2,
    )


_drawn_inputs = setup_inputs


def setup_inputs(seed=0):
    import zlib

    import numpy as np

    out = dict(_drawn_inputs(seed))
    spreads = {}
    factors = {'ffn_conv_b': 3.201,
     'norm_mix_g_2': 8.0,
     'b_dw_2': 23.913,
     'conv_ln_g_2': 37.753,
     'conv_ln_b_2': 39.032,
     'norm_ffn_g_2': 8.0,
     'b_ada_2': 4.335,
     'norm_final_g_2': 7.697}
    for name, (base, spread) in spreads.items():
        noise = np.random.default_rng([zlib.crc32(name.encode()), seed]).standard_normal(out[name].shape)
        drawn = base * np.exp(spread * noise) if base else spread * noise
        out[name] = __import__('jax').numpy.asarray(drawn.astype(out[name].dtype))
    for name, factor in factors.items():
        out[name] = (out[name] * factor).astype(out[name].dtype)
    return out
```

```python
import numpy as np
import concourse.bass as bass
from concourse import mybir
from contextlib import ExitStack

F32 = mybir.dt.float32
F32R = mybir.dt.float32r
I32 = mybir.dt.int32
ALU = mybir.AluOpType
ACT = mybir.ActivationFunctionType
AX = mybir.AxisListType

P = 128
D = 1024
KD = D // P
SEQ = 512
META = 16
T = META + SEQ
EPS = 1e-6
GRID_W, GRID_R = 64, 8
NA_H, DH = 8, 64
GLA_H, DK, DV, CHUNK = 4, 64, 128, 64
NCHUNK = SEQ // CHUNK + 1
RANK = 16
DFF = 2816
JF = DFF // P
CONVF = 3
CONV_CH, CONV_W = 512, 31
NMOD = 6
FT0 = 12
FT = T - FT0
TOPK = 128
TAKEN = -3e38
RING = 3
BLK = 8

VECS = [("mix_pre", 8), ("na_gain", 4), ("gate_bias", 4), ("gla_gain", 1), ("mix_post", 8),
        ("ffn_pre", 8), ("cw", 44 * CONVF), ("cb", 44), ("ffn_post", 8),
        ("mix2", 8), ("w_dw", 4 * CONV_W), ("b_dw", 4), ("ln_g", 4), ("ln_b", 4), ("ffn2", 8),
        ("b_ada", 48), ("final", 8), ("c", 8), ("eps", 1)]
VCOL = {}
_at = 0
for _n, _w in VECS:
    VCOL[_n] = _at
    _at += _w
NVEC = _at

UNITS = [("z", 1), ("q_gl", 2), ("k_gl", 2), ("v_gl", 4), ("q_na", 4), ("k_na", 4), ("v_na", 4),
         ("g_gl", 4), ("w_o", 8), ("ffn_in", 2 * JF), ("ffn_out", 24),
         ("u2", 8), ("qi2", 4), ("ki2", 1), ("wi2", 1), ("q2", 4), ("k2", 4), ("v2", 4),
         ("ga2", 8), ("gb2", 8), ("proj2", 8), ("out2", 8), ("ffn_in2", 2 * JF), ("ffn_out2", 24)]
U0 = {}
_at = 0
for _n, _w in UNITS:
    U0[_n] = _at
    _at += _w
NUNIT = _at

T0 = {}
_at = 0
for _n, _w in UNITS:
    T0[_n] = _at
    _at += {"ffn_out": 8, "ffn_out2": 8, "proj2": 16}.get(_n, _w)


def na_window(a):
    lo, hi = max(0, 16 * (a - 1)), min(GRID_W, 16 * (a + 2))
    return lo, hi - lo


def chunk_place(c):
    if c == 0:
        return 4, 0, META, 0
    return (c - 1) // 2, CHUNK * ((c - 1) % 2), CHUNK, META + CHUNK * (c - 1)


def build(nc, wstream, ada, hT, vecs, consts, masks, scanm, bias, up, out):
    ctx = ExitStack()
    with ctx:

        def sb(name, shape, at, dt=F32):
            return nc.alloc_sbuf_tensor_at(name, shape, dt, offset=at)

        class Signals(dict):
            def __missing__(self, name):
                self[name] = ctx.enter_context(nc.semaphore(name))
                return self[name]

        s = Signals()

        at = 16512
        h = sb("h", [P, KD, T], at); at += KD * T * 4
        U_AT = at
        uhi = sb("uhi", [P, KD, T], at, F32R); at += KD * T * 4
        ulo = sb("ulo", [P, KD, T], at, F32R); at += KD * T * 4
        raw = sb("raw", [P, RING, BLK * P], at); at += RING * BLK * P * 4
        whi = sb("whi", [P, RING, BLK * P], at, F32R); at += RING * BLK * P * 4
        wlo = sb("wlo", [P, RING, BLK * P], at, F32R); at += RING * BLK * P * 4
        vec = sb("vec", [P, NVEC], at); at += -(-4 * NVEC // 64) * 64
        ident = sb("ident", [P, P], at); at += 512
        ones = sb("ones", [P, P], at); at += 512
        one_col = sb("one_col", [P, 1], at); at += 64
        small = sb("small", [P, 160], at); at += 640
        A0 = -(-at // 64) * 64

        def arena(offset):
            return A0 + offset

        def v(name, k=0, n=1):
            return vec[:, VCOL[name] + k:VCOL[name] + k + n]

        csilu = small[:, 0:8]
        mod = small[:, 8:56]
        gm2 = small[:, 56:64]
        gf2 = small[:, 64:72]
        mx = small[:, 72:80]
        nmx = small[:, 80:88]
        rs = small[:, 88:96]
        rinv = small[:, 96:104]
        ssn = small[:, 104:105]
        rstdn = small[:, 105:106]
        top8 = small[:, 112:120]

        o = 0
        qna = sb("qna", [P, 4, T], arena(o)); o += 8448
        kna = sb("kna", [P, 4, T], arena(o)); o += 8448
        vna = sb("vna", [P, 5, 512], arena(o)); o += 10240
        vgl = sb("vgl", [P, 5, 512], arena(o)); o += 10240
        sg = sb("sg", [P, 4, T], arena(o)); o += 8448
        biasn = sb("biasn", [P, NA_H, 48 * 8], arena(o)); o += 12288
        KEND = o
        kend = sb("kend", [P, 4, T], arena(o)); o += 8448
        QDEC = o
        qdec = sb("qdec", [P, 4, T], arena(o)); o += 8448
        KINV = o
        kinv = sb("kinv", [P, 4, T], arena(o)); o += 8448
        QGL = o
        qgl = sb("qgl", [P, 2, T], arena(o)); o += 4224
        kgl = sb("kgl", [P, 2, T], arena(o)); o += 4224
        TX = o
        tx = sb("tx", [P, 2, T], arena(o)); o += 4224
        TE = o
        te = sb("te", [P, 2, T], arena(o)); o += 4224
        scan_keep = sb("scan_keep", [P, 2, T], arena(o)); o += 4224
        zT = sb("zT", [32, T], arena(o)); o += 2112
        upt = sb("upt", [32, 512], arena(o)); o += 2048
        dec = sb("dec", [P, 4, NCHUNK], arena(o)); o += 192
        gmask = sb("gmask", [P, 2, P], arena(o), I32); o += 1024
        wmask = sb("wmask", [P, 4, 48], arena(o)); o += 768
        adabuf = sb("adabuf", [P, 2, BLK * P], arena(o)); o += 8192
        sq1 = sb("sq1", [P, 2, T], arena(KEND))
        ub1 = sb("ub1", [P, 2, T], arena(KEND + 4224))
        rstd1 = sb("rstd1", [P, T], arena(QDEC))
        kendT = sb("kendT", [P, 5, 512], U_AT)
        S = sb("S", [P, 2, NCHUNK, 2, DV], U_AT + 10240)
        Amat = sb("Amat", [P, 2, 512], U_AT + 28672)
        oT = sb("oT", [P, 4, T], arena(KEND))
        onaT = sb("onaT", [P, 4, T], arena(QDEC))
        gsq = sb("gsq", [P, 2, T], arena(KINV))
        grs = sb("grs", [P, 2, T], arena(KINV + 4224))
        sc = sb("sc", [P, 2, 2, 400], arena(QGL))
        vT = sb("vT", [P, 4, T], arena(TX))
        pt = sb("pt", [P, 2, 512], arena(TX))
        otok = sb("otok", [P, 512], arena(TE))
        osq = sb("osq", [P, 512], arena(TE + 2048))
        yhi = sb("yhi", [P, JF, SEQ], arena(0), F32R)
        ylo = sb("ylo", [P, JF, SEQ], arena(45056), F32R)
        FB = 90112
        av = sb("av", [P, 3, FT + 4], arena(FB))
        ag = sb("ag", [P, 3, FT + 4], arena(FB + 6240))
        tv = sb("tv", [P, 3, SEQ], arena(FB + 12480))
        tg = sb("tg", [P, 3, SEQ], arena(FB + 18624))
        yf = sb("yf", [P, 3, SEQ], arena(FB + 24768))
        m1 = sb("m1", [P, KD, FT], arena(0))
        sq2 = sb("sq2", [P, 2, T], arena(FB))
        ub2 = sb("ub2", [P, 2, T], arena(FB + 4224))
        rstd2 = sb("rstd2", [P, T], arena(FB + 8448))
        m2 = sb("m2", [P, KD, SEQ], U_AT)

        z2 = sb("z2", [P, 4, CONV_W - 1 + SEQ], arena(0))
        ch = sb("ch", [P, 4, SEQ], arena(0), F32R)
        cacc = sb("cacc", [P, 4, SEQ], arena(8704))
        cl = sb("cl", [P, 4, SEQ], arena(8704), F32R)
        sgm = sb("sgm", [P, 2, SEQ], arena(16896))
        rt = sb("rt", [P, 2, SEQ], arena(16896))
        q2 = sb("q2_", [P, 4, SEQ], arena(20992))
        k2 = sb("k2_", [P, 4, SEQ], arena(29184))
        qi2 = sb("qi2_", [P, 4, SEQ], arena(37376))
        ki2 = sb("ki2_", [P, SEQ], arena(45568))
        v2 = sb("v2_", [P, 4, 512], arena(47616))
        mh = sb("mh", [P, KD, SEQ], arena(20992), F32R)
        ml = sb("ml", [P, KD, SEQ], arena(37376), F32R)
        wi2 = sb("wi2_", [P, 4, 8], arena(55808))
        sga = sb("sga", [P, KD, SEQ], arena(55936))
        sgb = sb("sgb", [P, KD, SEQ], arena(72320))
        scb = sb("scb", [P, 1152], arena(72320))
        S2 = sb("S2", [P, 3, SEQ], arena(76928))
        pt2 = sb("pt2", [P, 2, SEQ], arena(83072))
        otok2 = sb("otok2", [P, 512], arena(87168))
        sq4 = sb("sq4", [P, 2, T], arena(76928))
        ub4 = sb("ub4", [P, 2, T], arena(81152))
        rstd4 = sb("rstd4", [P, T], arena(85376))
        dtab = sb("dtab", [P, 896], arena(89216))
        caus = sb("caus", [P, P], arena(92800))
        ah = sb("ah", [P, 4, SEQ], arena(93312), F32R)
        al = sb("al", [P, 4, SEQ], arena(101504), F32R)
        lnt = sb("lnt", [P, 2, SEQ], arena(109696))
        lnr = sb("lnr", [P, SEQ], arena(113792))
        yab = sb("yab", [P, 4, SEQ], arena(109696))
        res = sb("res", [P, KD, SEQ], U_AT)

        G = ctx.enter_context(nc.psum_tensor("G", [P, 2, 2, 512], F32))
        B4 = ctx.enter_context(nc.psum_tensor("B4", [P, 4, 512], F32))

        def norm_halves(W):
            return (1, W) if W <= 512 else (2, W // 2)

        ROWS4 = [(0, META + SEQ // 2), (META + SEQ // 2, SEQ // 2)]

        NORMS = {"mix_pre": (0, T), "mix_post": (1, FT), "ffn_pre": (2, FT), "ffn_post": (3, SEQ),
                 "mix2": (4, SEQ), "ffn2": (5, SEQ), "final": (6, SEQ)}
        SPLITS = {"mix_pre": 0, "mix": 1, "ffn_pre": 2, "mix2": 3, "ffn2": 4}

        def scratch(norm):
            return {"mix_pre": (sq1, ub1, rstd1), "mix2": (sq4, ub4, rstd4)}.get(norm, (sq2, ub2, rstd2))

        block = ctx.enter_context(nc.Block())

        @block.sync
        def _(sp):
            for k in range(KD):
                sp.dma_start(h[:, k, :], hT[:, k, :]).then_inc(s[f"h_in{k % 2}"], 16)
            sp.dma_start(vec[:, :], vecs).then_inc(s["vec_in"], 16)
            sp.dma_start(ones[:, :], consts[:, P:2 * P]).then_inc(s["ones_in"], 16)

            def load_unit(n, i, wait):
                if wait is not None:
                    sp.wait_ge(s["unit_split"], wait)
                sp.dma_start(raw[:, i, :], wstream[bass.ds(n, 1), :, :].rearrange("a p n -> p (a n)"))\
                    .then_inc(s[f"unit_in{i}"], 16)

            for n in range(RING):
                load_unit(n, n, None)
            sp.dma_start(ident[:, :], consts[:, 0:P]).then_inc(s["ident_in"], 16)
            sp.dma_start(scan_keep[:, :, :], scanm).then_inc(s["gla_in"], 16)
            sp.dma_start(upt[:, :], up).then_inc(s["up_in"], 16)
            sp.dma_start(gmask[:, :, :], masks).then_inc(s["gmask_in"], 16)
            sp.dma_start(biasn[:, :, :], bias).then_inc(s["bias_in"], 16)
            sp.dma_start(wmask[:, :, :], consts[:, 2 * P:2 * P + 192].rearrange("p (a w) -> p a w", a=4))\
                .then_inc(s["wmask_in"], 16)
            with sp.Fori(1, U0["w_o"] // RING + 1) as i:
                for r in range(RING):
                    load_unit(RING * i + r, r, RING * i + r - (RING - 1))
            for m in range(NMOD * KD):
                if m >= 2:
                    sp.wait_ge(s["ada_used"], m - 1)
                sp.dma_start(adabuf[:, m % 2, :], ada[m, :, :]).then_inc(s[f"ada_in{m % 2}"], 16)
            with sp.Fori(U0["w_o"] // RING + 1, NUNIT // RING) as i:
                for r in range(RING):
                    load_unit(RING * i + r, r, RING * i + r - (RING - 1))
            for n in range(NUNIT // RING * RING, NUNIT):
                load_unit(n, n % RING, n - (RING - 1))
            for k in range(KD):
                sp.wait_ge(s["res_done"], k + 1)
                sp.dma_start(out[:, k, :], res[:, k, :]).then_inc(s["stored"], 16)
            sp.wait_ge(s["stored"], 16 * KD)


        @block.gpsimd
        def _(pool):
            pool.memset(one_col[:, :], 1.0).then_inc(s["one_col"], 1)
            pool.wait_ge(s["one_col"], 1)

            def split_unit(n, i, arrived):
                pool.wait_ge(s[f"unit_in{i}"], arrived)
                pool.tensor_tensor(whi[:, i, :], raw[:, i, :], one_col[:, 0:1].broadcast_to([P, BLK * P]),
                                   ALU.mult).then_inc(s["unit_hi"], 1)
                pool.wait_ge(s["unit_hi"], n + 1)
                pool.tensor_tensor(wlo[:, i, :], raw[:, i, :], whi[:, i, :].bitcast(F32), ALU.subtract)\
                    .then_inc(s["unit_split"], 1)

            for n in range(RING):
                split_unit(n, n, 16)
            with pool.Fori(1, NUNIT // RING) as i:
                for r in range(RING):
                    pool.wait_ge(s["unit_used"], RING * i + r - (RING - 1))
                    split_unit(RING * i + r, r, 16 * i + 16)
            for n in range(NUNIT // RING * RING, NUNIT):
                pool.wait_ge(s["unit_used"], n - (RING - 1))
                split_unit(n, n % RING, 16 * (n // RING) + 16)

        @block.tensor
        def _(pe):
            def sums(norm):
                r, W = NORMS[norm]
                nh, hw = norm_halves(W)
                for k in range(KD):
                    pe.wait_ge(s["sq_done"], KD * r + k + 1)
                    for x in range(nh):
                        last = pe.matmul(B4[:, x, 0:hw], ones[:, :], scratch(norm)[0][:, k % 2, x * hw:(x + 1) * hw],
                                         start=(k == 0), stop=(k == KD - 1))
                    last.then_inc(s["sq_used"], 1)

            def split_ready(group, k):
                pe.wait_ge(s["ulo_done"], KD * SPLITS[group] + k + 1)

            def unit_ready(n):
                pe.wait_ge(s["unit_split"], n + 1)

            def tile_free(t, at_least=2):
                pe.wait_ge(s["evac_done"], t - 1)

            def product(dst, slot, blocks, hi, lo, off, W, first=True, last=True, ready=None, halves=None):
                nh, hw = norm_halves(W)
                halves = halves or [(x * hw, hw) for x in range(nh)]
                for i, (b, k) in enumerate(blocks):
                    if ready:
                        ready(k)
                    for j, (w, u) in enumerate(((whi, hi), (whi, lo), (wlo, hi))):
                        for x, (x0, xw) in enumerate(halves):
                            ins = pe.matmul(dst[:, x, 0:xw], w[:, slot, b * P:(b + 1) * P],
                                            u[:, k, off + x0:off + x0 + xw],
                                            start=(first and i == 0 and j == 0),
                                            stop=(last and i == len(blocks) - 1 and j == 2))
                return ins

            def fm_tile(n, t, off=0, W=T, group=None, halves=None):
                unit_ready(n)
                if t >= 2:
                    tile_free(t)
                product(G[:, t % 2], n % RING, [(k, k) for k in range(KD)], uhi, ulo, off, W,
                        ready=(lambda k: split_ready(group, k)) if group else None, halves=halves)\
                    .then_inc(s["unit_used"], 1)

            def tm_tile(n, t, places, cols=P):
                unit_ready(n)
                tile_free(t)
                for dst, tok in places:
                    for k in range(KD):
                        for j, (w, u) in enumerate(((whi, uhi), (whi, ulo), (wlo, uhi))):
                            ins = pe.matmul(dst, tok(u, k), w[:, n % RING, k * P:k * P + cols],
                                            start=(k == 0 and j == 0), stop=(k == KD - 1 and j == 2))
                ins.then_inc(s["unit_used"], 1)

            pe.wait_ge(s["ones_in"], 16)
            sums("mix_pre")
            for name in ("z", "q_gl", "k_gl"):
                for i in range(dict(UNITS)[name]):
                    fm_tile(U0[name] + i, T0[name] + i, group="mix_pre" if name == "z" else None)
            pe.wait_ge(s["up_in"], 16)
            pe.wait_ge(s["evac_done"], T0["z"] + 1)
            def gate_logits(j):
                if j >= 2:
                    pe.wait_ge(s["gate_x"], j - 1)
                for x in range(2):
                    last = pe.matmul(B4[:, 2 * (j % 2) + x, 0:T // 2], upt[:, j * P:(j + 1) * P],
                                     zT[:, x * (T // 2):(x + 1) * (T // 2)], start=True, stop=True)
                last.then_inc(s["gate_ps"], 1)

            gate_logits(0)
            gate_logits(1)

            def natural(t):
                return [(G[:, t % 2, 0, i * P:(i + 1) * P],
                         lambda u, k, i=i: u[:, k, META + i * P:META + (i + 1) * P]) for i in range(4)] \
                    + [(G[0:META, t % 2, 1, 0:P], lambda u, k: u[:, k, 0:META])]

            for i in range(4):
                tm_tile(U0["v_gl"] + i, T0["v_gl"] + i, natural(T0["v_gl"] + i))
                if i < 2:
                    gate_logits(i + 2)
            for name in ("q_na", "k_na", "v_na"):
                for i in range(4):
                    fm_tile(U0[name] + i, T0[name] + i, halves=ROWS4)
            for i in range(4):
                fm_tile(U0["g_gl"] + i, T0["g_gl"] + i)

            pe.wait_ge(s["ident_in"], 16)
            pe.wait_ge(s["evac_done"], T0["v_na"] + 4)
            for i in range(5):
                n, t0 = (P, META + P * i) if i < 4 else (META, 0)
                if i >= 4:
                    pe.wait_ge(s["by_token_done"], i - 3)
                for f in range(4):
                    last = pe.transpose(B4[0:n, i % 4, f * P:(f + 1) * P], vT[:, f, t0:t0 + n], ident[:, :])
                last.then_inc(s["by_token_ps"], 1)

            for j in range(4):
                pe.wait_ge(s["kend_done"], j + 1)
            for i in range(5):
                n, t0 = (P, META + P * i) if i < 4 else (META, 0)
                pe.wait_ge(s["by_token_done"], i + 2)
                for j in range(4):
                    last = pe.transpose(B4[0:n, (i + 5) % 4, j * P:(j + 1) * P], kend[:, j, t0:t0 + n], ident[:, :])
                last.then_inc(s["by_token_ps"], 1)
            pe.wait_ge(s["evac_done"], T0["v_gl"] + 4)
            for i in range(NCHUNK - 1):
                for d, c in ((0, i), (1, NCHUNK - 1 - i)):
                    tile, p0, n, _t = chunk_place(c)
                    bank = 2 * (i % 2) + d
                    if i >= 2:
                        pe.wait_ge(s["state_done"], 4 * (i - 1))
                    else:
                        pe.wait_ge(s["by_token_done"], 10)
                    for hh in range(GLA_H):
                        hp, par = hh // 2, hh % 2
                        last = pe.matmul(B4[par * DK:(par + 1) * DK, bank, hp * DV:(hp + 1) * DV],
                                         kendT[p0:p0 + n, tile, (2 * d + hp) * P + par * DK:(2 * d + hp) * P + (par + 1) * DK],
                                         vgl[p0:p0 + n, tile, hh * DV:(hh + 1) * DV], start=True, stop=True)
                    last.then_inc(s["ds_ps"], 1)
            pe.wait_ge(s["state_done"], 4 * (NCHUNK - 1))
            for i in range(5):
                n, t0 = (P, META + P * i) if i < 4 else (META, 0)
                if i >= 2:
                    pe.wait_ge(s["amat_done"], i - 1)
                for par in range(2):
                    bank = 2 * (i % 2) + par
                    for d in range(2):
                        for hp in range(2):
                            last = pe.matmul(B4[0:n, bank, (2 * d + hp) * P:(2 * d + hp) * P + n],
                                             kinv[par * DK:(par + 1) * DK, 2 * d + hp, t0:t0 + n],
                                             qdec[par * DK:(par + 1) * DK, 2 * d + hp, t0:t0 + n],
                                             start=True, stop=True)
                last.then_inc(s["a_ps"], 1)
                pe.wait_ge(s["amat_done"], i + 1)
                if i >= 2:
                    pe.wait_ge(s["ogl_done"], i - 1)
                if i == 0:
                    pe.wait_ge(s["evac_done"], T0["g_gl"] + 4)
                chunks = (2 * i + 1, 2 * i + 2) if i < 4 else (0,)
                for par in range(2):
                    for hp in range(2):
                        hh = 2 * hp + par
                        pe.matmul(G[:, i % 2, par, hp * P:hp * P + n], vgl[0:n, i, hh * DV:(hh + 1) * DV],
                                  Amat[0:n, i % 2, (2 * par + hp) * P:(2 * par + hp) * P + n],
                                  start=True, stop=False)
                        for x, c in enumerate(chunks):
                            cn, ct = chunk_place(c)[2:]
                            for d in range(2):
                                last = pe.matmul(G[:, i % 2, par, hp * P + x * CHUNK:hp * P + x * CHUNK + cn],
                                                 S[par * DK:(par + 1) * DK, d, c, hp, :],
                                                 qdec[par * DK:(par + 1) * DK, 2 * d + hp, ct:ct + cn],
                                                 start=False, stop=(d == 1 and x == len(chunks) - 1))
                last.then_inc(s["ogl_ps"], 1)
            for hh in range(GLA_H):
                pe.wait_ge(s["gsq_done"], hh + 1)
                if hh == 0:
                    pe.wait_ge(s["ogl_done"], 5)
                if hh >= 2:
                    pe.wait_ge(s["grs_done"], hh - 1)
                for x in range(2):
                    last = pe.matmul(G[:, hh % 2, x, 0:T // 2], ones[:, :], gsq[:, hh % 2, x * (T // 2):(x + 1) * (T // 2)],
                                     start=True, stop=True)
                last.then_inc(s["gss_ps"], 1)

            def ada_unit(m):
                pe.wait_ge(s[f"ada_in{m % 2}"], 16 * (m // 2) + 16)
                for k in range(KD):
                    ins = pe.matmul(G[:, 1, 1, m:m + 1], adabuf[:, m % 2, k * P:(k + 1) * P], csilu[:, k:k + 1],
                                    start=(k == 0), stop=(k == KD - 1))
                ins.then_inc(s["ada_used"], 1)

            def na_scores(st):
                a, hp = st // 4, st % 4
                c0, W = na_window(a)
                if st >= 2:
                    pe.wait_ge(s["na_s"], st - 1)
                for par in range(2):
                    bank = 2 * (st % 2) + par
                    q = qna[par * DH:(par + 1) * DH, hp, META + P * a:META + P * (a + 1)]
                    pe.matmul(B4[:, bank, 0:8 * W], q,
                              kna[par * DH:(par + 1) * DH, hp, META + 8 * c0:META + 8 * (c0 + W)],
                              start=True, stop=True)
                    last = pe.matmul(B4[:, bank, 8 * W:8 * W + META], q, kna[par * DH:(par + 1) * DH, hp, 0:META],
                                     start=True, stop=True)
                last.then_inc(s["na_s_ps"], 1)

            def na_values(st):
                a, hp = st // 4, st % 4
                c0, W = na_window(a)
                nb = W // 16
                for par in range(2):
                    i = 2 * st + par
                    pe.wait_ge(s["na_p"], i + 1)
                    for b in range(nb):
                        pe.transpose(G[:, 0, par, b * P:(b + 1) * P], sc[:, st % 2, par, b * P:(b + 1) * P], ident[:, :])
                    pe.transpose(G[0:META, 0, par, 384:512], sc[:, st % 2, par, 8 * W:8 * W + META], ident[:, :])\
                        .then_inc(s["na_t_ps"], 1)
                for par in range(2):
                    i = 2 * st + par
                    hh = 2 * hp + par
                    pe.wait_ge(s["na_pt1" if par else "na_pt0"], st + 1)
                    if st % 4 == 0 and par == 0 and a >= 1:
                        pe.wait_ge(s["na_evac"], a)
                    for b in range(nb):
                        pe.matmul(G[:, 1, 0, hh * DH:(hh + 1) * DH], pt[:, par, b * P:(b + 1) * P],
                                  vna[:, c0 // 16 + b, hh * DH:(hh + 1) * DH], start=(b == 0), stop=False)
                    pe.matmul(G[:, 1, 0, hh * DH:(hh + 1) * DH], pt[0:META, par, 384:512],
                              vna[0:META, 4, hh * DH:(hh + 1) * DH], start=False, stop=True)\
                        .then_inc(s["na_o_ps"], 1)

            def na_turn(a, n=P):
                pe.wait_ge(s["na_otok"], a + 1)
                for f in range(4):
                    last = pe.transpose(G[:, 1, 0, f * P:f * P + n], otok[0:n, f * P:(f + 1) * P], ident[0:n, 0:n])
                last.then_inc(s["na_turned"], 1)

            pe.wait_ge(s["grs_done"], 4)
            pe.wait_ge(s["csilu"], 1)
            for st in range(17):
                if st < 16:
                    na_scores(st)
                    for m in range(3 * st, 3 * st + 3):
                        ada_unit(m)
                if st >= 1:
                    na_values(st - 1)
                    if (st - 1) % 4 == 3:
                        na_turn((st - 1) // 4)
            pe.wait_ge(s["na_s"], 16)
            for par in range(2):
                for hp in range(4):
                    last = pe.matmul(B4[0:META, par, hp * META:(hp + 1) * META], qna[par * DH:(par + 1) * DH, hp, 0:META],
                                     kna[par * DH:(par + 1) * DH, hp, 0:META], start=True, stop=True)
            last.then_inc(s["meta_s_ps"], 1)
            pe.wait_ge(s["meta_e"], 1)
            for hh in range(NA_H):
                last = pe.transpose(B4[0:META, 2, hh * META:(hh + 1) * META], sc[0:META, 0, 0, hh * META:(hh + 1) * META],
                                    ident[0:META, 0:META])
            last.then_inc(s["meta_t_ps"], 1)
            pe.wait_ge(s["meta_pt"], 1)
            pe.wait_ge(s["na_evac"], 4)
            for hh in range(NA_H):
                i = 4 * (hh % 2) + hh // 2
                last = pe.matmul(G[0:META, 1, 0, hh * DH:(hh + 1) * DH], pt[0:META, 0, i * META:(i + 1) * META],
                                 vna[0:META, 4, hh * DH:(hh + 1) * DH], start=True, stop=True)
            last.then_inc(s["na_o_ps"], 1)
            na_turn(4, META)

            for i in range(8):
                if i == 0:
                    pe.wait_ge(s["mod_done"], 1)
                fm_tile(U0["w_o"] + i, T0["w_o"] + i, FT0, FT, group="mix" if i == 0 else None)
            sums("mix_post")
            sums("ffn_pre")

            def ffn_pair(name, p, x, group=None, W=FT):
                for half in range(2):
                    n = U0[name] + 2 * p + half
                    t = T0[name] + 2 * p + half
                    pe.wait_ge(s["unit_split"], n + 1)
                    pe.wait_ge(s["evac_done"], t - 1)
                    product(G[:, (T0[name] + half) % 2], (U0[name] + 2 * x + half) % RING, [(k, k) for k in range(KD)],
                            uhi, ulo, 0, W,
                            ready=(lambda k: split_ready(group, k)) if group and half == 0 else None)\
                        .then_inc(s["unit_used"], 1)

            def ffn_in(name, group, W):
                for p in range(4):
                    ffn_pair(name, p, p, group if p == 0 else None, W)
                with pe.Fori(0, (JF - 4) // 3) as i:
                    for r in range(3):
                        ffn_pair(name, 3 * i + 4 + r, 4 + r, None, W)

            def ffn_out(name):
                pe.wait_ge(s["ylow_done"], JF * (1 if name == "ffn_out" else 2))
                with pe.Fori(0, KD // 2) as i:
                    for r in range(2):
                        for x in range(3):
                            pe.wait_ge(s["unit_split"], 6 * i + (U0[name] + 3 * r + x + 1))
                            if x == 0:
                                pe.wait_ge(s["evac_done"], 2 * i + (T0[name] + r - 1))
                            ks = range(BLK * x, min(BLK * (x + 1), JF))
                            product(G[:, (T0[name] + r) % 2], (U0[name] + 3 * r + x) % RING,
                                    [(k - BLK * x, k) for k in ks], yhi, ylo, 0, SEQ, first=(x == 0), last=(x == 2))\
                                .then_inc(s["unit_used"], 1)

            ffn_in("ffn_in", "ffn_pre", FT)
            ffn_out("ffn_out")
            sums("ffn_post")

            sums("mix2")
            for i in range(8):
                fm_tile(U0["u2"] + i, T0["u2"] + i, 0, SEQ, group="mix2" if i == 0 else None)
            for i in range(4):
                fm_tile(U0["qi2"] + i, T0["qi2"] + i, 0, SEQ)
            fm_tile(U0["ki2"], T0["ki2"], 0, SEQ)

            def blocks(t, cols=P):
                return [(G[:, t % 2, 0, i * P:i * P + cols], lambda u, k, i=i: u[:, k, i * P:(i + 1) * P])
                        for i in range(4)]

            tm_tile(U0["wi2"], T0["wi2"], blocks(T0["wi2"], 8), 8)
            for name in ("q2", "k2"):
                for i in range(4):
                    fm_tile(U0[name] + i, T0[name] + i, 0, SEQ)
            for i in range(4):
                tm_tile(U0["v2"] + i, T0["v2"] + i, blocks(T0["v2"] + i))

            e = 0
            for b in range(1, 4):
                for j in range(8):
                    par = j % 2
                    if e == 0:
                        pe.wait_ge(s["evac_done"], T0["wi2"] + 1)
                    if e >= 4:
                        pe.wait_ge(s["relu_done"], e - 3)
                    pe.matmul(B4[:, e % 4, 0:P * (b + 1)], qi2[par * 64:(par + 1) * 64, j // 2, P * b:P * (b + 1)],
                              ki2[par * 64:(par + 1) * 64, 0:P * (b + 1)], start=True, stop=True)\
                        .then_inc(s["idx_ps"], 1)
                    e += 1

            pe.wait_ge(s["relu_done"], 24)
            for j in range(4):
                pe.wait_ge(s["conv31_done"], j + 1)
                last = pe.matmul(B4[:, 0, :], ones[:, :], cacc[:, j, :], start=(j == 0), stop=(j == 3))
            last.then_inc(s["ln_ps"], 1)
            for j in range(4):
                pe.wait_ge(s["lnsq_done"], j + 1)
                last = pe.matmul(B4[:, 1, :], ones[:, :], lnt[:, j % 2, :], start=(j == 0), stop=(j == 3))
                last.then_inc(s["lnsq_used"], 1)

            def scores2(q):
                b, hh = q // 8, q % 8
                par = hh % 2
                if q >= 3:
                    pe.wait_ge(s["s2_read"], q - 2)
                elif q == 0:
                    pe.wait_ge(s["ln_read"], 1)
                    pe.wait_ge(s["lnv_read"], 1)
                pe.matmul(B4[:, q % 3, 0:P * (b + 1)], q2[par * 64:(par + 1) * 64, hh // 2, P * b:P * (b + 1)],
                          k2[par * 64:(par + 1) * 64, hh // 2, 0:P * (b + 1)], start=True, stop=True)\
                    .then_inc(s["s2_ps"], 1)

            def values2(q):
                b, hh = q // 8, q % 8
                pe.wait_ge(s["p2_done"], q + 1)
                if q >= 2:
                    pe.wait_ge(s["pt2_done"], q - 1)
                for c in range(b + 1):
                    last = pe.transpose(G[:, q % 2, 1, c * P:(c + 1) * P], S2[:, q % 3, c * P:(c + 1) * P], ident[:, :])
                last.then_inc(s["t2_ps"], 1)
                pe.wait_ge(s["pt2_done"], q + 1)
                if hh == 0 and b >= 1:
                    pe.wait_ge(s["al_done"], 4 * b)
                for c in range(b + 1):
                    last = pe.matmul(B4[:, 3, hh * 64:(hh + 1) * 64], pt2[:, q % 2, c * P:(c + 1) * P],
                                     v2[:, c, hh * 64:(hh + 1) * 64], start=(c == 0), stop=(c == b))
                last.then_inc(s["o2_ps"], 1)

            def turn2(b):
                pe.wait_ge(s["otok2_done"], b + 1)
                for f in range(4):
                    last = pe.transpose(B4[:, 3, f * P:(f + 1) * P], otok2[:, f * P:(f + 1) * P], ident[:, :])
                last.then_inc(s["turned2"], 1)

            gate_tile = 0
            for b in range(4):
                for i in range((0, 2, 3, 3)[b]):
                    fm_tile(U0["ga2"] + gate_tile, T0["ga2"] + gate_tile, 0, SEQ)
                    gate_tile += 1
                for hh in range(9):
                    if hh < 8:
                        scores2(8 * b + hh)
                    if hh >= 1:
                        values2(8 * b + hh - 1)
                turn2(b)
            for i in range(8):
                fm_tile(U0["gb2"] + i, T0["gb2"] + i, 0, SEQ)

            for i in range(8):
                n, hi, lo = U0["proj2"] + i, (ah, ch)[i % 2], (al, cl)[i % 2]
                unit_ready(n)
                if i == 0:
                    pe.wait_ge(s["al_done"], 16)
                    pe.wait_ge(s["evac_done"], T0["proj2"])
                if i == 1:
                    pe.wait_ge(s["cl_done"], 4)
                for ct in range(2):
                    t = T0["proj2"] + 2 * i + ct
                    pe.wait_ge(s["evac_done"], t - 3)
                    last = product(G[:, t % 2, (t // 2) % 2:(t // 2) % 2 + 1], n % RING, [(4 * ct + k, k) for k in range(4)],
                                   hi, lo, 0, SEQ)
                last.then_inc(s["unit_used"], 1)
            for i in range(8):
                n, t = U0["out2"] + i, T0["out2"] + i
                unit_ready(n)
                tile_free(t)
                if i < 2:
                    pe.wait_ge(s["evac_done"], T0["out2"])
                product(G[:, t % 2], n % RING, [(k, k) for k in range(KD)], mh, ml, 0, SEQ,
                        ready=(lambda k: pe.wait_ge(s["ml_done"], k + 1)) if i == 0 else None)\
                    .then_inc(s["unit_used"], 1)
            sums("ffn2")
            ffn_in("ffn_in2", "ffn2", SEQ)
            ffn_out("ffn_out2")
            sums("final")

        @block.scalar
        def _(act):
            def squares(norm, src, ready):
                r, W = NORMS[norm]
                for k in range(KD):
                    ready(k)
                    if k >= 2:
                        act.wait_ge(s["sq_used"], KD * r + k - 1)
                    act.activation(scratch(norm)[0][:, k % 2, 0:W], src(k), ACT.Square).then_inc(s["sq_done"], 1)

            def root(norm):
                r, W = NORMS[norm]
                nh, hw = norm_halves(W)
                rstd = scratch(norm)[2]
                act.wait_ge(s["sq_used"], KD * (r + 1))
                act.activation(rstd[:, 0:W].rearrange("p (x w) -> p x w", x=nh), B4[:, 0:nh, 0:hw], ACT.Ln,
                               bias=v("eps"), scale=1.0 / D).then_inc(s["ln_done"], 1)
                act.wait_ge(s["ln_done"], r + 1)
                act.activation(rstd[:, 0:W], rstd[:, 0:W], ACT.Exp, scale=-0.5).then_inc(s["rstd_done"], 1)

            def high(group, norm, off, shift=None):
                W = NORMS[norm][1]
                for k in range(KD):
                    act.wait_ge(s["u_done"], KD * {"mix_pre": 0, "ffn_pre": 1, "mix2": 2, "ffn2": 3}[norm] + k + 1)
                    if shift is None:
                        ins = act.activation(uhi[:, k, off:off + W], scratch(norm)[1][:, k % 2, 0:W], ACT.Copy)
                    else:
                        ins = act.activation(uhi[:, k, off:off + W], scratch(norm)[1][:, k % 2, 0:W], ACT.Identity,
                                             bias=shift(k))
                    ins.then_inc(s["uhi_done"], 1)

            def tile_ready(n):
                act.wait_ge(s["unit_used"], n + 1)

            def evac(name, i, dst, func=ACT.Copy, rows=P, W=T, **kw):
                n, t = U0[name] + i, T0[name] + i
                nh, hw = norm_halves(W)
                tile_ready(n)
                act.activation(dst.rearrange("p (x w) -> p x w", x=nh), G[0:rows, t % 2, 0:nh, 0:hw], func, **kw)\
                    .then_inc(s["evac_done"], 1)

            def h_here(k):
                act.wait_ge(s[f"h_in{k % 2}"], 16 * (k // 2) + 16)
            act.wait_ge(s["vec_in"], 16)
            act.activation(csilu, v("c", 0, 8), ACT.Silu).then_inc(s["csilu"], 1)
            squares("mix_pre", lambda k: h[:, k, :], h_here)
            root("mix_pre")
            high("mix_pre", "mix_pre", 0)
            evac("z", 0, zT[:, :], rows=32)
            for i in range(2):
                evac("q_gl", i, qgl[:, i, :])
            for i in range(2):
                evac("k_gl", i, kgl[:, i, :])

            def gate(j):
                b = j % 2
                act.wait_ge(s["gate_x"], j + 1)
                act.activation(te[:, b, :], tx[:, b, :], ACT.Abs).then_inc(s["act_step"], 1)
                act.wait_ge(s["act_step"], 2 * j + 1)
                act.activation(te[:, b, :], te[:, b, :], ACT.Exp, scale=-1.0).then_inc(s["act_step"], 1)
                act.wait_ge(s["act_step"], 2 * j + 2)
                act.activation(te[:, b, :], te[:, b, :], ACT.Ln, bias=1.0).then_inc(s["gate_ln"], 1)
                act.wait_ge(s["gate_b"], 2 * j + 1)
                act.activation(te[:, b, :], kend[:, j, :], ACT.Exp, scale=1.0 / 16).then_inc(s["gate_eb"], 1)
                ends = (META - 1, META + CHUNK - 1) if j < 2 else (0, META)
                act.activation(dec[:, j, 0:1], kend[:, j, ends[0]:ends[0] + 1], ACT.Exp, scale=1.0 / 16)
                act.activation(dec[:, j, 1:NCHUNK], kend[:, j, ends[1]:ends[1] + CHUNK * (NCHUNK - 2) + 1:CHUNK], ACT.Exp,
                               scale=1.0 / 16)
                act.wait_ge(s["gate_used"], 2 * j + 1)
                act.activation(te[:, b, :], kend[:, j, :], ACT.Exp, scale=-1.0 / 16).then_inc(s["gate_eb"], 1)
                act.wait_ge(s["gate_b"], 2 * j + 2)
                act.activation(tx[:, b, :], tx[:, b, :], ACT.Exp, scale=1.0 / 16).then_inc(s["gate_ed"], 1)

            def evac_tokens(name, i, dst):
                t = T0[name] + i
                tile_ready(U0[name] + i)
                act.activation(dst[:, 0:4, i * P:(i + 1) * P],
                               G[:, t % 2, 0, :].rearrange("p (a n) -> p a n", a=4), ACT.Copy)
                act.activation(dst[0:META, 4, i * P:(i + 1) * P], G[0:META, t % 2, 1, 0:P], ACT.Copy)\
                    .then_inc(s["evac_done"], 1)

            for i in range(4):
                gate(i)
                evac_tokens("v_gl", i, vgl)
            def evac_columns(name, i, dst):
                t = T0[name] + i
                tile_ready(U0[name] + i)
                to = dst[:, META:T].rearrange("p (c r) -> p r c", r=GRID_R)
                act.activation(dst[:, 0:META], G[:, t % 2, 0, 0:META], ACT.Copy)
                act.activation(to[:, 0:4, :], G[:, t % 2, 0, META:META + 256].rearrange("p (r c) -> p r c", r=4), ACT.Copy)
                act.activation(to[:, 4:8, :], G[:, t % 2, 1, 0:256].rearrange("p (r c) -> p r c", r=4), ACT.Copy)\
                    .then_inc(s["evac_done"], 1)

            for i in range(4):
                evac_columns("q_na", i, qna[:, i, :])
            for i in range(4):
                evac_columns("k_na", i, kna[:, i, :])
            act.wait_ge(s["kend_done"], 4)
            for i in range(4):
                evac_columns("v_na", i, vT[:, i, :])
            for i in range(4):
                evac("g_gl", i, sg[:, i, :], ACT.Silu)

            for i in range(5):
                n = P if i < 4 else META
                act.wait_ge(s["by_token_ps"], i + 1)
                act.activation(vna[0:n, i, :], B4[0:n, i % 4, :], ACT.Copy).then_inc(s["by_token_done"], 1)

            for i in range(5):
                n = P if i < 4 else META
                act.wait_ge(s["by_token_ps"], i + 6)
                if i == 0:
                    act.wait_ge(s["unit_used"], U0["g_gl"] + 4)
                act.activation(kendT[0:n, i, :], B4[0:n, (i + 5) % 4, :], ACT.Copy).then_inc(s["by_token_done"], 1)
            for i in range(5):
                n, t0 = (P, META + P * i) if i < 4 else (META, 0)
                act.wait_ge(s["ogl_ps"], i + 1)
                for par in range(2):
                    ins = act.activation(oT[:, par:4:2, t0:t0 + n],
                                         G[:, i % 2, par, 0:2 * P].rearrange("p (a n) -> p a n", a=2)[:, :, 0:n], ACT.Copy)
                ins.then_inc(s["ogl_done"], 1)
            act.wait_ge(s["ogl_done"], 5)
            for hh in range(GLA_H + 1):
                if hh < GLA_H:
                    if hh >= 2:
                        act.wait_ge(s["gss_ps"], hh - 1)
                    act.activation(gsq[:, hh % 2, :], oT[:, hh, :], ACT.Square).then_inc(s["gsq_done"], 1)
                if hh >= 1:
                    g = hh - 1
                    act.wait_ge(s["gss_ps"], g + 1)
                    if g >= 2:
                        act.wait_ge(s["ogl_out"], g - 1)
                    act.activation(grs[:, g % 2, :].rearrange("p (x w) -> p x w", x=2), G[:, g % 2, :, 0:T // 2], ACT.Ln,
                                   bias=v("eps"), scale=1.0 / DV).then_inc(s["gln_done"], 1)
                    act.wait_ge(s["gln_done"], g + 1)
                    act.activation(grs[:, g % 2, :], grs[:, g % 2, :], ACT.Exp, scale=-0.5).then_inc(s["grs_done"], 1)

            def na_exp(st):
                a = st // 4
                W = na_window(a)[1]
                act.wait_ge(s["na_nmx"], st + 1)
                if st % 4 == 0 and a >= 1:
                    act.wait_ge(s["na_rinv"], a)
                for par in range(2):
                    hh = 2 * (st % 4) + par
                    act.activation(sc[:, st % 2, par, 0:8 * W + META], sc[:, st % 2, par, 0:8 * W + META], ACT.Exp,
                                   bias=nmx[:, 2 * (st % 2) + par:2 * (st % 2) + par + 1],
                                   accum_out=rs[:, hh:hh + 1]).then_inc(s["na_p"], 1)

            def na_turned(a, n=P):
                act.wait_ge(s["na_turned"], a + 1)
                for f in range(4):
                    if a < 4:
                        dst = onaT[:, f, META:T].rearrange("p (r c) -> p c r", r=GRID_R)[:, 16 * a:16 * a + 16, :]
                        src = G[:, 1, 0, f * P:(f + 1) * P].rearrange("p (c r) -> p c r", r=GRID_R)
                    else:
                        dst, src = onaT[:, f, 0:META], G[:, 1, 0, f * P:f * P + n]
                    ins = act.activation(dst, src, ACT.Copy, scale=v("na_gain", f))
                ins.then_inc(s["na_evac"], 1)

            def na_root(a, n=P):
                act.wait_ge(s["na_o_scaled"], a + 1)
                act.activation(osq[0:n], otok[0:n], ACT.Square, accum_out=ssn[0:n]).then_inc(s["na_ss"], 1)
                act.wait_ge(s["na_ss"], a + 1)
                act.activation(rstdn[0:n], ssn[0:n], ACT.Ln, bias=vec[0:n, VCOL["eps"]:VCOL["eps"] + 1],
                               scale=1.0 / 512).then_inc(s["na_ln"], 1)
                act.wait_ge(s["na_ln"], a + 1)
                act.activation(rstdn[0:n], rstdn[0:n], ACT.Exp, scale=-0.5).then_inc(s["na_rstd"], 1)

            def na_pt_evac(st):
                nb = na_window(st // 4)[1] // 16
                act.wait_ge(s["na_t_ps"], 2 * st + 1)
                if st >= 1:
                    act.wait_ge(s["na_o_ps"], 2 * st - 1)
                act.activation(pt[:, 0, 0:nb * P], G[:, 0, 0, 0:nb * P], ACT.Copy)
                act.activation(pt[0:META, 0, 384:512], G[0:META, 0, 0, 384:512], ACT.Copy).then_inc(s["na_pt0"], 1)

            for st in range(17):
                if st < 16:
                    na_exp(st)
                if st >= 1:
                    na_pt_evac(st - 1)
                    if (st - 1) % 4 == 3:
                        na_root((st - 1) // 4)
                        na_turned((st - 1) // 4)
            act.wait_ge(s["meta_s"], 1)
            act.activation(sc[0:META, 0, 0, 0:P], sc[0:META, 0, 0, 0:P], ACT.Exp).then_inc(s["meta_e"], 1)
            act.wait_ge(s["meta_t_ps"], 1)
            act.activation(pt[0:META, 0, 0:P], B4[0:META, 2, 0:P], ACT.Copy).then_inc(s["meta_pt"], 1)
            na_root(4, META)
            na_turned(4, META)
            act.wait_ge(s["ada_used"], NMOD * KD)
            act.activation(mod, G[:, 1, 1, 0:NMOD * KD], ACT.Copy).then_inc(s["mod_done"], 1)
            for k in range(KD):
                if k < 4:
                    src = onaT[:, k, :]
                else:
                    act.wait_ge(s["ogl_out"], k - 3)
                    src = oT[:, k - 4, :]
                if k == 0:
                    act.wait_ge(s["na_evac"], 5)
                act.activation(uhi[:, k, :], src, ACT.Copy).then_inc(s["uhi_done"], 1)
            for i in range(8):
                n, t = U0["w_o"] + i, T0["w_o"] + i
                evac("w_o", i, m1[:, i, :], W=FT)
            squares("mix_post", lambda k: m1[:, k, :], lambda k: act.wait_ge(s["evac_done"], T0["w_o"] + k + 1))
            root("mix_post")
            squares("ffn_pre", lambda k: h[:, k, FT0:T], lambda k: act.wait_ge(s["h_done"], k + 1))
            root("ffn_pre")
            high("ffn_pre", "ffn_pre", 0)

            def ffn_evac(name, p, x, half, dst, func=ACT.Copy, W=FT):
                act.wait_ge(s["unit_used"], U0[name] + 2 * p + (half + 1))
                nh, hw = norm_halves(W)
                act.activation(dst.rearrange("p (x w) -> p x w", x=nh), G[:, (T0[name] + half) % 2, 0:nh, 0:hw], func)\
                    .then_inc(s["evac_done"], 1)

            def ffn_act(p, x, early):
                if not early:
                    act.wait_ge(s["conv_done"], 2 * p - 5)
                ffn_evac("ffn_in", p, x, 0, av[:, x, 0:FT])
                if not early:
                    act.wait_ge(s["conv_done"], 2 * p - 4)
                ffn_evac("ffn_in", p, x, 1, ag[:, x, 0:FT])
                act.wait_ge(s["conv_done"], 2 * p + 2)
                act.activation(tg[:, x, :], tg[:, x, :], ACT.Gelu_apprx_tanh).then_inc(s["gelu_done"], 1)
                ffn_high(p, x, 0)

            def ffn_high(p, x, before):
                act.wait_ge(s["yf_done"], p + (before + 1))
                act.wait_ge(s["yf_done"], 1)
                act.activation(yhi[:, bass.ds(p, 1), :].rearrange("p a n -> p (a n)"), yf[:, x, :], ACT.Copy)\
                    .then_inc(s["yhi_done"], 1)

            for p in range(4):
                ffn_act(p, p % 3, p < 3)
            with act.Fori(0, (JF - 4) // 3) as i:
                for r in range(3):
                    ffn_act(3 * i + 4 + r, (4 + r) % 3, False)
            for c in range(KD):
                t = T0["ffn_out"] + c
                act.wait_ge(s["unit_used"], U0["ffn_out"] + 3 * c + 3)
                act.activation(m2[:, c, :], G[:, t % 2, 0, :], ACT.Copy).then_inc(s["evac_done"], 1)
            squares("ffn_post", lambda k: m2[:, k, :], lambda k: act.wait_ge(s["evac_done"], T0["ffn_out"] + k + 1))
            root("ffn_post")

            squares("mix2", lambda k: h[:, k, META:T], lambda k: act.wait_ge(s["h_done"], KD + k + 1))
            act.dma_start(dtab[:, :], consts[:, 576:576 + 896]).then_inc(s["dtab_in"], 16)
            act.dma_start(caus[:, :], consts[:, 448:576]).then_inc(s["caus_in"], 16)
            root("mix2")
            act.wait_ge(s["modv_done"], 1)
            high("mix2", "mix2", 0, lambda k: mod[:, k:k + 1])
            for j in range(4):
                evac("u2", 2 * j, z2[:, j, CONV_W - 1:CONV_W - 1 + SEQ], W=SEQ)
                if j >= 2:
                    act.wait_ge(s["z_done"], j - 1)
                evac("u2", 2 * j + 1, sgm[:, j % 2, :], ACT.Sigmoid, W=SEQ)
            for i in range(4):
                evac("qi2", i, qi2[:, i, :], W=SEQ)
            evac("ki2", 0, ki2[:, :], W=SEQ)
            t = T0["wi2"]
            tile_ready(U0["wi2"])
            act.activation(wi2[:, :, :], G[:, t % 2, 0, :].rearrange("p (a n) -> p a n", a=4)[:, :, 0:8], ACT.Copy,
                           scale=8 ** -0.5).then_inc(s["evac_done"], 1)
            for i in range(4):
                evac("q2", i, q2[:, i, :], W=SEQ)
            for i in range(4):
                evac("k2", i, k2[:, i, :], W=SEQ)
            for i in range(4):
                t = T0["v2"] + i
                tile_ready(U0["v2"] + i)
                act.activation(v2[:, :, i * P:(i + 1) * P], G[:, t % 2, 0, :].rearrange("p (a n) -> p a n", a=4), ACT.Copy)\
                    .then_inc(s["evac_done"], 1)
            act.wait_ge(s["z_done"], 4)
            e = 0
            for b in range(1, 4):
                for j in range(8):
                    act.wait_ge(s["idx_ps"], e + 1)
                    if e >= 2:
                        act.wait_ge(s["idx_acc"], e - 1)
                    act.activation(sgm[:, e % 2, 0:P * (b + 1)], B4[:, e % 4, 0:P * (b + 1)], ACT.Relu, scale=64 ** -0.5)\
                        .then_inc(s["relu_done"], 1)
                    e += 1
            for j in range(4):
                act.wait_ge(s["lnc_done"], j + 1)
                if j >= 2:
                    act.wait_ge(s["lnsq_used"], j - 1)
                act.activation(lnt[:, j % 2, :], cacc[:, j, :], ACT.Square).then_inc(s["lnsq_done"], 1)
            act.wait_ge(s["lnsq_used"], 4)
            act.activation(lnr[:, :], B4[:, 1, :], ACT.Ln, bias=v("eps"), scale=1.0 / CONV_CH).then_inc(s["lnv_read"], 1)
            act.wait_ge(s["lnv_read"], 1)
            act.activation(lnr[:, :], lnr[:, :], ACT.Exp, scale=-0.5).then_inc(s["lnr_done"], 1)
            for j in range(4):
                act.wait_ge(s["lnx_done"], j + 1)
                if j >= 2:
                    act.wait_ge(s["cl_done"], j - 1)
                act.activation(lnt[:, j % 2, :], cacc[:, j, :], ACT.Silu, bias=v("ln_b", j)).then_inc(s["silu_done"], 1)
                act.wait_ge(s["silu_done"], j + 1)
                act.activation(ch[:, j, :], lnt[:, j % 2, :], ACT.Copy).then_inc(s["ch_done"], 1)

            def exp2(q):
                b, hh = q // 8, q % 8
                act.wait_ge(s["nmx2"], q + 1)
                if hh == 0 and b >= 1:
                    act.wait_ge(s["rinv2"], b)
                act.activation(S2[:, q % 3, 0:P * (b + 1)], S2[:, q % 3, 0:P * (b + 1)], ACT.Exp,
                               bias=nmx[:, q % 3:q % 3 + 1], accum_out=rs[:, hh:hh + 1]).then_inc(s["p2_done"], 1)

            def pt2_evac(q):
                b = q // 8
                act.wait_ge(s["t2_ps"], q + 1)
                if q >= 2:
                    act.wait_ge(s["o2_ps"], q - 1)
                act.activation(pt2[:, q % 2, 0:P * (b + 1)], G[:, q % 2, 1, 0:P * (b + 1)], ACT.Copy)\
                    .then_inc(s["pt2_done"], 1)

            gate_tile = 0
            for b in range(4):
                for i in range((0, 2, 3, 3)[b]):
                    evac("ga2", gate_tile, sga[:, gate_tile, :], ACT.Sigmoid, W=SEQ)
                    gate_tile += 1
                for hh in range(9):
                    if hh < 8:
                        exp2(8 * b + hh)
                    if hh >= 1:
                        pt2_evac(8 * b + hh - 1)
                act.wait_ge(s["turned2"], b + 1)
                for f in range(4):
                    act.activation(ah[:, f, P * b:P * (b + 1)], B4[:, 3, f * P:(f + 1) * P], ACT.Copy)\
                        .then_inc(s["ah_done"], 1)
            for i in range(8):
                if i == 0:
                    act.wait_ge(s["al_done"], 16)
                evac("gb2", i, sgb[:, i, :], ACT.Sigmoid, W=SEQ)
            for i in range(4):
                for br in range(2):
                    tile_ready(U0["proj2"] + 2 * i + br)
                    if i >= 1:
                        act.wait_ge(s["ml_done"], 2 * i)
                    for ct in range(2):
                        t = T0["proj2"] + 4 * i + 2 * br + ct
                        act.activation(yab[:, 2 * br + ct, :], G[:, t % 2, (t // 2) % 2, :], ACT.Copy)\
                            .then_inc(s["evac_done"], 1)
                for ct in range(2):
                    c = 2 * i + ct
                    act.wait_ge(s["mrg_done"], c + 1)
                    act.activation(mh[:, c, :], yab[:, ct, :], ACT.Copy).then_inc(s["mh_done"], 1)

            def residual_tiles(name, per, scale, before, rt):
                for c in range(KD):
                    t = T0[name] + c
                    act.wait_ge(s["unit_used"], U0[name] + per * (c + 1))
                    if c >= 2:
                        act.wait_ge(s["h_done"], before + c - 1)
                    act.activation(rt[:, c % 2, :], G[:, t % 2, 0, :], ACT.Copy, scale=scale(c)).then_inc(s["evac_done"], 1)

            residual_tiles("out2", 1, lambda c: mod[:, 16 + c:17 + c], 2 * KD, rt)
            squares("ffn2", lambda k: h[:, k, META:T], lambda k: act.wait_ge(s["h_done"], 2 * KD + k + 1))
            root("ffn2")
            high("ffn2", "ffn2", 0, lambda k: mod[:, 24 + k:25 + k])

            def ffn2_act(p, x, early):
                if not early:
                    act.wait_ge(s["yf_done"], p + (JF - 2))
                ffn_evac("ffn_in2", p, x, 0, tv[:, x, :], ACT.Silu, W=SEQ)
                ffn_evac("ffn_in2", p, x, 1, tg[:, x, :], W=SEQ)
                ffn_high(p, x, JF)

            for p in range(4):
                ffn2_act(p, p % 3, p < 3)
            with act.Fori(0, (JF - 4) // 3) as i:
                for r in range(3):
                    ffn2_act(3 * i + 4 + r, (4 + r) % 3, False)
            residual_tiles("ffn_out2", 3, lambda c: mod[:, 40 + c:41 + c], 3 * KD, tv)
            squares("final", lambda k: h[:, k, META:T], lambda k: act.wait_ge(s["h_done"], 3 * KD + k + 1))
            root("final")

        @block.vector
        def _(dve):
            step = [0]

            def link(ins):
                step[0] += 1
                ins.then_inc(s["dve_step"], 1)
                dve.wait_ge(s["dve_step"], step[0])

            def normalise(norm, group, off, hoff, gain, shift=None):
                r, W = NORMS[norm]
                base = KD * SPLITS[group]
                ub, rstd = scratch(norm)[1], scratch(norm)[2]
                dve.wait_ge(s["rstd_done"], r + 1)
                for k in range(KD + 1):
                    if k < KD:
                        if k >= 2:
                            dve.wait_ge(s["ulo_done"], base + k - 1)
                        dve.scalar_tensor_tensor(ub[:, k % 2, 0:W], h[:, k, hoff:hoff + W], gain(k), rstd[:, 0:W],
                                                 ALU.mult, ALU.mult).then_inc(s["u_done"], 1)
                    if k >= 1:
                        q = k - 1
                        dve.wait_ge(s["uhi_done"], base + q + 1)
                        if shift is None:
                            ins = dve.tensor_tensor(ulo[:, q, off:off + W], ub[:, q % 2, 0:W],
                                                    uhi[:, q, off:off + W].bitcast(F32), ALU.subtract)
                        else:
                            ins = dve.scalar_tensor_tensor(ulo[:, q, off:off + W], ub[:, q % 2, 0:W], shift(q),
                                                           uhi[:, q, off:off + W].bitcast(F32), ALU.add, ALU.subtract)
                        ins.then_inc(s["ulo_done"], 1)
                dve.wait_ge(s["ulo_done"], base + KD)

            def add_normed(norm, m, gain, hoff, count):
                r, W = NORMS[norm]
                ub, rstd = scratch(norm)[1], scratch(norm)[2]
                dve.wait_ge(s["rstd_done"], r + 1)
                for k in range(KD):
                    link(dve.scalar_tensor_tensor(ub[:, k % 2, 0:W], m[:, k, 0:W], gain(k), rstd[:, 0:W],
                                                  ALU.mult, ALU.mult))
                    dve.tensor_tensor(h[:, k, hoff:hoff + W], h[:, k, hoff:hoff + W], ub[:, k % 2, 0:W], ALU.add)\
                       .then_inc(s["h_done"], 1)

            normalise("mix_pre", "mix_pre", 0, 0, lambda k: v("mix_pre", k))

            dve.wait_ge(s["gla_in"], 16)
            for j in range(4):
                b, hp, fwd = j % 2, j % 2, j < 2
                dve.wait_ge(s["gate_ps"], j + 1)
                dve.tensor_scalar(tx[:, b, :].rearrange("p (x w) -> p x w", x=2), B4[:, 2 * b:2 * b + 2, 0:T // 2],
                                  v("gate_bias", j), None, ALU.add).then_inc(s["gate_x"], 1)
                dve.wait_ge(s["gate_ln"], j + 1)
                link(dve.scalar_tensor_tensor(tx[:, b, :], tx[:, b, :], 0.0, te[:, b, :], ALU.min, ALU.subtract))
                flip = slice(None) if fwd else slice(None, None, -1)
                dve.tensor_tensor_scan(kend[:, j, flip], scan_keep[:, j // 2, flip], tx[:, b, flip], 0.0,
                                       ALU.mult, ALU.add).then_inc(s["gate_b"], 1)
                if j == 0:
                    dve.wait_ge(s["evac_done"], T0["k_gl"] + 2)
                dve.wait_ge(s["gate_eb"], 2 * j + 1)
                dve.scalar_tensor_tensor(qdec[:, j, :], qgl[:, hp, :], DK ** -0.5, te[:, b, :], ALU.mult, ALU.mult)\
                   .then_inc(s["gate_used"], 1)
                dve.wait_ge(s["gate_b"], 2 * j + 1)
                e0, e1 = (META - 1, CHUNK - 1) if fwd else (0, 0)
                body = kend[:, j, META:T].rearrange("p (c n) -> p c n", n=CHUNK)
                dve.tensor_tensor(tx[:, b, META:T].rearrange("p (c n) -> p c n", n=CHUNK),
                                  body[:, :, e1:e1 + 1].broadcast_to([P, NCHUNK - 1, CHUNK]), body, ALU.subtract)
                dve.tensor_tensor(tx[:, b, 0:META], kend[:, j, e0:e0 + 1].broadcast_to([P, META]), kend[:, j, 0:META],
                                  ALU.subtract).then_inc(s["gate_b"], 1)
                dve.wait_ge(s["gate_eb"], 2 * j + 2)
                dve.tensor_tensor(kinv[:, j, :], kgl[:, hp, :], te[:, b, :], ALU.mult).then_inc(s["gate_used"], 1)
                dve.wait_ge(s["gate_ed"], j + 1)
                dve.tensor_tensor(kend[:, j, :], kgl[:, hp, :], tx[:, b, :], ALU.mult).then_inc(s["kend_done"], 1)

            dve.wait_ge(s["unit_used"], U0["g_gl"] + 4)
            dve.memset(S[:, 0, 0, :, :], 0.0)
            link(dve.memset(S[:, 1, NCHUNK - 1, :, :], 0.0))
            for i in range(NCHUNK - 1):
                for d, c in ((0, i), (1, NCHUNK - 1 - i)):
                    to = c + 1 if d == 0 else c - 1
                    dve.wait_ge(s["ds_ps"], 2 * i + d + 1)
                    if i >= 1:
                        dve.wait_ge(s["state_done"], 4 * i)
                    for hp in range(2):
                        dve.scalar_tensor_tensor(S[:, d, to, hp, :], S[:, d, c, hp, :], dec[:, 2 * d + hp, c:c + 1],
                                                 B4[:, 2 * (i % 2) + d, hp * DV:(hp + 1) * DV], ALU.mult, ALU.add)\
                           .then_inc(s["state_done"], 1)
            dve.wait_ge(s["gmask_in"], 16)
            link(dve.memset(Amat[:, :, :], 0.0))
            for i in range(5):
                n = P if i < 4 else META
                dve.wait_ge(s["a_ps"], i + 1)
                if i >= 2:
                    dve.wait_ge(s["ogl_ps"], i - 1)
                for par in range(2):
                    for d in range(2):
                        if d == 1:
                            link(last)
                        last = dve.copy_predicated(
                            Amat[0:n, i % 2, 256 * par:256 * par + 256].rearrange("p (a c) -> p a c", a=2)[:, :, 0:n],
                            gmask[0:n, d, 0:n].unsqueeze(1).broadcast_to([n, 2, n]),
                            B4[0:n, 2 * (i % 2) + par, 256 * d:256 * d + 256].rearrange("p (a c) -> p a c", a=2)[:, :, 0:n])
                last.then_inc(s["amat_done"], 1)
            dve.wait_ge(s["evac_done"], T0["g_gl"] + 4)
            for hh in range(GLA_H):
                dve.wait_ge(s["grs_done"], hh + 1)
                link(dve.scalar_tensor_tensor(oT[:, hh, :], oT[:, hh, :], v("gla_gain"), grs[:, hh % 2, :],
                                              ALU.mult, ALU.mult))
                dve.tensor_tensor(oT[:, hh, :], oT[:, hh, :], sg[:, hh, :], ALU.mult).then_inc(s["ogl_out"], 1)

            dve.wait_ge(s["bias_in"], 16)
            dve.wait_ge(s["wmask_in"], 16)

            def na_soft(st):
                a, hp = st // 4, st % 4
                c0, W = na_window(a)
                w0 = c0 - 16 * (a - 1)
                b = st % 2
                dve.wait_ge(s["na_s_ps"], st + 1)
                if st >= 2:
                    dve.wait_ge(s["na_t_ps"], 2 * (st - 1))
                dve.scalar_tensor_tensor(sc[:, b, :, 0:8 * W], B4[:, 2 * b:2 * b + 2, 0:8 * W], DH ** -0.5,
                                         biasn[:, 2 * hp:2 * hp + 2, 8 * w0:8 * (w0 + W)], ALU.mult, ALU.add)
                dve.tensor_scalar(sc[:, b, :, 8 * W:8 * W + META], B4[:, 2 * b:2 * b + 2, 8 * W:8 * W + META],
                                  DH ** -0.5, None, ALU.mult).then_inc(s["na_s"], 1)
                dve.wait_ge(s["na_s"], st + 1)
                for par in range(2):
                    x = sc[:, b, par, 0:8 * W].rearrange("p (w r) -> p w r", r=8)
                    last = dve.tensor_tensor(x, x, wmask[:, a, 0:W].unsqueeze(2).broadcast_to([P, W, 8]), ALU.add)
                link(last)
                link(dve.tensor_reduce(mx[:, 0:2], sc[:, b, :, 0:8 * W + META], AX.X, ALU.max))
                dve.tensor_scalar(nmx[:, 2 * b:2 * b + 2], mx[:, 0:2], -1.0, None, ALU.mult).then_inc(s["na_nmx"], 1)

            def na_out(a, n=P):
                dve.reciprocal(rinv[0:n], rs[0:n]).then_inc(s["na_rinv"], 1)
                dve.wait_ge(s["na_rinv"], a + 1)
                dve.wait_ge(s["na_o_ps"], 8 * (a + 1) if a < 4 else 33)
                dve.tensor_tensor(otok[0:n].rearrange("p (h e) -> p h e", h=NA_H),
                                  G[0:n, 1, 0, :].rearrange("p (h e) -> p h e", h=NA_H),
                                  rinv[0:n].unsqueeze(2).broadcast_to([n, NA_H, DH]), ALU.mult)\
                   .then_inc(s["na_o_scaled"], 1)
                dve.wait_ge(s["na_rstd"], a + 1)
                dve.tensor_scalar(otok[0:n], otok[0:n], rstdn[0:n], None, ALU.mult).then_inc(s["na_otok"], 1)

            for st in range(17):
                if st < 16:
                    na_soft(st)
                if st >= 1:
                    q = st - 1
                    a = q // 4
                    nb = na_window(a)[1] // 16
                    dve.wait_ge(s["na_t_ps"], 2 * q + 2)
                    if q >= 1:
                        dve.wait_ge(s["na_o_ps"], 2 * q)
                    dve.tensor_copy(pt[:, 1, 0:nb * P], G[:, 0, 1, 0:nb * P])
                    dve.tensor_copy(pt[0:META, 1, 384:512], G[0:META, 0, 1, 384:512]).then_inc(s["na_pt1"], 1)
                    if q % 4 == 3:
                        dve.wait_ge(s["na_p"], 8 * (a + 1))
                        na_out(a)
            dve.wait_ge(s["meta_s_ps"], 1)
            ms = sc[0:META, 0, 0, 0:P].rearrange("p (h k) -> p h k", h=NA_H)
            link(dve.tensor_scalar(sc[0:META, 0, 0, 0:P].rearrange("p (a n) -> p a n", a=2), B4[0:META, 0:2, 0:64],
                                   DH ** -0.5, None, ALU.mult))
            link(dve.tensor_reduce(mx[0:META], ms, AX.X, ALU.max))
            dve.tensor_tensor(ms, ms, mx[0:META].unsqueeze(2).broadcast_to([META, NA_H, META]), ALU.subtract)\
               .then_inc(s["meta_s"], 1)
            dve.wait_ge(s["meta_e"], 1)
            link(dve.tensor_reduce(rs[0:META].rearrange("p (b a) -> p a b", a=2), ms.rearrange("p (a b) k -> p a b k", a=2),
                                   AX.X, ALU.add))
            na_out(4, META)

            for k in range(KD):
                dve.wait_ge(s["uhi_done"], KD * SPLITS["mix"] + k + 1)
                src = onaT[:, k, :] if k < 4 else oT[:, k - 4, :]
                dve.tensor_tensor(ulo[:, k, :], src, uhi[:, k, :].bitcast(F32), ALU.subtract).then_inc(s["ulo_done"], 1)
            dve.wait_ge(s["mod_done"], 1)
            add_normed("mix_post", m1, lambda k: v("mix_post", k), FT0, 0)
            normalise("ffn_pre", "ffn_pre", 0, FT0, lambda k: v("ffn_pre", k))

            dve.memset(av[:, :, FT:FT + 1], 0.0)
            link(dve.memset(ag[:, :, FT:FT + 1], 0.0))

            def conv3(p, x, half, early):
                src, dst = ((av, tv), (ag, tg))[half]
                w = lambda k: vec[:, bass.ds(VCOL["cw"] + 44 * k + half + 2 * p, 1)]
                taps = [src[:, x, META - FT0 - 1 + k:META - FT0 - 1 + k + SEQ] for k in range(3)]
                dve.wait_ge(s["evac_done"], 2 * p + (T0["ffn_in"] + half + 1))
                if not early:
                    dve.wait_ge(s["ylow_done"], p - 2)
                dve.tensor_scalar(dst[:, x, :], taps[0], w(0), vec[:, bass.ds(VCOL["cb"] + half + 2 * p, 1)],
                                  ALU.mult, ALU.add).then_inc(s["conv_step"], 1)
                dve.wait_ge(s["conv_step"], 4 * p + (2 * half + 1))
                dve.scalar_tensor_tensor(dst[:, x, :], taps[1], w(1), dst[:, x, :], ALU.mult, ALU.add)\
                   .then_inc(s["conv_step"], 1)
                dve.wait_ge(s["conv_step"], 4 * p + (2 * half + 2))
                dve.scalar_tensor_tensor(dst[:, x, :], taps[2], w(2), dst[:, x, :], ALU.mult, ALU.add)\
                   .then_inc(s["conv_done"], 1)

            def gated(p, x, before):
                dve.tensor_tensor(yf[:, x, :], tv[:, x, :], tg[:, x, :], ALU.mult).then_inc(s["yf_done"], 1)
                dve.wait_ge(s["yhi_done"], p + (before + 1))
                dve.tensor_tensor(ylo[:, bass.ds(p, 1), :].rearrange("p a n -> p (a n)"), yf[:, x, :],
                                  yhi[:, bass.ds(p, 1), :].rearrange("p a n -> p (a n)").bitcast(F32), ALU.subtract)\
                   .then_inc(s["ylow_done"], 1)

            def ffn_dve(p, x, early):
                conv3(p, x, 0, early)
                conv3(p, x, 1, early)
                dve.wait_ge(s["gelu_done"], p + 1)
                gated(p, x, 0)

            for p in range(4):
                ffn_dve(p, p % 3, p < 3)
            with dve.Fori(0, (JF - 4) // 3) as i:
                for r in range(3):
                    ffn_dve(3 * i + 4 + r, (4 + r) % 3, False)
            add_normed("ffn_post", m2, lambda k: v("ffn_post", k), META, KD)

            link(dve.tensor_tensor(mod, mod, v("b_ada", 0, 48), ALU.add))
            dve.scalar_tensor_tensor(gm2, mod[:, 8:16], 1.0, v("mix2", 0, 8), ALU.add, ALU.mult)
            dve.scalar_tensor_tensor(gf2, mod[:, 32:40], 1.0, v("ffn2", 0, 8), ALU.add, ALU.mult).then_inc(s["modv_done"], 1)
            dve.wait_ge(s["modv_done"], 1)
            normalise("mix2", "mix2", 0, META, lambda k: gm2[:, k:k + 1], lambda k: mod[:, k:k + 1])
            link(dve.memset(z2[:, :, 0:CONV_W - 1], 0.0))
            for j in range(4):
                dve.wait_ge(s["evac_done"], T0["u2"] + 2 * j + 2)
                x = z2[:, j, CONV_W - 1:CONV_W - 1 + SEQ]
                dve.tensor_tensor(x, x, sgm[:, j % 2, :], ALU.mult).then_inc(s["z_done"], 1)
            dve.wait_ge(s["z_done"], 4)
            for j in range(4):
                dve.tensor_scalar(cacc[:, j, :], z2[:, j, 0:SEQ], v("w_dw", j), v("b_dw", j), ALU.mult, ALU.add)\
                   .then_inc(s["tap_done"], 1)
            with dve.Fori(1, CONV_W - 1) as k:
                for j in range(4):
                    dve.wait_ge(s["tap_done"], 4 * k + (j - 3))
                    dve.scalar_tensor_tensor(cacc[:, j, :], z2[:, j, bass.ds(k, SEQ)],
                                             vec[:, bass.ds(VCOL["w_dw"] + j + 4 * k, 1)], cacc[:, j, :],
                                             ALU.mult, ALU.add).then_inc(s["tap_done"], 1)
            for j in range(4):
                k = CONV_W - 1
                dve.wait_ge(s["tap_done"], 4 * k + (j - 3))
                dve.scalar_tensor_tensor(cacc[:, j, :], z2[:, j, k:k + SEQ], v("w_dw", 4 * k + j), cacc[:, j, :],
                                         ALU.mult, ALU.add).then_inc(s["conv31_done"], 1)

            def scx(b):
                first = (0, 0, 256, 640)[b]
                return scb[:, first:first + P * (b + 1)]

            dve.wait_ge(s["evac_done"], T0["wi2"] + 1)
            e = 0
            for b in range(1, 4):
                for j in range(8):
                    dve.wait_ge(s["relu_done"], e + 1)
                    r = sgm[:, e % 2, 0:P * (b + 1)]
                    w = wi2[:, b, j:j + 1]
                    if j == 0:
                        ins = dve.tensor_scalar(scx(b), r, w, None, ALU.mult)
                    else:
                        ins = dve.scalar_tensor_tensor(scx(b), r, w, scx(b), ALU.mult, ALU.add)
                    ins.then_inc(s["idx_acc"], 1)
                    e += 1
                    dve.wait_ge(s["idx_acc"], e)
            dve.wait_ge(s["ln_ps"], 1)
            for j in range(4):
                dve.scalar_tensor_tensor(cacc[:, j, :], B4[:, 0, :], -1.0 / CONV_CH, cacc[:, j, :], ALU.mult, ALU.add)\
                   .then_inc(s["lnc_done"], 1)
            dve.wait_ge(s["lnc_done"], 4)
            dve.memset(mx[:, 0:1], 0.0).then_inc(s["ln_read"], 1)
            dve.wait_ge(s["lnr_done"], 1)
            for j in range(4):
                dve.scalar_tensor_tensor(cacc[:, j, :], cacc[:, j, :], v("ln_g", j), lnr[:, :], ALU.mult, ALU.mult)\
                   .then_inc(s["lnx_done"], 1)
            for j in range(4):
                dve.wait_ge(s["ch_done"], j + 1)
                dve.tensor_tensor(cl[:, j, :], lnt[:, j % 2, :], ch[:, j, :].bitcast(F32), ALU.subtract)\
                   .then_inc(s["cl_done"], 1)

            dve.wait_ge(s["caus_in"], 16)
            dve.wait_ge(s["dtab_in"], 16)

            def select(b):
                x = scx(b)
                diag = x[:, P * b:P * (b + 1)]
                link(dve.tensor_tensor(diag, diag, caus[:, :], ALU.add))
                for _ in range(TOPK // 8):
                    link(dve.max(top8, x))
                    link(dve.match_replace(x, top8, x, TAKEN))
                link(dve.tensor_scalar(x, x, TAKEN / 2, -1e30, ALU.is_gt, ALU.mult))

            def soft2(q):
                b, hh = q // 8, q % 8
                W = P * (b + 1)
                dve.wait_ge(s["s2_ps"], q + 1)
                if q >= 3:
                    dve.wait_ge(s["t2_ps"], q - 2)
                x = S2[:, q % 3, 0:W]
                link(dve.scalar_tensor_tensor(x, dtab[:, 384 - P * b:384 - P * b + W], 2.0 ** -(hh + 1),
                                              scx(b) if b else caus[:, :], ALU.mult, ALU.add))
                dve.scalar_tensor_tensor(x, B4[:, q % 3, 0:W], 64 ** -0.5, x, ALU.mult, ALU.add).then_inc(s["s2_read"], 1)
                dve.wait_ge(s["s2_read"], q + 1)
                link(dve.tensor_reduce(mx[:, 0:1], x, AX.X, ALU.max))
                dve.tensor_scalar(nmx[:, q % 3:q % 3 + 1], mx[:, 0:1], -1.0, None, ALU.mult).then_inc(s["nmx2"], 1)
                dve.wait_ge(s["nmx2"], q + 1)

            for b in range(4):
                if b:
                    select(b)
                for hh in range(8):
                    soft2(8 * b + hh)
                dve.wait_ge(s["p2_done"], 8 * b + 8)
                dve.reciprocal(rinv, rs).then_inc(s["rinv2"], 1)
                dve.wait_ge(s["rinv2"], b + 1)
                dve.wait_ge(s["o2_ps"], 8 * b + 8)
                dve.tensor_tensor(otok2[:, :].rearrange("p (h e) -> p h e", h=8),
                                  B4[:, 3, :].rearrange("p (h e) -> p h e", h=8),
                                  rinv.unsqueeze(2).broadcast_to([P, 8, 64]), ALU.mult).then_inc(s["otok2_done"], 1)
                for f in range(4):
                    dve.wait_ge(s["ah_done"], 4 * b + 4)
                    dve.tensor_tensor(al[:, f, P * b:P * (b + 1)], B4[:, 3, f * P:(f + 1) * P],
                                      ah[:, f, P * b:P * (b + 1)].bitcast(F32), ALU.subtract).then_inc(s["al_done"], 1)

            for i in range(4):
                dve.wait_ge(s["evac_done"], T0["proj2"] + 4 * (i + 1))
                for ct in range(2):
                    c = 2 * i + ct
                    dve.tensor_tensor(yab[:, ct, :], yab[:, ct, :], sga[:, c, :], ALU.mult)
                    link(dve.tensor_tensor(yab[:, 2 + ct, :], yab[:, 2 + ct, :], sgb[:, c, :], ALU.mult))
                    dve.tensor_tensor(yab[:, ct, :], yab[:, ct, :], yab[:, 2 + ct, :], ALU.add).then_inc(s["mrg_done"], 1)
                for ct in range(2):
                    c = 2 * i + ct
                    dve.wait_ge(s["mh_done"], c + 1)
                    dve.tensor_tensor(ml[:, c, :], yab[:, ct, :], mh[:, c, :].bitcast(F32), ALU.subtract)\
                       .then_inc(s["ml_done"], 1)

            def add_residual(name, rt):
                for c in range(KD):
                    dve.wait_ge(s["evac_done"], T0[name] + c + 1)
                    dve.tensor_tensor(h[:, c, META:T], h[:, c, META:T], rt[:, c % 2, :], ALU.add).then_inc(s["h_done"], 1)

            add_residual("out2", rt)
            normalise("ffn2", "ffn2", 0, META, lambda k: gf2[:, k:k + 1], lambda k: mod[:, 24 + k:25 + k])

            def ffn2_dve(p, x):
                dve.wait_ge(s["evac_done"], 2 * p + (T0["ffn_in2"] + 2))
                gated(p, x, JF)

            for p in range(4):
                ffn2_dve(p, p % 3)
            with dve.Fori(0, (JF - 4) // 3) as i:
                for r in range(3):
                    ffn2_dve(3 * i + 4 + r, (4 + r) % 3)
            add_residual("ffn_out2", tv)
            dve.wait_ge(s["rstd_done"], 7)
            for k in range(KD):
                dve.scalar_tensor_tensor(res[:, k, :], h[:, k, META:T], v("final", k), rstd2[:, 0:SEQ], ALU.mult, ALU.mult)\
                   .then_inc(s["res_done"], 1)


def _columns(w, cols):
    cols = list(cols)
    units = []
    for i in range(0, len(cols), P):
        c = cols[i:i + P]
        u = np.zeros((P, KD, P), np.float32)
        u[:, :, :len(c)] = w[:, c].reshape(KD, P, len(c)).transpose(1, 0, 2)
        units.append(u.reshape(P, KD * P))
    return units


def _deep(w):
    units = []
    for c in range(KD):
        b = np.zeros((24, P, P), np.float32)
        b[:JF] = w[:, c * P:(c + 1) * P].reshape(JF, P, P)
        units += list(b.reshape(3, BLK, P, P).transpose(0, 2, 1, 3).reshape(3, P, BLK * P))
    return units


def _shallow(w, i):
    return w[:, 256 * i:256 * (i + 1)].reshape(4, P, 2, P).transpose(1, 2, 0, 3).reshape(P, BLK * P)


def layout(x):
    f = {k: np.asarray(a) for k, a in x.items()}
    w1, w2 = f["w_in"][0], f["w_in_2"][0]
    o = np.cumsum([0, 512, 512, 512, 256, 256, 512, 512, 32])
    r = lambda a, n=None: range(o[a], o[a + 1])
    stream = _columns(w1, r(7)) + _columns(w1, r(3)) + _columns(w1, r(4)) + _columns(w1, r(5))
    stream += _columns(w1, r(0)) + _columns(w1, r(1)) + _columns(w1, r(2)) + _columns(w1, r(6))
    stream += _columns(f["w_o"][0], range(D))
    ffn = [c for j in range(JF) for half in (0, DFF) for c in range(half + P * j, half + P * (j + 1))]
    stream += _columns(f["w_ffn_in"][0], ffn) + _deep(f["w_ffn_out"][0])
    q2, k2, v2, qi, ki, wi, u2, ga, gb = np.cumsum([0, 512, 512, 512, 512, 64, 8, 1024, 1024])
    span = lambda a, n: range(a, a + n)
    stream += _columns(w2, [c for j in range(4) for half in (0, CONV_CH) for c in span(u2 + half + P * j, P)])
    stream += _columns(w2, span(qi, 512)) + _columns(w2, list(span(ki, 64)) * 2) + _columns(w2, span(wi, 8))
    stream += _columns(w2, span(q2, 512)) + _columns(w2, span(k2, 512)) + _columns(w2, span(v2, 512))
    stream += _columns(w2, span(ga, 1024)) + _columns(w2, span(gb, 1024))
    for i in range(4):
        stream += [_shallow(f["w_attn_proj_2"][0], i), _shallow(f["w_conv_proj_2"][0], i)]
    stream += _columns(f["w_out_2"][0], range(D))
    stream += _columns(f["w_ffn_in_2"][0], ffn) + _deep(f["w_ffn_out_2"][0])
    stream = np.stack(stream[:NUNIT])

    h = np.concatenate([f["meta_tokens"], f["x"][0]], axis=0)
    h = np.ascontiguousarray(h.T.reshape(KD, P, T).transpose(1, 0, 2))
    col = lambda a: np.asarray(a).reshape(-1, P).T
    vecs = {"mix_pre": f["norm_mix_pre"], "na_gain": f["na_out_gain"],
            "gate_bias": np.concatenate([f["gla_gate_bias_fwd"], f["gla_gate_bias_bwd"]], 1),
            "gla_gain": f["gla_out_gain"], "mix_post": f["norm_mix_post"], "ffn_pre": f["norm_ffn_pre"],
            "cw": f["ffn_conv_w"], "cb": f["ffn_conv_b"], "ffn_post": f["norm_ffn_post"],
            "mix2": f["norm_mix_g_2"], "w_dw": f["w_dw_2"], "b_dw": f["b_dw_2"], "ln_g": f["conv_ln_g_2"],
            "ln_b": f["conv_ln_b_2"], "ffn2": f["norm_ffn_g_2"], "b_ada": f["b_ada_2"],
            "final": f["norm_final_g_2"], "c": f["c_2"], "eps": np.full((1, P), EPS, np.float32)}
    pairs = lambda a: np.asarray(a).reshape(-1, 2, JF, P).transpose(0, 2, 1, 3)
    vecs["cw"], vecs["cb"] = pairs(vecs["cw"]), pairs(vecs["cb"])
    vecs = np.ascontiguousarray(np.concatenate([col(vecs[n]) for n, _ in VECS], 1))
    assert vecs.shape[1] == NVEC

    p = np.arange(P)
    ident = np.eye(P, dtype=np.float32)
    onesm = np.ones((P, P), np.float32)
    wmask = np.zeros((P, 4, 48), np.float32)
    for a in range(4):
        lo, W = na_window(a)
        c, key = 16 * a + p // 8, lo + np.arange(W)
        first = np.clip(c - 8, 0, GRID_W - 16)
        seen = (key[None] >= first[:, None]) & (key[None] < first[:, None] + 16)
        wmask[:, a, :W] = np.where(seen, 0.0, -1e30)
    causal = np.where(p[None] <= p[:, None], 0.0, -1e30).astype(np.float32)
    dist = (np.arange(896)[None] - 384 - p[:, None]).astype(np.float32)
    consts = np.ascontiguousarray(np.concatenate([ident, onesm, wmask.reshape(P, -1), causal, dist], 1))
    same = (p[:, None] // CHUNK) == (p[None] // CHUNK)
    masks = np.stack([same & (p[:, None] <= p[None]), same & (p[:, None] > p[None])], 1).astype(np.int32)
    keep = np.ones((P, 2, T), np.float32)
    keep[:, 0, META::CHUNK] = 0.0
    keep[:, 1, META - 1::CHUNK] = 0.0

    rpb = np.zeros((NA_H, 15, 64), np.float32)
    rpb[:, :, 16:47] = f["na_rel_bias"][0]
    bias = np.zeros((P, NA_H, 48, 8), np.float32)
    for q in range(P):
        bias[q] = rpb[:, 7 - q % 8:15 - q % 8, 15 - q // 8:63 - q // 8].transpose(0, 2, 1)
    bias = bias.reshape(P, NA_H, 384)
    up = np.zeros((32, 512), np.float32)
    up[:RANK, :256] = f["gla_gate_up_fwd"][0]
    up[RANK:, 256:] = f["gla_gate_up_bwd"][0]
    ada = np.stack(_columns(f["w_ada_2"][0], range(NMOD * D)))
    return {"wstream": stream, "ada": ada, "hT": h, "vecs": vecs, "consts": consts, "masks": masks,
            "scanm": keep, "bias": bias, "up": up}


def kernel(**inputs):
    import concourse.bacc as bacc
    from concourse.bass_utils import run_bass_kernel_spmd

    arrays = layout(inputs)
    nc = bacc.Bacc("TRN2", target_bir_lowering=False, num_devices=1)
    aps = {n: nc.dram_tensor(n, a.shape, mybir.dt.from_np(a.dtype), kind="ExternalInput").ap()
           for n, a in arrays.items()}
    out = nc.dram_tensor("out", (P, KD, SEQ), F32, kind="ExternalOutput").ap()
    build(nc, out=out, **aps)
    result = run_bass_kernel_spmd(nc, [arrays], core_ids=[0]).results[0]["out"]
    return np.ascontiguousarray(np.asarray(result).transpose(2, 1, 0).reshape(1, SEQ, D))
```

```python
import numpy as np
import concourse.bass as bass
from concourse import mybir
from contextlib import ExitStack

F32 = mybir.dt.float32
F32R = mybir.dt.float32r
I32 = mybir.dt.int32
ALU = mybir.AluOpType
ACT = mybir.ActivationFunctionType
AX = mybir.AxisListType

P = 128
D = 1024
KD = D // P
SEQ = 512
META = 16
T = META + SEQ
EPS = 1e-6
GRID_W, GRID_R = 64, 8
NA_H, DH = 8, 64
GLA_H, DK, DV, CHUNK = 4, 64, 128, 64
NCHUNK = SEQ // CHUNK + 1
RANK = 16
DFF = 2816
JF = DFF // P
CONVF = 3
CONV_CH, CONV_W = 512, 31
NMOD = 6
FT0 = 12
FT = T - FT0
TOPK = 128
TAKEN = -3e38
RING = 3
BLK = 8
ADA_RING = 4

VECS = [("mix_pre", 8), ("na_gain", 4), ("gate_bias", 4), ("gla_gain", 1), ("mix_post", 8),
        ("ffn_pre", 8), ("cw", 44 * CONVF), ("cb", 44), ("ffn_post", 8),
        ("mix2", 8), ("w_dw", 4 * CONV_W), ("b_dw", 4), ("ln_g", 4), ("ln_b", 4), ("ffn2", 8),
        ("b_ada", 48), ("final", 8), ("c", 8), ("eps", 1)]
VCOL = {}
_at = 0
for _n, _w in VECS:
    VCOL[_n] = _at
    _at += _w
NVEC = _at

UNITS = [("z", 1), ("q_gl", 2), ("k_gl", 2), ("v_gl", 4), ("q_na", 4), ("k_na", 4), ("v_na", 4),
         ("g_gl", 4), ("w_o", 8), ("ffn_in", 2 * JF), ("ffn_out", 24),
         ("u2", 8), ("qi2", 4), ("ki2", 1), ("wi2", 1), ("q2", 4), ("k2", 4), ("v2", 4),
         ("ga2", 8), ("gb2", 8), ("proj2", 8), ("out2", 8), ("ffn_in2", 2 * JF), ("ffn_out2", 24)]
U0 = {}
_at = 0
for _n, _w in UNITS:
    U0[_n] = _at
    _at += _w
NUNIT = _at

T0 = {}
_at = 0
for _n, _w in UNITS:
    T0[_n] = _at
    _at += {"ffn_out": 8, "ffn_out2": 8, "proj2": 16}.get(_n, _w)


def na_window(a):
    lo, hi = max(0, 16 * (a - 1)), min(GRID_W, 16 * (a + 2))
    return lo, hi - lo


def chunk_place(c):
    if c == 0:
        return 4, 0, META, 0
    return (c - 1) // 2, CHUNK * ((c - 1) % 2), CHUNK, META + CHUNK * (c - 1)


def build(nc, wstream, ada, hT, vecs, consts, masks, scanm, bias, up, out):
    ctx = ExitStack()
    with ctx:

        def sb(name, shape, at, dt=F32):
            return nc.alloc_sbuf_tensor_at(name, shape, dt, offset=at)

        class Signals(dict):
            def __missing__(self, name):
                self[name] = ctx.enter_context(nc.semaphore(name))
                return self[name]

        s = Signals()

        at = 16512
        h = sb("h", [P, KD, T], at); at += KD * T * 4
        U_AT = at
        uhi = sb("uhi", [P, KD, T], at, F32R); at += KD * T * 4
        ulo = sb("ulo", [P, KD, T], at, F32R); at += KD * T * 4
        raw = sb("raw", [P, RING, BLK * P], at); at += RING * BLK * P * 4
        whi = sb("whi", [P, RING, BLK * P], at, F32R); at += RING * BLK * P * 4
        wlo = sb("wlo", [P, RING, BLK * P], at, F32R); at += RING * BLK * P * 4
        vec = sb("vec", [P, NVEC], at); at += -(-4 * NVEC // 64) * 64
        ident = sb("ident", [P, P], at); at += 512
        ones = sb("ones", [P, P], at); at += 512
        one_col = sb("one_col", [P, 1], at); at += 64
        small = sb("small", [P, 160], at); at += 640
        A0 = -(-at // 64) * 64

        def arena(offset):
            return A0 + offset

        def v(name, k=0, n=1):
            return vec[:, VCOL[name] + k:VCOL[name] + k + n]

        csilu = small[:, 0:8]
        mod = small[:, 8:56]
        gm2 = small[:, 56:64]
        gf2 = small[:, 64:72]
        mx = small[:, 72:80]
        nmx = small[:, 80:88]
        rs = small[:, 88:96]
        rinv = small[:, 96:104]
        ssn = small[:, 104:105]
        rstdn = small[:, 105:106]
        top8 = small[:, 112:120]
        row_sum = small[:, 120:136].rearrange("p (b h) -> p b h", b=2)

        o = 0
        qna = sb("qna", [P, 4, T], arena(o)); o += 8448
        kna = sb("kna", [P, 4, T], arena(o)); o += 8448
        vna = sb("vna", [P, 5, 512], arena(o)); o += 10240
        vgl = sb("vgl", [P, 5, 512], arena(o)); o += 10240
        sg = sb("sg", [P, 4, T], arena(o)); o += 8448
        biasn = sb("biasn", [P, NA_H, 48 * 8], arena(o)); o += 12288
        KEND = o
        kend = sb("kend", [P, 4, T], arena(o)); o += 8448
        QDEC = o
        qdec = sb("qdec", [P, 4, T], arena(o)); o += 8448
        KINV = o
        kinv = sb("kinv", [P, 4, T], arena(o)); o += 8448
        QGL = o
        qgl = sb("qgl", [P, 2, T], arena(o)); o += 4224
        kgl = sb("kgl", [P, 2, T], arena(o)); o += 4224
        TX = o
        tx = sb("tx", [P, 2, T], arena(o)); o += 4224
        TE = o
        te = sb("te", [P, 2, T], arena(o)); o += 4224
        scan_keep = sb("scan_keep", [P, 2, T], arena(o)); o += 4224
        zT = sb("zT", [32, T], arena(o)); o += 2112
        upt = sb("upt", [32, 512], arena(o)); o += 2048
        dec = sb("dec", [P, 4, NCHUNK], arena(o)); o += 192
        gmask = sb("gmask", [P, 2, P], arena(o), I32); o += 1024
        wmask = sb("wmask", [P, 4, 48], arena(o)); o += 768
        sq1 = sb("sq1", [P, 2, T], arena(KEND))
        ub1 = sb("ub1", [P, 2, T], arena(KEND + 4224))
        rstd1 = sb("rstd1", [P, T], arena(QDEC))
        kendT = sb("kendT", [P, 5, 512], U_AT)
        S = sb("S", [P, 2, NCHUNK, 2, DV], U_AT + 10240)
        Amat = sb("Amat", [P, 2, 512], U_AT + 28672)
        oT = sb("oT", [P, 4, T], arena(KEND))
        onaT = sb("onaT", [P, 4, T], arena(QDEC))
        gsq = sb("gsq", [P, 2, T], arena(KINV))
        grs = sb("grs", [P, 2, T], arena(KINV + 4224))
        sc = sb("sc", [P, 3, 2, 400], arena(QGL))
        vT = sb("vT", [P, 4, T], arena(TX))
        pt = sb("pt", [P, 2, 2, 512], arena(QGL + 9600))
        otok = sb("otok", [P, 512], arena(QGL + 17792))
        osq = sb("osq", [P, 512], arena(QGL + 19840))
        yhi = sb("yhi", [P, JF, SEQ], arena(0), F32R)
        ylo = sb("ylo", [P, JF, SEQ], arena(45056), F32R)
        FB = 90112
        av = sb("av", [P, 3, FT + 4], arena(FB))
        ag = sb("ag", [P, 3, FT + 4], arena(FB + 6240))
        tv = sb("tv", [P, 3, SEQ], arena(FB + 12480))
        tg = sb("tg", [P, 3, SEQ], arena(FB + 18624))
        yf = sb("yf", [P, 3, SEQ], arena(FB + 24768))
        m1 = sb("m1", [P, KD, FT], arena(0))
        sq2 = sb("sq2", [P, 2, T], arena(FB))
        ub2 = sb("ub2", [P, 2, T], arena(FB + 4224))
        rstd2 = sb("rstd2", [P, T], arena(FB + 8448))
        m2 = sb("m2", [P, KD, SEQ], U_AT)
        ada_in = sb("ada_in", [P, ADA_RING, 1024], U_AT + 16384)
        ada_acc = sb("ada_acc", [P, NMOD * 1024], arena(FB))
        sq3 = sb("sq3", [P, 2, SEQ], arena(FB + 24768))
        rstd3 = sb("rstd3", [P, SEQ], arena(FB + 28864))
        ub3 = sb("ub3", [P, 2, SEQ], arena(0))

        z2 = sb("z2", [P, 4, CONV_W - 1 + SEQ], arena(0))
        ch = sb("ch", [P, 4, SEQ], arena(0), F32R)
        cacc = sb("cacc", [P, 4, SEQ], arena(8704))
        cl = sb("cl", [P, 4, SEQ], arena(8704), F32R)
        sgm = sb("sgm", [P, 2, SEQ], arena(16896))
        rt = sb("rt", [P, 2, SEQ], arena(16896))
        q2 = sb("q2_", [P, 4, SEQ], arena(20992))
        k2 = sb("k2_", [P, 4, SEQ], arena(29184))
        qi2 = sb("qi2_", [P, 4, SEQ], arena(37376))
        ki2 = sb("ki2_", [P, SEQ], arena(45568))
        v2 = sb("v2_", [P, 4, 512], arena(47616))
        mh = sb("mh", [P, KD, SEQ], arena(20992), F32R)
        ml = sb("ml", [P, KD, SEQ], arena(72320), F32R)
        yab = sb("yab", [P, 4, SEQ], arena(47616))
        wi2 = sb("wi2_", [P, 4, 8], arena(55808))
        sga = sb("sga", [P, KD, SEQ], arena(55936))
        sgb = [sb("sgb0", [P, 4, SEQ], arena(37376)), sb("sgb1", [P, 4, SEQ], arena(109696))]
        scb = sb("scb", [P, 1152], arena(72320))
        S2 = sb("S2", [P, 3, SEQ], arena(76928))
        pt2 = sb("pt2", [P, 2, SEQ], arena(83072))
        otok2 = sb("otok2", [P, 512], arena(87168))
        sq4 = sb("sq4", [P, 2, T], arena(76928))
        ub4 = sb("ub4", [P, 2, T], arena(81152))
        rstd4 = sb("rstd4", [P, T], arena(85376))
        dtab = sb("dtab", [P, 896], arena(89216))
        caus = sb("caus", [P, P], arena(92800))
        ah = sb("ah", [P, 4, SEQ], arena(93312), F32R)
        al = sb("al", [P, 4, SEQ], arena(101504), F32R)
        lnt = sb("lnt", [P, 2, SEQ], arena(109696))
        lnr = sb("lnr", [P, SEQ], arena(113792))
        res = sb("res", [P, KD, SEQ], U_AT)

        G = ctx.enter_context(nc.psum_tensor("G", [P, 2, 2, 512], F32))
        B4 = ctx.enter_context(nc.psum_tensor("B4", [P, 4, 512], F32))

        def norm_halves(W):
            return (1, W) if W <= 512 else (2, W // 2)

        ROWS4 = [(0, META + SEQ // 2), (META + SEQ // 2, SEQ // 2)]

        NORMS = {"mix_pre": (0, T), "mix_post": (1, FT), "ffn_pre": (2, FT), "ffn_post": (3, SEQ),
                 "mix2": (4, SEQ), "ffn2": (5, SEQ), "final": (6, SEQ)}
        SPLITS = {"mix_pre": 0, "mix": 1, "ffn_pre": 2, "mix2": 3, "ffn2": 4}

        def scratch(norm):
            return {"mix_pre": (sq1, ub1, rstd1), "ffn_post": (sq3, ub3, rstd3),
                    "mix2": (sq4, ub4, rstd4)}.get(norm, (sq2, ub2, rstd2))

        block = ctx.enter_context(nc.Block())

        @block.sync
        def _(sp):
            for k in range(KD):
                sp.dma_start(h[:, k, :], hT[:, k, :]).then_inc(s[f"h_in{k % 2}"], 16)
            sp.dma_start(vec[:, :], vecs).then_inc(s["vec_in"], 16)
            sp.dma_start(ones[:, :], consts[:, P:2 * P]).then_inc(s["ones_in"], 16)

            def load_unit(n, i, wait):
                if wait is not None:
                    sp.wait_ge(s["unit_split"], wait)
                sp.dma_start(raw[:, i, :], wstream[bass.ds(n, 1), :, :].rearrange("a p n -> p (a n)"))\
                    .then_inc(s[f"unit_in{i}"], 16)

            for n in range(RING):
                load_unit(n, n, None)
            sp.dma_start(ident[:, :], consts[:, 0:P]).then_inc(s["ident_in"], 16)
            sp.dma_start(scan_keep[:, :, :], scanm).then_inc(s["gla_in"], 16)
            sp.dma_start(upt[:, :], up).then_inc(s["up_in"], 16)
            sp.dma_start(gmask[:, :, :], masks).then_inc(s["gmask_in"], 16)
            sp.dma_start(biasn[:, :, :], bias).then_inc(s["bias_in"], 16)
            sp.dma_start(wmask[:, :, :], consts[:, 2 * P:2 * P + 192].rearrange("p (a w) -> p a w", a=4))\
                .then_inc(s["wmask_in"], 16)
            with sp.Fori(1, NUNIT // RING) as i:
                for r in range(RING):
                    load_unit(RING * i + r, r, RING * i + r - (RING - 1))
            for n in range(NUNIT // RING * RING, NUNIT):
                load_unit(n, n % RING, n - (RING - 1))
            for k in range(KD):
                sp.wait_ge(s["res_done"], k + 1)
                sp.dma_start(out[:, k, :], res[:, k, :]).then_inc(s["stored"], 16)
            sp.wait_ge(s["stored"], 16 * KD)


        @block.gpsimd
        def _(pool):
            pool.memset(one_col[:, :], 1.0).then_inc(s["one_col"], 1)
            pool.wait_ge(s["one_col"], 1)

            def split_unit(n, i, arrived):
                pool.wait_ge(s[f"unit_in{i}"], arrived)
                pool.tensor_tensor(whi[:, i, :], raw[:, i, :], one_col[:, 0:1].broadcast_to([P, BLK * P]),
                                   ALU.mult).then_inc(s["unit_hi"], 1)
                pool.wait_ge(s["unit_hi"], n + 1)
                pool.tensor_tensor(wlo[:, i, :], raw[:, i, :], whi[:, i, :].bitcast(F32), ALU.subtract)\
                    .then_inc(s["unit_split"], 1)

            for n in range(RING):
                split_unit(n, n, 16)
            with pool.Fori(1, NUNIT // RING) as i:
                for r in range(RING):
                    pool.wait_ge(s["unit_used"], RING * i + r - (RING - 1))
                    split_unit(RING * i + r, r, 16 * i + 16)
            for n in range(NUNIT // RING * RING, NUNIT):
                pool.wait_ge(s["unit_used"], n - (RING - 1))
                split_unit(n, n % RING, 16 * (n // RING) + 16)

        @block.tensor
        def _(pe):
            def sums(norm):
                r, W = NORMS[norm]
                nh, hw = norm_halves(W)
                for k in range(KD):
                    pe.wait_ge(s["sq_done"], KD * r + k + 1)
                    for x in range(nh):
                        last = pe.matmul(B4[:, x, 0:hw], ones[:, :], scratch(norm)[0][:, k % 2, x * hw:(x + 1) * hw],
                                         start=(k == 0), stop=(k == KD - 1))
                    last.then_inc(s["sq_used"], 1)

            def split_ready(group, k):
                pe.wait_ge(s["ulo_done"], KD * SPLITS[group] + k + 1)

            def unit_ready(n):
                pe.wait_ge(s["unit_split"], n + 1)

            def tile_free(t, at_least=2):
                pe.wait_ge(s["evac_done"], t - 1)

            def product(dst, slot, blocks, hi, lo, off, W, first=True, last=True, ready=None, halves=None):
                nh, hw = norm_halves(W)
                halves = halves or [(x * hw, hw) for x in range(nh)]
                for i, (b, k) in enumerate(blocks):
                    if ready:
                        ready(k)
                    for j, (w, u) in enumerate(((whi, hi), (whi, lo), (wlo, hi))):
                        for x, (x0, xw) in enumerate(halves):
                            ins = pe.matmul(dst[:, x, 0:xw], w[:, slot, b * P:(b + 1) * P],
                                            u[:, k, off + x0:off + x0 + xw],
                                            start=(first and i == 0 and j == 0),
                                            stop=(last and i == len(blocks) - 1 and j == 2))
                return ins

            def fm_tile(n, t, off=0, W=T, group=None, halves=None):
                unit_ready(n)
                if t >= 2:
                    tile_free(t)
                product(G[:, t % 2], n % RING, [(k, k) for k in range(KD)], uhi, ulo, off, W,
                        ready=(lambda k: split_ready(group, k)) if group else None, halves=halves)\
                    .then_inc(s["unit_used"], 1)

            def tm_tile(n, t, places, cols=P):
                unit_ready(n)
                tile_free(t)
                for dst, tok in places:
                    for k in range(KD):
                        for j, (w, u) in enumerate(((whi, uhi), (whi, ulo), (wlo, uhi))):
                            ins = pe.matmul(dst, tok(u, k), w[:, n % RING, k * P:k * P + cols],
                                            start=(k == 0 and j == 0), stop=(k == KD - 1 and j == 2))
                ins.then_inc(s["unit_used"], 1)

            pe.wait_ge(s["ones_in"], 16)
            sums("mix_pre")
            for name in ("z", "q_gl", "k_gl"):
                for i in range(dict(UNITS)[name]):
                    fm_tile(U0[name] + i, T0[name] + i, group="mix_pre" if name == "z" else None)
            pe.wait_ge(s["up_in"], 16)
            pe.wait_ge(s["evac_done"], T0["z"] + 1)
            def gate_logits(j):
                if j >= 2:
                    pe.wait_ge(s["gate_x"], j - 1)
                for x in range(2):
                    last = pe.matmul(B4[:, 2 * (j % 2) + x, 0:T // 2], upt[:, j * P:(j + 1) * P],
                                     zT[:, x * (T // 2):(x + 1) * (T // 2)], start=True, stop=True)
                last.then_inc(s["gate_ps"], 1)

            gate_logits(0)
            gate_logits(1)

            def natural(t):
                return [(G[:, t % 2, 0, i * P:(i + 1) * P],
                         lambda u, k, i=i: u[:, k, META + i * P:META + (i + 1) * P]) for i in range(4)] \
                    + [(G[0:META, t % 2, 1, 0:P], lambda u, k: u[:, k, 0:META])]

            for i in range(4):
                tm_tile(U0["v_gl"] + i, T0["v_gl"] + i, natural(T0["v_gl"] + i))
                if i < 2:
                    gate_logits(i + 2)
            for name in ("q_na", "k_na", "v_na"):
                for i in range(4):
                    fm_tile(U0[name] + i, T0[name] + i, halves=ROWS4)
            for i in range(4):
                fm_tile(U0["g_gl"] + i, T0["g_gl"] + i)

            pe.wait_ge(s["ident_in"], 16)
            pe.wait_ge(s["evac_done"], T0["v_na"] + 4)
            for i in range(5):
                n, t0 = (P, META + P * i) if i < 4 else (META, 0)
                if i >= 4:
                    pe.wait_ge(s["by_token_done"], i - 3)
                for f in range(4):
                    last = pe.transpose(B4[0:n, i % 4, f * P:(f + 1) * P], vT[:, f, t0:t0 + n], ident[:, :])
                last.then_inc(s["by_token_ps"], 1)

            for j in range(4):
                pe.wait_ge(s["kend_done"], j + 1)
            for i in range(5):
                n, t0 = (P, META + P * i) if i < 4 else (META, 0)
                pe.wait_ge(s["by_token_done"], i + 2)
                for j in range(4):
                    last = pe.transpose(B4[0:n, (i + 5) % 4, j * P:(j + 1) * P], kend[:, j, t0:t0 + n], ident[:, :])
                last.then_inc(s["by_token_ps"], 1)
            pe.wait_ge(s["evac_done"], T0["v_gl"] + 4)
            for i in range(NCHUNK - 1):
                for d, c in ((0, i), (1, NCHUNK - 1 - i)):
                    tile, p0, n, _t = chunk_place(c)
                    bank = 2 * (i % 2) + d
                    if i >= 2:
                        pe.wait_ge(s["state_done"], 4 * (i - 1))
                    else:
                        pe.wait_ge(s["by_token_done"], 10)
                    for hh in range(GLA_H):
                        hp, par = hh // 2, hh % 2
                        last = pe.matmul(B4[par * DK:(par + 1) * DK, bank, hp * DV:(hp + 1) * DV],
                                         kendT[p0:p0 + n, tile, (2 * d + hp) * P + par * DK:(2 * d + hp) * P + (par + 1) * DK],
                                         vgl[p0:p0 + n, tile, hh * DV:(hh + 1) * DV], start=True, stop=True)
                    last.then_inc(s["ds_ps"], 1)
            pe.wait_ge(s["state_done"], 4 * (NCHUNK - 1))
            for i in range(5):
                n, t0 = (P, META + P * i) if i < 4 else (META, 0)
                if i >= 2:
                    pe.wait_ge(s["amat_done"], i - 1)
                for par in range(2):
                    bank = 2 * (i % 2) + par
                    for d in range(2):
                        for hp in range(2):
                            last = pe.matmul(B4[0:n, bank, (2 * d + hp) * P:(2 * d + hp) * P + n],
                                             kinv[par * DK:(par + 1) * DK, 2 * d + hp, t0:t0 + n],
                                             qdec[par * DK:(par + 1) * DK, 2 * d + hp, t0:t0 + n],
                                             start=True, stop=True)
                last.then_inc(s["a_ps"], 1)
                pe.wait_ge(s["amat_done"], i + 1)
                if i >= 2:
                    pe.wait_ge(s["ogl_done"], i - 1)
                if i == 0:
                    pe.wait_ge(s["evac_done"], T0["g_gl"] + 4)
                chunks = (2 * i + 1, 2 * i + 2) if i < 4 else (0,)
                for par in range(2):
                    for hp in range(2):
                        hh = 2 * hp + par
                        pe.matmul(G[:, i % 2, par, hp * P:hp * P + n], vgl[0:n, i, hh * DV:(hh + 1) * DV],
                                  Amat[0:n, i % 2, (2 * par + hp) * P:(2 * par + hp) * P + n],
                                  start=True, stop=False)
                        for x, c in enumerate(chunks):
                            cn, ct = chunk_place(c)[2:]
                            for d in range(2):
                                last = pe.matmul(G[:, i % 2, par, hp * P + x * CHUNK:hp * P + x * CHUNK + cn],
                                                 S[par * DK:(par + 1) * DK, d, c, hp, :],
                                                 qdec[par * DK:(par + 1) * DK, 2 * d + hp, ct:ct + cn],
                                                 start=False, stop=(d == 1 and x == len(chunks) - 1))
                last.then_inc(s["ogl_ps"], 1)
            for hh in range(GLA_H):
                pe.wait_ge(s["gsq_done"], hh + 1)
                if hh == 0:
                    pe.wait_ge(s["ogl_done"], 5)
                if hh >= 2:
                    pe.wait_ge(s["grs_done"], hh - 1)
                for x in range(2):
                    last = pe.matmul(G[:, hh % 2, x, 0:T // 2], ones[:, :], gsq[:, hh % 2, x * (T // 2):(x + 1) * (T // 2)],
                                     start=True, stop=True)
                last.then_inc(s["gss_ps"], 1)

            def na_scores(st):
                a, hp = st // 4, st % 4
                c0, W = na_window(a)
                if st >= 2:
                    pe.wait_ge(s["na_s"], st - 1)
                for par in range(2):
                    bank = 2 * (st % 2) + par
                    q = qna[par * DH:(par + 1) * DH, hp, META + P * a:META + P * (a + 1)]
                    pe.matmul(B4[:, bank, 0:8 * W], q,
                              kna[par * DH:(par + 1) * DH, hp, META + 8 * c0:META + 8 * (c0 + W)],
                              start=True, stop=True)
                    last = pe.matmul(B4[:, bank, 8 * W:8 * W + META], q, kna[par * DH:(par + 1) * DH, hp, 0:META],
                                     start=True, stop=True)
                last.then_inc(s["na_s_ps"], 1)

            def na_transposes(st):
                nb = na_window(st // 4)[1] // 16
                W = 16 * nb
                if st >= 1:
                    pe.wait_ge(s["na_pt0"], st)
                    pe.wait_ge(s["na_pt1"], st)
                for par in range(2):
                    pe.wait_ge(s["na_p"], 2 * st + par + 1)
                    for b in range(nb):
                        pe.transpose(G[:, 0, par, b * P:(b + 1) * P], sc[:, st % 3, par, b * P:(b + 1) * P], ident[:, :])
                    pe.transpose(G[0:META, 0, par, 384:512], sc[:, st % 3, par, 8 * W:8 * W + META], ident[:, :])\
                        .then_inc(s["na_t_ps"], 1)

            def na_values(st):
                a, hp = st // 4, st % 4
                c0, W = na_window(a)
                nb = W // 16
                for par in range(2):
                    hh = 2 * hp + par
                    pe.wait_ge(s["na_pt1" if par else "na_pt0"], st + 1)
                    if st % 4 == 0 and par == 0 and a >= 2:
                        pe.wait_ge(s["na_evac"], a - 1)
                    for b in range(nb):
                        pe.matmul(G[:, 1, a % 2, hh * DH:(hh + 1) * DH], pt[:, st % 2, par, b * P:(b + 1) * P],
                                  vna[:, c0 // 16 + b, hh * DH:(hh + 1) * DH], start=(b == 0), stop=False)
                    pe.matmul(G[:, 1, a % 2, hh * DH:(hh + 1) * DH], pt[0:META, st % 2, par, 384:512],
                              vna[0:META, 4, hh * DH:(hh + 1) * DH], start=False, stop=True)\
                        .then_inc(s["na_o_ps"], 1)

            def na_turn(a, n=P):
                pe.wait_ge(s["na_otok"], a + 1)
                for f in range(4):
                    last = pe.transpose(G[:, 1, a % 2, f * P:f * P + n], otok[0:n, f * P:(f + 1) * P], ident[0:n, 0:n])
                last.then_inc(s["na_turned"], 1)

            pe.wait_ge(s["grs_done"], 4)
            for st in range(21):
                if st < 16:
                    na_scores(st)
                if 1 <= st <= 16:
                    na_transposes(st - 1)
                if 2 <= st <= 17:
                    na_values(st - 2)
                if st >= 8 and st % 4 == 0:
                    na_turn(st // 4 - 2)
            pe.wait_ge(s["na_s"], 16)
            for par in range(2):
                for hp in range(4):
                    last = pe.matmul(B4[0:META, par, hp * META:(hp + 1) * META], qna[par * DH:(par + 1) * DH, hp, 0:META],
                                     kna[par * DH:(par + 1) * DH, hp, 0:META], start=True, stop=True)
            last.then_inc(s["meta_s_ps"], 1)
            pe.wait_ge(s["meta_e"], 1)
            for hh in range(NA_H):
                last = pe.transpose(B4[0:META, 2, hh * META:(hh + 1) * META], sc[0:META, 0, 0, hh * META:(hh + 1) * META],
                                    ident[0:META, 0:META])
            last.then_inc(s["meta_t_ps"], 1)
            pe.wait_ge(s["meta_pt"], 1)
            pe.wait_ge(s["na_evac"], 3)
            for hh in range(NA_H):
                i = 4 * (hh % 2) + hh // 2
                last = pe.matmul(G[0:META, 1, 0, hh * DH:(hh + 1) * DH], pt[0:META, 0, 0, i * META:(i + 1) * META],
                                 vna[0:META, 4, hh * DH:(hh + 1) * DH], start=True, stop=True)
            last.then_inc(s["na_o_ps"], 1)
            na_turn(4, META)

            for i in range(8):
                fm_tile(U0["w_o"] + i, T0["w_o"] + i, FT0, FT, group="mix" if i == 0 else None)
            sums("mix_post")
            sums("ffn_pre")

            def ffn_pair(name, p, x, group=None, W=FT):
                for half in range(2):
                    n = U0[name] + 2 * p + half
                    t = T0[name] + 2 * p + half
                    pe.wait_ge(s["unit_split"], n + 1)
                    pe.wait_ge(s["evac_done"], t - 1)
                    product(G[:, (T0[name] + half) % 2], (U0[name] + 2 * x + half) % RING, [(k, k) for k in range(KD)],
                            uhi, ulo, 0, W,
                            ready=(lambda k: split_ready(group, k)) if group and half == 0 else None)\
                        .then_inc(s["unit_used"], 1)

            def ffn_in(name, group, W):
                for p in range(4):
                    ffn_pair(name, p, p, group if p == 0 else None, W)
                with pe.Fori(0, (JF - 4) // 3) as i:
                    for r in range(3):
                        ffn_pair(name, 3 * i + 4 + r, 4 + r, None, W)

            def ffn_out(name):
                pe.wait_ge(s["ylow_done"], JF * (1 if name == "ffn_out" else 2))
                with pe.Fori(0, KD // 2) as i:
                    for r in range(2):
                        for x in range(3):
                            pe.wait_ge(s["unit_split"], 6 * i + (U0[name] + 3 * r + x + 1))
                            if x == 0:
                                pe.wait_ge(s["evac_done"], 2 * i + (T0[name] + r - 1))
                            ks = range(BLK * x, min(BLK * (x + 1), JF))
                            product(G[:, (T0[name] + r) % 2], (U0[name] + 3 * r + x) % RING,
                                    [(k - BLK * x, k) for k in ks], yhi, ylo, 0, SEQ, first=(x == 0), last=(x == 2))\
                                .then_inc(s["unit_used"], 1)

            ffn_in("ffn_in", "ffn_pre", FT)
            ffn_out("ffn_out")
            sums("ffn_post")
            pe.wait_ge(s["ada_used"], NMOD * KD)
            pe.wait_ge(s["rstd_done"], NORMS["ffn_post"][0] + 1)
            for m in range(NMOD * KD):
                last = pe.matmul(B4[:, 3, m:m + 1], ada_acc[:, m * P:(m + 1) * P], ones[:, 0:1], start=True, stop=True)
            last.then_inc(s["mod_ps"], 1)

            sums("mix2")
            for i in range(8):
                fm_tile(U0["u2"] + i, T0["u2"] + i, 0, SEQ, group="mix2" if i == 0 else None)
            for i in range(4):
                fm_tile(U0["qi2"] + i, T0["qi2"] + i, 0, SEQ)
            fm_tile(U0["ki2"], T0["ki2"], 0, SEQ)

            def blocks(t, cols=P):
                return [(G[:, t % 2, 0, i * P:i * P + cols], lambda u, k, i=i: u[:, k, i * P:(i + 1) * P])
                        for i in range(4)]

            tm_tile(U0["wi2"], T0["wi2"], blocks(T0["wi2"], 8), 8)
            for name in ("q2", "k2"):
                for i in range(4):
                    fm_tile(U0[name] + i, T0[name] + i, 0, SEQ)
            for i in range(4):
                tm_tile(U0["v2"] + i, T0["v2"] + i, blocks(T0["v2"] + i))

            def gate_tile(name, i):
                fm_tile(U0[name] + i, T0[name] + i, 0, SEQ)

            for e in range(24):
                b, j = 1 + e // 8, e % 8
                par = j % 2
                if e == 0:
                    pe.wait_ge(s["evac_done"], T0["wi2"] + 1)
                if e >= 4:
                    pe.wait_ge(s["relu_done"], e - 3)
                pe.matmul(B4[:, e % 4, 0:P * (b + 1)], qi2[par * 64:(par + 1) * 64, j // 2, P * b:P * (b + 1)],
                          ki2[par * 64:(par + 1) * 64, 0:P * (b + 1)], start=True, stop=True)\
                    .then_inc(s["idx_ps"], 1)
                if e % 6 == 5:
                    gate_tile("ga2", e // 6)

            pe.wait_ge(s["relu_done"], 24)
            for j in range(4):
                pe.wait_ge(s["conv31_done"], j + 1)
                last = pe.matmul(B4[:, 0, :], ones[:, :], cacc[:, j, :], start=(j == 0), stop=(j == 3))
            last.then_inc(s["ln_ps"], 1)
            gate_tile("ga2", 4)
            for j in range(4):
                pe.wait_ge(s["lnsq_done"], j + 1)
                last = pe.matmul(B4[:, 1, :], ones[:, :], lnt[:, j % 2, :], start=(j == 0), stop=(j == 3))
                last.then_inc(s["lnsq_used"], 1)
            for i in range(5, 8):
                gate_tile("ga2", i)

            def scores2(q):
                b, hh = q // 8, q % 8
                par = hh % 2
                if q >= 2:
                    pe.wait_ge(s["s2_read"], q - 1)
                elif q == 0:
                    pe.wait_ge(s["ln_read"], 1)
                    pe.wait_ge(s["lnv_read"], 1)
                pe.matmul(B4[:, q % 2, 0:P * (b + 1)], q2[par * 64:(par + 1) * 64, hh // 2, P * b:P * (b + 1)],
                          k2[par * 64:(par + 1) * 64, hh // 2, 0:P * (b + 1)], start=True, stop=True)\
                    .then_inc(s["s2_ps"], 1)

            def transposes2(q):
                b = q // 8
                pe.wait_ge(s["p2_done"], q + 1)
                if q >= 2:
                    pe.wait_ge(s["pt2_done"], q - 1)
                for c in range(b + 1):
                    last = pe.transpose(G[:, q % 2, 1, c * P:(c + 1) * P], S2[:, q % 3, c * P:(c + 1) * P], ident[:, :])
                last.then_inc(s["t2_ps"], 1)

            def values2(q):
                b, hh = q // 8, q % 8
                pe.wait_ge(s["pt2_done"], q + 1)
                if hh == 0 and b >= 2:
                    pe.wait_ge(s["al_done"], 4 * (b - 1))
                for c in range(b + 1):
                    last = pe.matmul(B4[:, 2 + b % 2, hh * 64:(hh + 1) * 64], pt2[:, q % 2, c * P:(c + 1) * P],
                                     v2[:, c, hh * 64:(hh + 1) * 64], start=(c == 0), stop=(c == b))
                last.then_inc(s["o2_ps"], 1)

            def turn2(b):
                pe.wait_ge(s["otok2_done"], b + 1)
                for f in range(4):
                    last = pe.transpose(B4[:, 2 + b % 2, f * P:(f + 1) * P], otok2[:, f * P:(f + 1) * P], ident[:, :])
                last.then_inc(s["turned2"], 1)

            for q in range(37):
                if q < 32:
                    scores2(q)
                    if q % 4 == 1:
                        gate_tile("gb2", q // 4)
                if 1 <= q <= 32:
                    transposes2(q - 1)
                if 2 <= q <= 33:
                    values2(q - 2)
                if q >= 12 and q % 8 == 4:
                    turn2(q // 8 - 1)

            for i in range(8):
                n, hi, lo = U0["proj2"] + i, (ah, ch)[i % 2], (al, cl)[i % 2]
                unit_ready(n)
                if i == 0:
                    pe.wait_ge(s["al_done"], 16)
                    pe.wait_ge(s["evac_done"], T0["proj2"])
                if i == 1:
                    pe.wait_ge(s["cl_done"], 4)
                for ct in range(2):
                    t = T0["proj2"] + 2 * i + ct
                    pe.wait_ge(s["evac_done"], t - 3)
                    last = product(G[:, t % 2, (t // 2) % 2:(t // 2) % 2 + 1], n % RING, [(4 * ct + k, k) for k in range(4)],
                                   hi, lo, 0, SEQ)
                last.then_inc(s["unit_used"], 1)
            for i in range(8):
                n, t = U0["out2"] + i, T0["out2"] + i
                unit_ready(n)
                tile_free(t)
                if i < 2:
                    pe.wait_ge(s["evac_done"], T0["out2"])
                product(G[:, t % 2], n % RING, [(k, k) for k in range(KD)], mh, ml, 0, SEQ,
                        ready=(lambda k: pe.wait_ge(s["ml_done"], k + 1)) if i == 0 else None)\
                    .then_inc(s["unit_used"], 1)
            sums("ffn2")
            ffn_in("ffn_in2", "ffn2", SEQ)
            ffn_out("ffn_out2")
            sums("final")

        @block.scalar
        def _(act):
            def squares(norm, src, ready):
                r, W = NORMS[norm]
                for k in range(KD):
                    ready(k)
                    if k >= 2:
                        act.wait_ge(s["sq_used"], KD * r + k - 1)
                    act.activation(scratch(norm)[0][:, k % 2, 0:W], src(k), ACT.Square).then_inc(s["sq_done"], 1)

            def root(norm):
                r, W = NORMS[norm]
                nh, hw = norm_halves(W)
                rstd = scratch(norm)[2]
                act.wait_ge(s["sq_used"], KD * (r + 1))
                act.activation(rstd[:, 0:W].rearrange("p (x w) -> p x w", x=nh), B4[:, 0:nh, 0:hw], ACT.Ln,
                               bias=v("eps"), scale=1.0 / D).then_inc(s["ln_done"], 1)
                act.wait_ge(s["ln_done"], r + 1)
                act.activation(rstd[:, 0:W], rstd[:, 0:W], ACT.Exp, scale=-0.5).then_inc(s["rstd_done"], 1)

            def high(group, norm, off, shift=None):
                W = NORMS[norm][1]
                for k in range(KD):
                    act.wait_ge(s["u_done"], KD * {"mix_pre": 0, "ffn_pre": 1, "mix2": 2, "ffn2": 3}[norm] + k + 1)
                    if shift is None:
                        ins = act.activation(uhi[:, k, off:off + W], scratch(norm)[1][:, k % 2, 0:W], ACT.Copy)
                    else:
                        ins = act.activation(uhi[:, k, off:off + W], scratch(norm)[1][:, k % 2, 0:W], ACT.Identity,
                                             bias=shift(k))
                    ins.then_inc(s["uhi_done"], 1)

            def tile_ready(n):
                act.wait_ge(s["unit_used"], n + 1)

            def evac(name, i, dst, func=ACT.Copy, rows=P, W=T, **kw):
                n, t = U0[name] + i, T0[name] + i
                nh, hw = norm_halves(W)
                tile_ready(n)
                act.activation(dst.rearrange("p (x w) -> p x w", x=nh), G[0:rows, t % 2, 0:nh, 0:hw], func, **kw)\
                    .then_inc(s["evac_done"], 1)

            def h_here(k):
                act.wait_ge(s[f"h_in{k % 2}"], 16 * (k // 2) + 16)
            act.wait_ge(s["vec_in"], 16)
            act.activation(csilu, v("c", 0, 8), ACT.Silu).then_inc(s["csilu"], 1)
            squares("mix_pre", lambda k: h[:, k, :], h_here)
            root("mix_pre")
            high("mix_pre", "mix_pre", 0)
            evac("z", 0, zT[:, :], rows=32)
            for i in range(2):
                evac("q_gl", i, qgl[:, i, :])
            for i in range(2):
                evac("k_gl", i, kgl[:, i, :])

            def gate(j):
                b = j % 2
                act.wait_ge(s["gate_x"], j + 1)
                act.activation(te[:, b, :], tx[:, b, :], ACT.Abs).then_inc(s["act_step"], 1)
                act.wait_ge(s["act_step"], 2 * j + 1)
                act.activation(te[:, b, :], te[:, b, :], ACT.Exp, scale=-1.0).then_inc(s["act_step"], 1)
                act.wait_ge(s["act_step"], 2 * j + 2)
                act.activation(te[:, b, :], te[:, b, :], ACT.Ln, bias=1.0).then_inc(s["gate_ln"], 1)
                act.wait_ge(s["gate_b"], 2 * j + 1)
                act.activation(te[:, b, :], kend[:, j, :], ACT.Exp, scale=1.0 / 16).then_inc(s["gate_eb"], 1)
                ends = (META - 1, META + CHUNK - 1) if j < 2 else (0, META)
                act.activation(dec[:, j, 0:1], kend[:, j, ends[0]:ends[0] + 1], ACT.Exp, scale=1.0 / 16)
                act.activation(dec[:, j, 1:NCHUNK], kend[:, j, ends[1]:ends[1] + CHUNK * (NCHUNK - 2) + 1:CHUNK], ACT.Exp,
                               scale=1.0 / 16)
                act.wait_ge(s["gate_used"], 2 * j + 1)
                act.activation(te[:, b, :], kend[:, j, :], ACT.Exp, scale=-1.0 / 16).then_inc(s["gate_eb"], 1)
                act.wait_ge(s["gate_b"], 2 * j + 2)
                act.activation(tx[:, b, :], tx[:, b, :], ACT.Exp, scale=1.0 / 16).then_inc(s["gate_ed"], 1)

            def evac_tokens(name, i, dst):
                t = T0[name] + i
                tile_ready(U0[name] + i)
                act.activation(dst[:, 0:4, i * P:(i + 1) * P],
                               G[:, t % 2, 0, :].rearrange("p (a n) -> p a n", a=4), ACT.Copy)
                act.activation(dst[0:META, 4, i * P:(i + 1) * P], G[0:META, t % 2, 1, 0:P], ACT.Copy)\
                    .then_inc(s["evac_done"], 1)

            for i in range(4):
                gate(i)
                evac_tokens("v_gl", i, vgl)
            def evac_columns(name, i, dst):
                t = T0[name] + i
                tile_ready(U0[name] + i)
                to = dst[:, META:T].rearrange("p (c r) -> p r c", r=GRID_R)
                act.activation(dst[:, 0:META], G[:, t % 2, 0, 0:META], ACT.Copy)
                act.activation(to[:, 0:4, :], G[:, t % 2, 0, META:META + 256].rearrange("p (r c) -> p r c", r=4), ACT.Copy)
                act.activation(to[:, 4:8, :], G[:, t % 2, 1, 0:256].rearrange("p (r c) -> p r c", r=4), ACT.Copy)\
                    .then_inc(s["evac_done"], 1)

            for i in range(4):
                evac_columns("q_na", i, qna[:, i, :])
            for i in range(4):
                evac_columns("k_na", i, kna[:, i, :])
            act.wait_ge(s["kend_done"], 4)
            for i in range(4):
                evac_columns("v_na", i, vT[:, i, :])
            for i in range(4):
                evac("g_gl", i, sg[:, i, :], ACT.Silu)

            for i in range(5):
                n = P if i < 4 else META
                act.wait_ge(s["by_token_ps"], i + 1)
                act.activation(vna[0:n, i, :], B4[0:n, i % 4, :], ACT.Copy).then_inc(s["by_token_done"], 1)

            for i in range(5):
                n = P if i < 4 else META
                act.wait_ge(s["by_token_ps"], i + 6)
                if i == 0:
                    act.wait_ge(s["unit_used"], U0["g_gl"] + 4)
                act.activation(kendT[0:n, i, :], B4[0:n, (i + 5) % 4, :], ACT.Copy).then_inc(s["by_token_done"], 1)
            for i in range(5):
                n, t0 = (P, META + P * i) if i < 4 else (META, 0)
                act.wait_ge(s["ogl_ps"], i + 1)
                for par in range(2):
                    ins = act.activation(oT[:, par:4:2, t0:t0 + n],
                                         G[:, i % 2, par, 0:2 * P].rearrange("p (a n) -> p a n", a=2)[:, :, 0:n], ACT.Copy)
                ins.then_inc(s["ogl_done"], 1)
            act.wait_ge(s["ogl_done"], 5)
            for hh in range(GLA_H + 1):
                if hh < GLA_H:
                    if hh >= 2:
                        act.wait_ge(s["gss_ps"], hh - 1)
                    act.activation(gsq[:, hh % 2, :], oT[:, hh, :], ACT.Square).then_inc(s["gsq_done"], 1)
                if hh >= 1:
                    g = hh - 1
                    act.wait_ge(s["gss_ps"], g + 1)
                    if g >= 2:
                        act.wait_ge(s["ogl_out"], g - 1)
                    act.activation(grs[:, g % 2, :].rearrange("p (x w) -> p x w", x=2), G[:, g % 2, :, 0:T // 2], ACT.Ln,
                                   bias=v("eps"), scale=1.0 / DV).then_inc(s["gln_done"], 1)
                    act.wait_ge(s["gln_done"], g + 1)
                    act.activation(grs[:, g % 2, :], grs[:, g % 2, :], ACT.Exp, scale=-0.5).then_inc(s["grs_done"], 1)

            def na_exp(st):
                a = st // 4
                W = na_window(a)[1]
                act.wait_ge(s["na_nmx"], st + 1)
                if st % 4 == 0 and a >= 2:
                    act.wait_ge(s["na_rinv"], a - 1)
                for par in range(2):
                    hh = 2 * (st % 4) + par
                    act.activation(sc[:, st % 3, par, 0:8 * W + META], sc[:, st % 3, par, 0:8 * W + META], ACT.Exp,
                                   bias=nmx[:, 2 * (st % 3) + par:2 * (st % 3) + par + 1],
                                   accum_out=row_sum[:, a % 2, hh:hh + 1]).then_inc(s["na_p"], 1)

            def na_turned(a, n=P):
                act.wait_ge(s["na_turned"], a + 1)
                for f in range(4):
                    if a < 4:
                        dst = onaT[:, f, META:T].rearrange("p (r c) -> p c r", r=GRID_R)[:, 16 * a:16 * a + 16, :]
                        src = G[:, 1, a % 2, f * P:(f + 1) * P].rearrange("p (c r) -> p c r", r=GRID_R)
                    else:
                        dst, src = onaT[:, f, 0:META], G[:, 1, 0, f * P:f * P + n]
                    ins = act.activation(dst, src, ACT.Copy, scale=v("na_gain", f))
                ins.then_inc(s["na_evac"], 1)

            def na_root(a, n=P):
                act.wait_ge(s["na_o_scaled"], a + 1)
                act.activation(osq[0:n], otok[0:n], ACT.Square, accum_out=ssn[0:n]).then_inc(s["na_ss"], 1)
                act.wait_ge(s["na_ss"], a + 1)
                act.activation(rstdn[0:n], ssn[0:n], ACT.Ln, bias=vec[0:n, VCOL["eps"]:VCOL["eps"] + 1],
                               scale=1.0 / 512).then_inc(s["na_ln"], 1)
                act.wait_ge(s["na_ln"], a + 1)
                act.activation(rstdn[0:n], rstdn[0:n], ACT.Exp, scale=-0.5).then_inc(s["na_rstd"], 1)

            def na_pt_evac(st):
                nb = na_window(st // 4)[1] // 16
                act.wait_ge(s["na_t_ps"], 2 * st + 1)
                if st >= 2:
                    act.wait_ge(s["na_o_ps"], 2 * st - 3)
                act.activation(pt[:, st % 2, 0, 0:nb * P], G[:, 0, 0, 0:nb * P], ACT.Copy)
                act.activation(pt[0:META, st % 2, 0, 384:512], G[0:META, 0, 0, 384:512], ACT.Copy).then_inc(s["na_pt0"], 1)

            for st in range(21):
                if 1 <= st <= 16:
                    na_pt_evac(st - 1)
                if st < 16:
                    na_exp(st)
                if 6 <= st <= 18 and st % 4 == 2:
                    na_root(st // 4 - 1)
                if st >= 8 and st % 4 == 0:
                    na_turned(st // 4 - 2)
            act.wait_ge(s["meta_s"], 1)
            act.activation(sc[0:META, 0, 0, 0:P], sc[0:META, 0, 0, 0:P], ACT.Exp).then_inc(s["meta_e"], 1)
            act.wait_ge(s["meta_t_ps"], 1)
            act.activation(pt[0:META, 0, 0, 0:P], B4[0:META, 2, 0:P], ACT.Copy).then_inc(s["meta_pt"], 1)
            na_root(4, META)
            na_turned(4, META)
            for k in range(KD):
                if k < 4:
                    src = onaT[:, k, :]
                else:
                    act.wait_ge(s["ogl_out"], k - 3)
                    src = oT[:, k - 4, :]
                if k == 0:
                    act.wait_ge(s["na_evac"], 5)
                act.activation(uhi[:, k, :], src, ACT.Copy).then_inc(s["uhi_done"], 1)
            for i in range(8):
                n, t = U0["w_o"] + i, T0["w_o"] + i
                evac("w_o", i, m1[:, i, :], W=FT)
            squares("mix_post", lambda k: m1[:, k, :], lambda k: act.wait_ge(s["evac_done"], T0["w_o"] + k + 1))
            root("mix_post")
            squares("ffn_pre", lambda k: h[:, k, FT0:T], lambda k: act.wait_ge(s["h_done"], k + 1))
            root("ffn_pre")
            high("ffn_pre", "ffn_pre", 0)

            def ffn_evac(name, p, x, half, dst, func=ACT.Copy, W=FT):
                act.wait_ge(s["unit_used"], U0[name] + 2 * p + (half + 1))
                nh, hw = norm_halves(W)
                act.activation(dst.rearrange("p (x w) -> p x w", x=nh), G[:, (T0[name] + half) % 2, 0:nh, 0:hw], func)\
                    .then_inc(s["evac_done"], 1)

            def ffn_act(p, x, early):
                if not early:
                    act.wait_ge(s["conv_done"], 2 * p - 5)
                ffn_evac("ffn_in", p, x, 0, av[:, x, 0:FT])
                if not early:
                    act.wait_ge(s["conv_done"], 2 * p - 4)
                ffn_evac("ffn_in", p, x, 1, ag[:, x, 0:FT])
                act.wait_ge(s["conv_done"], 2 * p + 2)
                act.activation(tg[:, x, :], tg[:, x, :], ACT.Gelu_apprx_tanh).then_inc(s["gelu_done"], 1)
                ffn_high(p, x, 0)

            def ffn_high(p, x, before):
                act.wait_ge(s["yf_done"], p + (before + 1))
                act.wait_ge(s["yf_done"], 1)
                act.activation(yhi[:, bass.ds(p, 1), :].rearrange("p a n -> p (a n)"), yf[:, x, :], ACT.Copy)\
                    .then_inc(s["yhi_done"], 1)

            for p in range(4):
                ffn_act(p, p % 3, p < 3)
            with act.Fori(0, (JF - 4) // 3) as i:
                for r in range(3):
                    ffn_act(3 * i + 4 + r, (4 + r) % 3, False)
            for c in range(KD):
                t = T0["ffn_out"] + c
                for m in range(NMOD * c, NMOD * (c + 1)):
                    if m >= ADA_RING:
                        act.wait_ge(s["ada_used"], m - ADA_RING + 1)
                    act.dma_start(ada_in[:, m % ADA_RING, :], ada[m, :, :]).then_inc(s[f"ada_in{m % ADA_RING}"], 16)
                act.wait_ge(s["unit_used"], U0["ffn_out"] + 3 * c + 3)
                act.activation(m2[:, c, :], G[:, t % 2, 0, :], ACT.Copy).then_inc(s["evac_done"], 1)
            squares("ffn_post", lambda k: m2[:, k, :], lambda k: act.wait_ge(s["evac_done"], T0["ffn_out"] + k + 1))
            root("ffn_post")
            act.wait_ge(s["mod_ps"], 1)
            act.activation(mod, B4[:, 3, 0:NMOD * KD], ACT.Copy).then_inc(s["mod_done"], 1)

            squares("mix2", lambda k: h[:, k, META:T], lambda k: act.wait_ge(s["h_done"], KD + k + 1))
            act.dma_start(dtab[:, :], consts[:, 576:576 + 896]).then_inc(s["dtab_in"], 16)
            act.dma_start(caus[:, :], consts[:, 448:576]).then_inc(s["caus_in"], 16)
            root("mix2")
            act.wait_ge(s["modv_done"], 1)
            high("mix2", "mix2", 0, lambda k: mod[:, k:k + 1])
            for j in range(4):
                evac("u2", 2 * j, z2[:, j, CONV_W - 1:CONV_W - 1 + SEQ], W=SEQ)
                if j >= 2:
                    act.wait_ge(s["z_done"], j - 1)
                evac("u2", 2 * j + 1, sgm[:, j % 2, :], ACT.Sigmoid, W=SEQ)
            for i in range(4):
                evac("qi2", i, qi2[:, i, :], W=SEQ)
            evac("ki2", 0, ki2[:, :], W=SEQ)
            t = T0["wi2"]
            tile_ready(U0["wi2"])
            act.activation(wi2[:, :, :], G[:, t % 2, 0, :].rearrange("p (a n) -> p a n", a=4)[:, :, 0:8], ACT.Copy,
                           scale=8 ** -0.5).then_inc(s["evac_done"], 1)
            for i in range(4):
                evac("q2", i, q2[:, i, :], W=SEQ)
            for i in range(4):
                evac("k2", i, k2[:, i, :], W=SEQ)
            for i in range(4):
                t = T0["v2"] + i
                tile_ready(U0["v2"] + i)
                act.activation(v2[:, :, i * P:(i + 1) * P], G[:, t % 2, 0, :].rearrange("p (a n) -> p a n", a=4), ACT.Copy)\
                    .then_inc(s["evac_done"], 1)
            def gate_evac(i):
                evac("ga2", i, sga[:, i, :], W=SEQ)

            act.wait_ge(s["z_done"], 4)
            for e in range(24):
                b = 1 + e // 8
                act.wait_ge(s["idx_ps"], e + 1)
                if e >= 2:
                    act.wait_ge(s["idx_acc"], e - 1)
                act.activation(sgm[:, e % 2, 0:P * (b + 1)], B4[:, e % 4, 0:P * (b + 1)], ACT.Relu, scale=64 ** -0.5)\
                    .then_inc(s["relu_done"], 1)
                if e % 6 == 5:
                    gate_evac(e // 6)
            for j in range(4):
                act.wait_ge(s["lnc_done"], j + 1)
                if j >= 2:
                    act.wait_ge(s["lnsq_used"], j - 1)
                act.activation(lnt[:, j % 2, :], cacc[:, j, :], ACT.Square).then_inc(s["lnsq_done"], 1)
            gate_evac(4)
            act.wait_ge(s["lnsq_used"], 4)
            act.activation(lnr[:, :], B4[:, 1, :], ACT.Ln, bias=v("eps"), scale=1.0 / CONV_CH).then_inc(s["lnv_read"], 1)
            act.wait_ge(s["lnv_read"], 1)
            act.activation(lnr[:, :], lnr[:, :], ACT.Exp, scale=-0.5).then_inc(s["lnr_done"], 1)
            for j in range(4):
                act.wait_ge(s["lnx_done"], j + 1)
                if j >= 2:
                    act.wait_ge(s["cl_done"], j - 1)
                act.activation(lnt[:, j % 2, :], cacc[:, j, :], ACT.Silu, bias=v("ln_b", j)).then_inc(s["silu_done"], 1)
                act.wait_ge(s["silu_done"], j + 1)
                act.activation(ch[:, j, :], lnt[:, j % 2, :], ACT.Copy).then_inc(s["ch_done"], 1)
            for i in range(5, 8):
                gate_evac(i)
            act.wait_ge(s["evac_done"], T0["ga2"] + 8)
            act.activation(sga[:, :, :], sga[:, :, :], ACT.Sigmoid).then_inc(s["sga_done"], 1)

            def exp2(q):
                b, hh = q // 8, q % 8
                act.wait_ge(s["nmx2"], q + 1)
                if hh == 0 and b >= 2:
                    act.wait_ge(s["rinv2"], b - 1)
                act.activation(S2[:, q % 3, 0:P * (b + 1)], S2[:, q % 3, 0:P * (b + 1)], ACT.Exp,
                               bias=nmx[:, q % 3:q % 3 + 1], accum_out=row_sum[:, b % 2, hh:hh + 1]).then_inc(s["p2_done"], 1)

            def pt2_evac(q):
                b = q // 8
                act.wait_ge(s["t2_ps"], q + 1)
                if q >= 2:
                    act.wait_ge(s["o2_ps"], q - 1)
                act.activation(pt2[:, q % 2, 0:P * (b + 1)], G[:, q % 2, 1, 0:P * (b + 1)], ACT.Copy)\
                    .then_inc(s["pt2_done"], 1)

            for q in range(37):
                if q < 32 and q % 4 == 1:
                    i = q // 4
                    if i == 4:
                        act.wait_ge(s["cl_done"], 4)
                    evac("gb2", i, sgb[i // 4][:, i % 4, :], W=SEQ)
                if 1 <= q <= 32:
                    pt2_evac(q - 1)
                if q < 32:
                    exp2(q)
                if q >= 12 and q % 8 == 4:
                    b = q // 8 - 1
                    act.wait_ge(s["turned2"], b + 1)
                    for f in range(4):
                        act.activation(ah[:, f, P * b:P * (b + 1)], B4[:, 2 + b % 2, f * P:(f + 1) * P], ACT.Copy)\
                            .then_inc(s["ah_done"], 1)
            act.wait_ge(s["evac_done"], T0["gb2"] + 8)
            for half in sgb:
                act.activation(half[:, :, :], half[:, :, :], ACT.Sigmoid).then_inc(s["sgb_done"], 1)
            for i in range(4):
                for br in range(2):
                    tile_ready(U0["proj2"] + 2 * i + br)
                    if i >= 1:
                        act.wait_ge(s["ml_done"], 2 * i)
                    for ct in range(2):
                        t = T0["proj2"] + 4 * i + 2 * br + ct
                        act.activation(yab[:, 2 * br + ct, :], G[:, t % 2, (t // 2) % 2, :], ACT.Copy)\
                            .then_inc(s["evac_done"], 1)
                for ct in range(2):
                    c = 2 * i + ct
                    act.wait_ge(s["mrg_done"], c + 1)
                    act.activation(mh[:, c, :], yab[:, ct, :], ACT.Copy).then_inc(s["mh_done"], 1)

            def residual_tiles(name, per, scale, before, rt):
                for c in range(KD):
                    t = T0[name] + c
                    act.wait_ge(s["unit_used"], U0[name] + per * (c + 1))
                    if c >= 2:
                        act.wait_ge(s["h_done"], before + c - 1)
                    act.activation(rt[:, c % 2, :], G[:, t % 2, 0, :], ACT.Copy, scale=scale(c)).then_inc(s["evac_done"], 1)

            residual_tiles("out2", 1, lambda c: mod[:, 16 + c:17 + c], 2 * KD, rt)
            squares("ffn2", lambda k: h[:, k, META:T], lambda k: act.wait_ge(s["h_done"], 2 * KD + k + 1))
            root("ffn2")
            high("ffn2", "ffn2", 0, lambda k: mod[:, 24 + k:25 + k])

            def ffn2_act(p, x, early):
                if not early:
                    act.wait_ge(s["yf_done"], p + (JF - 2))
                ffn_evac("ffn_in2", p, x, 0, tv[:, x, :], ACT.Silu, W=SEQ)
                ffn_evac("ffn_in2", p, x, 1, tg[:, x, :], W=SEQ)
                ffn_high(p, x, JF)

            for p in range(4):
                ffn2_act(p, p % 3, p < 3)
            with act.Fori(0, (JF - 4) // 3) as i:
                for r in range(3):
                    ffn2_act(3 * i + 4 + r, (4 + r) % 3, False)
            residual_tiles("ffn_out2", 3, lambda c: mod[:, 40 + c:41 + c], 3 * KD, tv)
            squares("final", lambda k: h[:, k, META:T], lambda k: act.wait_ge(s["h_done"], 3 * KD + k + 1))
            root("final")

        @block.vector
        def _(dve):
            step = [0]

            def link(ins):
                step[0] += 1
                ins.then_inc(s["dve_step"], 1)
                dve.wait_ge(s["dve_step"], step[0])

            def normalise(norm, group, off, hoff, gain, shift=None):
                r, W = NORMS[norm]
                base = KD * SPLITS[group]
                ub, rstd = scratch(norm)[1], scratch(norm)[2]
                dve.wait_ge(s["rstd_done"], r + 1)
                for k in range(KD + 1):
                    if k < KD:
                        if k >= 2:
                            dve.wait_ge(s["ulo_done"], base + k - 1)
                        dve.scalar_tensor_tensor(ub[:, k % 2, 0:W], h[:, k, hoff:hoff + W], gain(k), rstd[:, 0:W],
                                                 ALU.mult, ALU.mult).then_inc(s["u_done"], 1)
                    if k >= 1:
                        q = k - 1
                        dve.wait_ge(s["uhi_done"], base + q + 1)
                        if shift is None:
                            ins = dve.tensor_tensor(ulo[:, q, off:off + W], ub[:, q % 2, 0:W],
                                                    uhi[:, q, off:off + W].bitcast(F32), ALU.subtract)
                        else:
                            ins = dve.scalar_tensor_tensor(ulo[:, q, off:off + W], ub[:, q % 2, 0:W], shift(q),
                                                           uhi[:, q, off:off + W].bitcast(F32), ALU.add, ALU.subtract)
                        ins.then_inc(s["ulo_done"], 1)
                dve.wait_ge(s["ulo_done"], base + KD)

            def add_normed(norm, m, gain, hoff, count):
                r, W = NORMS[norm]
                ub, rstd = scratch(norm)[1], scratch(norm)[2]
                dve.wait_ge(s["rstd_done"], r + 1)
                for k in range(KD):
                    link(dve.scalar_tensor_tensor(ub[:, k % 2, 0:W], m[:, k, 0:W], gain(k), rstd[:, 0:W],
                                                  ALU.mult, ALU.mult))
                    dve.tensor_tensor(h[:, k, hoff:hoff + W], h[:, k, hoff:hoff + W], ub[:, k % 2, 0:W], ALU.add)\
                       .then_inc(s["h_done"], 1)

            normalise("mix_pre", "mix_pre", 0, 0, lambda k: v("mix_pre", k))

            dve.wait_ge(s["gla_in"], 16)
            for j in range(4):
                b, hp, fwd = j % 2, j % 2, j < 2
                dve.wait_ge(s["gate_ps"], j + 1)
                dve.tensor_scalar(tx[:, b, :].rearrange("p (x w) -> p x w", x=2), B4[:, 2 * b:2 * b + 2, 0:T // 2],
                                  v("gate_bias", j), None, ALU.add).then_inc(s["gate_x"], 1)
                dve.wait_ge(s["gate_ln"], j + 1)
                link(dve.scalar_tensor_tensor(tx[:, b, :], tx[:, b, :], 0.0, te[:, b, :], ALU.min, ALU.subtract))
                flip = slice(None) if fwd else slice(None, None, -1)
                dve.tensor_tensor_scan(kend[:, j, flip], scan_keep[:, j // 2, flip], tx[:, b, flip], 0.0,
                                       ALU.mult, ALU.add).then_inc(s["gate_b"], 1)
                if j == 0:
                    dve.wait_ge(s["evac_done"], T0["k_gl"] + 2)
                dve.wait_ge(s["gate_eb"], 2 * j + 1)
                dve.scalar_tensor_tensor(qdec[:, j, :], qgl[:, hp, :], DK ** -0.5, te[:, b, :], ALU.mult, ALU.mult)\
                   .then_inc(s["gate_used"], 1)
                dve.wait_ge(s["gate_b"], 2 * j + 1)
                e0, e1 = (META - 1, CHUNK - 1) if fwd else (0, 0)
                body = kend[:, j, META:T].rearrange("p (c n) -> p c n", n=CHUNK)
                dve.tensor_tensor(tx[:, b, META:T].rearrange("p (c n) -> p c n", n=CHUNK),
                                  body[:, :, e1:e1 + 1].broadcast_to([P, NCHUNK - 1, CHUNK]), body, ALU.subtract)
                dve.tensor_tensor(tx[:, b, 0:META], kend[:, j, e0:e0 + 1].broadcast_to([P, META]), kend[:, j, 0:META],
                                  ALU.subtract).then_inc(s["gate_b"], 1)
                dve.wait_ge(s["gate_eb"], 2 * j + 2)
                dve.tensor_tensor(kinv[:, j, :], kgl[:, hp, :], te[:, b, :], ALU.mult).then_inc(s["gate_used"], 1)
                dve.wait_ge(s["gate_ed"], j + 1)
                dve.tensor_tensor(kend[:, j, :], kgl[:, hp, :], tx[:, b, :], ALU.mult).then_inc(s["kend_done"], 1)

            dve.wait_ge(s["unit_used"], U0["g_gl"] + 4)
            dve.memset(S[:, 0, 0, :, :], 0.0)
            link(dve.memset(S[:, 1, NCHUNK - 1, :, :], 0.0))
            for i in range(NCHUNK - 1):
                for d, c in ((0, i), (1, NCHUNK - 1 - i)):
                    to = c + 1 if d == 0 else c - 1
                    dve.wait_ge(s["ds_ps"], 2 * i + d + 1)
                    if i >= 1:
                        dve.wait_ge(s["state_done"], 4 * i)
                    for hp in range(2):
                        dve.scalar_tensor_tensor(S[:, d, to, hp, :], S[:, d, c, hp, :], dec[:, 2 * d + hp, c:c + 1],
                                                 B4[:, 2 * (i % 2) + d, hp * DV:(hp + 1) * DV], ALU.mult, ALU.add)\
                           .then_inc(s["state_done"], 1)
            dve.wait_ge(s["gmask_in"], 16)
            link(dve.memset(Amat[:, :, :], 0.0))
            for i in range(5):
                n = P if i < 4 else META
                dve.wait_ge(s["a_ps"], i + 1)
                if i >= 2:
                    dve.wait_ge(s["ogl_ps"], i - 1)
                for par in range(2):
                    for d in range(2):
                        if d == 1:
                            link(last)
                        last = dve.copy_predicated(
                            Amat[0:n, i % 2, 256 * par:256 * par + 256].rearrange("p (a c) -> p a c", a=2)[:, :, 0:n],
                            gmask[0:n, d, 0:n].unsqueeze(1).broadcast_to([n, 2, n]),
                            B4[0:n, 2 * (i % 2) + par, 256 * d:256 * d + 256].rearrange("p (a c) -> p a c", a=2)[:, :, 0:n])
                last.then_inc(s["amat_done"], 1)
            dve.wait_ge(s["evac_done"], T0["g_gl"] + 4)
            for hh in range(GLA_H):
                dve.wait_ge(s["grs_done"], hh + 1)
                link(dve.scalar_tensor_tensor(oT[:, hh, :], oT[:, hh, :], v("gla_gain"), grs[:, hh % 2, :],
                                              ALU.mult, ALU.mult))
                dve.tensor_tensor(oT[:, hh, :], oT[:, hh, :], sg[:, hh, :], ALU.mult).then_inc(s["ogl_out"], 1)

            dve.wait_ge(s["bias_in"], 16)
            dve.wait_ge(s["wmask_in"], 16)

            def na_soft(st):
                a, hp = st // 4, st % 4
                c0, W = na_window(a)
                w0 = c0 - 16 * (a - 1)
                b = st % 3
                bank = 2 * (st % 2)
                dve.wait_ge(s["na_s_ps"], st + 1)
                if st >= 3:
                    dve.wait_ge(s["na_t_ps"], 2 * (st - 2))
                dve.scalar_tensor_tensor(sc[:, b, :, 0:8 * W], B4[:, bank:bank + 2, 0:8 * W], DH ** -0.5,
                                         biasn[:, 2 * hp:2 * hp + 2, 8 * w0:8 * (w0 + W)], ALU.mult, ALU.add)
                dve.tensor_scalar(sc[:, b, :, 8 * W:8 * W + META], B4[:, bank:bank + 2, 8 * W:8 * W + META],
                                  DH ** -0.5, None, ALU.mult).then_inc(s["na_s"], 1)
                dve.wait_ge(s["na_s"], st + 1)
                for par in range(2):
                    x = sc[:, b, par, 0:8 * W].rearrange("p (w r) -> p w r", r=8)
                    last = dve.tensor_tensor(x, x, wmask[:, a, 0:W].unsqueeze(2).broadcast_to([P, W, 8]), ALU.add)
                link(last)
                link(dve.tensor_reduce(mx[:, 0:2], sc[:, b, :, 0:8 * W + META], AX.X, ALU.max))
                dve.tensor_scalar(nmx[:, 2 * b:2 * b + 2], mx[:, 0:2], -1.0, None, ALU.mult).then_inc(s["na_nmx"], 1)

            def na_pt_copy(st):
                nb = na_window(st // 4)[1] // 16
                dve.wait_ge(s["na_t_ps"], 2 * st + 2)
                if st >= 2:
                    dve.wait_ge(s["na_o_ps"], 2 * st - 2)
                dve.tensor_copy(pt[:, st % 2, 1, 0:nb * P], G[:, 0, 1, 0:nb * P])
                dve.tensor_copy(pt[0:META, st % 2, 1, 384:512], G[0:META, 0, 1, 384:512]).then_inc(s["na_pt1"], 1)

            def na_divide(a, n=P):
                if a < 4:
                    dve.wait_ge(s["na_p"], 8 * (a + 1))
                dve.reciprocal(rinv[0:n], row_sum[0:n, a % 2, :]).then_inc(s["na_rinv"], 1)
                dve.wait_ge(s["na_rinv"], a + 1)
                dve.wait_ge(s["na_o_ps"], 8 * (a + 1) if a < 4 else 33)
                if a >= 1:
                    dve.wait_ge(s["na_turned"], a)
                dve.tensor_tensor(otok[0:n].rearrange("p (h e) -> p h e", h=NA_H),
                                  G[0:n, 1, a % 2, :].rearrange("p (h e) -> p h e", h=NA_H),
                                  rinv[0:n].unsqueeze(2).broadcast_to([n, NA_H, DH]), ALU.mult)\
                   .then_inc(s["na_o_scaled"], 1)

            def na_norm(a, n=P):
                dve.wait_ge(s["na_rstd"], a + 1)
                dve.tensor_scalar(otok[0:n], otok[0:n], rstdn[0:n], None, ALU.mult).then_inc(s["na_otok"], 1)

            for st in range(20):
                if st < 16:
                    na_soft(st)
                if 1 <= st <= 16:
                    na_pt_copy(st - 1)
                if 6 <= st <= 18 and st % 4 == 2:
                    na_divide(st // 4 - 1)
                if st >= 7 and st % 4 == 3:
                    na_norm(st // 4 - 1)
            dve.wait_ge(s["meta_s_ps"], 1)
            dve.wait_ge(s["na_t_ps"], 32)
            ms = sc[0:META, 0, 0, 0:P].rearrange("p (h k) -> p h k", h=NA_H)
            link(dve.tensor_scalar(sc[0:META, 0, 0, 0:P].rearrange("p (a n) -> p a n", a=2), B4[0:META, 0:2, 0:64],
                                   DH ** -0.5, None, ALU.mult))
            link(dve.tensor_reduce(mx[0:META], ms, AX.X, ALU.max))
            dve.tensor_tensor(ms, ms, mx[0:META].unsqueeze(2).broadcast_to([META, NA_H, META]), ALU.subtract)\
               .then_inc(s["meta_s"], 1)
            dve.wait_ge(s["meta_e"], 1)
            link(dve.tensor_reduce(row_sum[0:META, 0, :].rearrange("p (b a) -> p a b", a=2), ms.rearrange("p (a b) k -> p a b k", a=2),
                                   AX.X, ALU.add))
            na_divide(4, META)
            na_norm(4, META)

            for k in range(KD):
                dve.wait_ge(s["uhi_done"], KD * SPLITS["mix"] + k + 1)
                src = onaT[:, k, :] if k < 4 else oT[:, k - 4, :]
                dve.tensor_tensor(ulo[:, k, :], src, uhi[:, k, :].bitcast(F32), ALU.subtract).then_inc(s["ulo_done"], 1)
            add_normed("mix_post", m1, lambda k: v("mix_post", k), FT0, 0)
            normalise("ffn_pre", "ffn_pre", 0, FT0, lambda k: v("ffn_pre", k))

            dve.memset(av[:, :, FT:FT + 1], 0.0)
            link(dve.memset(ag[:, :, FT:FT + 1], 0.0))

            def conv3(p, x, half, early):
                src, dst = ((av, tv), (ag, tg))[half]
                w = lambda k: vec[:, bass.ds(VCOL["cw"] + 44 * k + half + 2 * p, 1)]
                taps = [src[:, x, META - FT0 - 1 + k:META - FT0 - 1 + k + SEQ] for k in range(3)]
                dve.wait_ge(s["evac_done"], 2 * p + (T0["ffn_in"] + half + 1))
                if not early:
                    dve.wait_ge(s["ylow_done"], p - 2)
                dve.tensor_scalar(dst[:, x, :], taps[0], w(0), vec[:, bass.ds(VCOL["cb"] + half + 2 * p, 1)],
                                  ALU.mult, ALU.add).then_inc(s["conv_step"], 1)
                dve.wait_ge(s["conv_step"], 4 * p + (2 * half + 1))
                dve.scalar_tensor_tensor(dst[:, x, :], taps[1], w(1), dst[:, x, :], ALU.mult, ALU.add)\
                   .then_inc(s["conv_step"], 1)
                dve.wait_ge(s["conv_step"], 4 * p + (2 * half + 2))
                dve.scalar_tensor_tensor(dst[:, x, :], taps[2], w(2), dst[:, x, :], ALU.mult, ALU.add)\
                   .then_inc(s["conv_done"], 1)

            def gated(p, x, before):
                dve.tensor_tensor(yf[:, x, :], tv[:, x, :], tg[:, x, :], ALU.mult).then_inc(s["yf_done"], 1)
                dve.wait_ge(s["yhi_done"], p + (before + 1))
                dve.tensor_tensor(ylo[:, bass.ds(p, 1), :].rearrange("p a n -> p (a n)"), yf[:, x, :],
                                  yhi[:, bass.ds(p, 1), :].rearrange("p a n -> p (a n)").bitcast(F32), ALU.subtract)\
                   .then_inc(s["ylow_done"], 1)

            def ffn_dve(p, x, early):
                conv3(p, x, 0, early)
                conv3(p, x, 1, early)
                dve.wait_ge(s["gelu_done"], p + 1)
                gated(p, x, 0)

            for p in range(4):
                ffn_dve(p, p % 3, p < 3)
            with dve.Fori(0, (JF - 4) // 3) as i:
                for r in range(3):
                    ffn_dve(3 * i + 4 + r, (4 + r) % 3, False)
            dve.wait_ge(s["ylow_done"], JF)
            dve.wait_ge(s["csilu"], 1)
            for m in range(NMOD * KD):
                k, part = m // NMOD, m % NMOD
                acc = ada_acc[:, 1024 * part:1024 * (part + 1)]
                dve.wait_ge(s[f"ada_in{m % ADA_RING}"], 16 * (m // ADA_RING) + 16)
                if k == 0:
                    ins = dve.tensor_scalar(acc, ada_in[:, m % ADA_RING, :], csilu[:, k:k + 1], None, ALU.mult)
                else:
                    dve.wait_ge(s["ada_used"], m - NMOD + 1)
                    ins = dve.scalar_tensor_tensor(acc, ada_in[:, m % ADA_RING, :], csilu[:, k:k + 1], acc,
                                                   ALU.mult, ALU.add)
                ins.then_inc(s["ada_used"], 1)
            add_normed("ffn_post", m2, lambda k: v("ffn_post", k), META, KD)

            dve.wait_ge(s["mod_done"], 1)
            link(dve.tensor_tensor(mod, mod, v("b_ada", 0, 48), ALU.add))
            dve.scalar_tensor_tensor(gm2, mod[:, 8:16], 1.0, v("mix2", 0, 8), ALU.add, ALU.mult)
            dve.scalar_tensor_tensor(gf2, mod[:, 32:40], 1.0, v("ffn2", 0, 8), ALU.add, ALU.mult).then_inc(s["modv_done"], 1)
            dve.wait_ge(s["modv_done"], 1)
            normalise("mix2", "mix2", 0, META, lambda k: gm2[:, k:k + 1], lambda k: mod[:, k:k + 1])
            link(dve.memset(z2[:, :, 0:CONV_W - 1], 0.0))
            for j in range(4):
                dve.wait_ge(s["evac_done"], T0["u2"] + 2 * j + 2)
                x = z2[:, j, CONV_W - 1:CONV_W - 1 + SEQ]
                dve.tensor_tensor(x, x, sgm[:, j % 2, :], ALU.mult).then_inc(s["z_done"], 1)
            dve.wait_ge(s["z_done"], 4)
            for j in range(4):
                dve.tensor_scalar(cacc[:, j, :], z2[:, j, 0:SEQ], v("w_dw", j), v("b_dw", j), ALU.mult, ALU.add)\
                   .then_inc(s["tap_done"], 1)
            with dve.Fori(1, CONV_W - 1) as k:
                for j in range(4):
                    dve.wait_ge(s["tap_done"], 4 * k + (j - 3))
                    dve.scalar_tensor_tensor(cacc[:, j, :], z2[:, j, bass.ds(k, SEQ)],
                                             vec[:, bass.ds(VCOL["w_dw"] + j + 4 * k, 1)], cacc[:, j, :],
                                             ALU.mult, ALU.add).then_inc(s["tap_done"], 1)
            for j in range(4):
                k = CONV_W - 1
                dve.wait_ge(s["tap_done"], 4 * k + (j - 3))
                dve.scalar_tensor_tensor(cacc[:, j, :], z2[:, j, k:k + SEQ], v("w_dw", 4 * k + j), cacc[:, j, :],
                                         ALU.mult, ALU.add).then_inc(s["conv31_done"], 1)

            def scx(b):
                first = (0, 0, 256, 640)[b]
                return scb[:, first:first + P * (b + 1)]

            dve.wait_ge(s["evac_done"], T0["wi2"] + 1)
            e = 0
            for b in range(1, 4):
                for j in range(8):
                    dve.wait_ge(s["relu_done"], e + 1)
                    r = sgm[:, e % 2, 0:P * (b + 1)]
                    w = wi2[:, b, j:j + 1]
                    if j == 0:
                        ins = dve.tensor_scalar(scx(b), r, w, None, ALU.mult)
                    else:
                        ins = dve.scalar_tensor_tensor(scx(b), r, w, scx(b), ALU.mult, ALU.add)
                    ins.then_inc(s["idx_acc"], 1)
                    e += 1
                    dve.wait_ge(s["idx_acc"], e)
            dve.wait_ge(s["ln_ps"], 1)
            for j in range(4):
                dve.scalar_tensor_tensor(cacc[:, j, :], B4[:, 0, :], -1.0 / CONV_CH, cacc[:, j, :], ALU.mult, ALU.add)\
                   .then_inc(s["lnc_done"], 1)
            dve.wait_ge(s["lnc_done"], 4)
            dve.memset(mx[:, 0:1], 0.0).then_inc(s["ln_read"], 1)
            dve.wait_ge(s["lnr_done"], 1)
            for j in range(4):
                dve.scalar_tensor_tensor(cacc[:, j, :], cacc[:, j, :], v("ln_g", j), lnr[:, :], ALU.mult, ALU.mult)\
                   .then_inc(s["lnx_done"], 1)
            for j in range(4):
                dve.wait_ge(s["ch_done"], j + 1)
                dve.tensor_tensor(cl[:, j, :], lnt[:, j % 2, :], ch[:, j, :].bitcast(F32), ALU.subtract)\
                   .then_inc(s["cl_done"], 1)

            dve.wait_ge(s["caus_in"], 16)
            dve.wait_ge(s["dtab_in"], 16)

            def select(b, part):
                x = scx(b)
                if part == 0:
                    diag = x[:, P * b:P * (b + 1)]
                    link(dve.tensor_tensor(diag, diag, caus[:, :], ALU.add))
                for _ in range(TOPK // 64):
                    link(dve.max(top8, x))
                    link(dve.match_replace(x, top8, x, TAKEN))
                if part == 7:
                    link(dve.tensor_scalar(x, x, TAKEN / 2, -1e30, ALU.is_gt, ALU.mult))

            def soft2(q):
                b, hh = q // 8, q % 8
                W = P * (b + 1)
                dve.wait_ge(s["s2_ps"], q + 1)
                if q >= 3:
                    dve.wait_ge(s["t2_ps"], q - 2)
                x = S2[:, q % 3, 0:W]
                link(dve.scalar_tensor_tensor(x, dtab[:, 384 - P * b:384 - P * b + W], 2.0 ** -(hh + 1),
                                              scx(b) if b else caus[:, :], ALU.mult, ALU.add))
                dve.scalar_tensor_tensor(x, B4[:, q % 2, 0:W], 64 ** -0.5, x, ALU.mult, ALU.add).then_inc(s["s2_read"], 1)
                dve.wait_ge(s["s2_read"], q + 1)
                link(dve.tensor_reduce(mx[:, 0:1], x, AX.X, ALU.max))
                dve.tensor_scalar(nmx[:, q % 3:q % 3 + 1], mx[:, 0:1], -1.0, None, ALU.mult).then_inc(s["nmx2"], 1)
                dve.wait_ge(s["nmx2"], q + 1)

            for q in range(37):
                if q < 32:
                    soft2(q)
                    if q < 24:
                        select(q // 8 + 1, q % 8)
                if q >= 10 and q % 8 == 2:
                    b = q // 8 - 1
                    dve.wait_ge(s["p2_done"], 8 * b + 8)
                    dve.reciprocal(rinv, row_sum[:, b % 2, :]).then_inc(s["rinv2"], 1)
                    dve.wait_ge(s["rinv2"], b + 1)
                    dve.wait_ge(s["o2_ps"], 8 * b + 8)
                    dve.tensor_tensor(otok2[:, :].rearrange("p (h e) -> p h e", h=8),
                                      B4[:, 2 + b % 2, :].rearrange("p (h e) -> p h e", h=8),
                                      rinv.unsqueeze(2).broadcast_to([P, 8, 64]), ALU.mult).then_inc(s["otok2_done"], 1)
                if q >= 12 and q % 8 == 4:
                    b = q // 8 - 1
                    dve.wait_ge(s["ah_done"], 4 * b + 4)
                    for f in range(4):
                        dve.tensor_tensor(al[:, f, P * b:P * (b + 1)], B4[:, 2 + b % 2, f * P:(f + 1) * P],
                                          ah[:, f, P * b:P * (b + 1)].bitcast(F32), ALU.subtract).then_inc(s["al_done"], 1)

            dve.wait_ge(s["sga_done"], 1)
            for i in range(4):
                dve.wait_ge(s["evac_done"], T0["proj2"] + 4 * (i + 1))
                dve.wait_ge(s["sgb_done"], i // 2 + 1)
                for ct in range(2):
                    c = 2 * i + ct
                    dve.tensor_tensor(yab[:, ct, :], yab[:, ct, :], sga[:, c, :], ALU.mult)
                    link(dve.tensor_tensor(yab[:, 2 + ct, :], yab[:, 2 + ct, :], sgb[c // 4][:, c % 4, :], ALU.mult))
                    dve.tensor_tensor(yab[:, ct, :], yab[:, ct, :], yab[:, 2 + ct, :], ALU.add).then_inc(s["mrg_done"], 1)
                for ct in range(2):
                    c = 2 * i + ct
                    dve.wait_ge(s["mh_done"], c + 1)
                    dve.tensor_tensor(ml[:, c, :], yab[:, ct, :], mh[:, c, :].bitcast(F32), ALU.subtract)\
                       .then_inc(s["ml_done"], 1)

            def add_residual(name, rt):
                for c in range(KD):
                    dve.wait_ge(s["evac_done"], T0[name] + c + 1)
                    dve.tensor_tensor(h[:, c, META:T], h[:, c, META:T], rt[:, c % 2, :], ALU.add).then_inc(s["h_done"], 1)

            add_residual("out2", rt)
            normalise("ffn2", "ffn2", 0, META, lambda k: gf2[:, k:k + 1], lambda k: mod[:, 24 + k:25 + k])

            def ffn2_dve(p, x):
                dve.wait_ge(s["evac_done"], 2 * p + (T0["ffn_in2"] + 2))
                gated(p, x, JF)

            for p in range(4):
                ffn2_dve(p, p % 3)
            with dve.Fori(0, (JF - 4) // 3) as i:
                for r in range(3):
                    ffn2_dve(3 * i + 4 + r, (4 + r) % 3)
            add_residual("ffn_out2", tv)
            dve.wait_ge(s["rstd_done"], 7)
            for k in range(KD):
                dve.scalar_tensor_tensor(res[:, k, :], h[:, k, META:T], v("final", k), rstd2[:, 0:SEQ], ALU.mult, ALU.mult)\
                   .then_inc(s["res_done"], 1)


def _columns(w, cols):
    cols = list(cols)
    units = []
    for i in range(0, len(cols), P):
        c = cols[i:i + P]
        u = np.zeros((P, KD, P), np.float32)
        u[:, :, :len(c)] = w[:, c].reshape(KD, P, len(c)).transpose(1, 0, 2)
        units.append(u.reshape(P, KD * P))
    return units


def _deep(w):
    units = []
    for c in range(KD):
        b = np.zeros((24, P, P), np.float32)
        b[:JF] = w[:, c * P:(c + 1) * P].reshape(JF, P, P)
        units += list(b.reshape(3, BLK, P, P).transpose(0, 2, 1, 3).reshape(3, P, BLK * P))
    return units


def _shallow(w, i):
    return w[:, 256 * i:256 * (i + 1)].reshape(4, P, 2, P).transpose(1, 2, 0, 3).reshape(P, BLK * P)


def layout(x):
    f = {k: np.asarray(a) for k, a in x.items()}
    w1, w2 = f["w_in"][0], f["w_in_2"][0]
    o = np.cumsum([0, 512, 512, 512, 256, 256, 512, 512, 32])
    r = lambda a, n=None: range(o[a], o[a + 1])
    stream = _columns(w1, r(7)) + _columns(w1, r(3)) + _columns(w1, r(4)) + _columns(w1, r(5))
    stream += _columns(w1, r(0)) + _columns(w1, r(1)) + _columns(w1, r(2)) + _columns(w1, r(6))
    stream += _columns(f["w_o"][0], range(D))
    ffn = [c for j in range(JF) for half in (0, DFF) for c in range(half + P * j, half + P * (j + 1))]
    stream += _columns(f["w_ffn_in"][0], ffn) + _deep(f["w_ffn_out"][0])
    q2, k2, v2, qi, ki, wi, u2, ga, gb = np.cumsum([0, 512, 512, 512, 512, 64, 8, 1024, 1024])
    span = lambda a, n: range(a, a + n)
    stream += _columns(w2, [c for j in range(4) for half in (0, CONV_CH) for c in span(u2 + half + P * j, P)])
    stream += _columns(w2, span(qi, 512)) + _columns(w2, list(span(ki, 64)) * 2) + _columns(w2, span(wi, 8))
    stream += _columns(w2, span(q2, 512)) + _columns(w2, span(k2, 512)) + _columns(w2, span(v2, 512))
    stream += _columns(w2, span(ga, 1024)) + _columns(w2, span(gb, 1024))
    for i in range(4):
        stream += [_shallow(f["w_attn_proj_2"][0], i), _shallow(f["w_conv_proj_2"][0], i)]
    stream += _columns(f["w_out_2"][0], range(D))
    stream += _columns(f["w_ffn_in_2"][0], ffn) + _deep(f["w_ffn_out_2"][0])
    stream = np.stack(stream[:NUNIT])

    h = np.concatenate([f["meta_tokens"], f["x"][0]], axis=0)
    h = np.ascontiguousarray(h.T.reshape(KD, P, T).transpose(1, 0, 2))
    col = lambda a: np.asarray(a).reshape(-1, P).T
    vecs = {"mix_pre": f["norm_mix_pre"], "na_gain": f["na_out_gain"],
            "gate_bias": np.concatenate([f["gla_gate_bias_fwd"], f["gla_gate_bias_bwd"]], 1),
            "gla_gain": f["gla_out_gain"], "mix_post": f["norm_mix_post"], "ffn_pre": f["norm_ffn_pre"],
            "cw": f["ffn_conv_w"], "cb": f["ffn_conv_b"], "ffn_post": f["norm_ffn_post"],
            "mix2": f["norm_mix_g_2"], "w_dw": f["w_dw_2"], "b_dw": f["b_dw_2"], "ln_g": f["conv_ln_g_2"],
            "ln_b": f["conv_ln_b_2"], "ffn2": f["norm_ffn_g_2"], "b_ada": f["b_ada_2"],
            "final": f["norm_final_g_2"], "c": f["c_2"], "eps": np.full((1, P), EPS, np.float32)}
    pairs = lambda a: np.asarray(a).reshape(-1, 2, JF, P).transpose(0, 2, 1, 3)
    vecs["cw"], vecs["cb"] = pairs(vecs["cw"]), pairs(vecs["cb"])
    vecs = np.ascontiguousarray(np.concatenate([col(vecs[n]) for n, _ in VECS], 1))
    assert vecs.shape[1] == NVEC

    p = np.arange(P)
    ident = np.eye(P, dtype=np.float32)
    onesm = np.ones((P, P), np.float32)
    wmask = np.zeros((P, 4, 48), np.float32)
    for a in range(4):
        lo, W = na_window(a)
        c, key = 16 * a + p // 8, lo + np.arange(W)
        first = np.clip(c - 8, 0, GRID_W - 16)
        seen = (key[None] >= first[:, None]) & (key[None] < first[:, None] + 16)
        wmask[:, a, :W] = np.where(seen, 0.0, -1e30)
    causal = np.where(p[None] <= p[:, None], 0.0, -1e30).astype(np.float32)
    dist = (np.arange(896)[None] - 384 - p[:, None]).astype(np.float32)
    consts = np.ascontiguousarray(np.concatenate([ident, onesm, wmask.reshape(P, -1), causal, dist], 1))
    same = (p[:, None] // CHUNK) == (p[None] // CHUNK)
    masks = np.stack([same & (p[:, None] <= p[None]), same & (p[:, None] > p[None])], 1).astype(np.int32)
    keep = np.ones((P, 2, T), np.float32)
    keep[:, 0, META::CHUNK] = 0.0
    keep[:, 1, META - 1::CHUNK] = 0.0

    rpb = np.zeros((NA_H, 15, 64), np.float32)
    rpb[:, :, 16:47] = f["na_rel_bias"][0]
    bias = np.zeros((P, NA_H, 48, 8), np.float32)
    for q in range(P):
        bias[q] = rpb[:, 7 - q % 8:15 - q % 8, 15 - q // 8:63 - q // 8].transpose(0, 2, 1)
    bias = bias.reshape(P, NA_H, 384)
    up = np.zeros((32, 512), np.float32)
    up[:RANK, :256] = f["gla_gate_up_fwd"][0]
    up[RANK:, 256:] = f["gla_gate_up_bwd"][0]
    ada = np.ascontiguousarray(f["w_ada_2"][0].reshape(KD, P, NMOD, D).transpose(0, 2, 1, 3).reshape(-1, P, D))
    return {"wstream": stream, "ada": ada, "hT": h, "vecs": vecs, "consts": consts, "masks": masks,
            "scanm": keep, "bias": bias, "up": up}


def kernel(**inputs):
    import concourse.bacc as bacc
    from concourse.bass_utils import run_bass_kernel_spmd

    arrays = layout(inputs)
    nc = bacc.Bacc("TRN2", target_bir_lowering=False, num_devices=1)
    aps = {n: nc.dram_tensor(n, a.shape, mybir.dt.from_np(a.dtype), kind="ExternalInput").ap()
           for n, a in arrays.items()}
    out = nc.dram_tensor("out", (P, KD, SEQ), F32, kind="ExternalOutput").ap()
    build(nc, out=out, **aps)
    result = run_bass_kernel_spmd(nc, [arrays], core_ids=[0]).results[0]["out"]
    return np.ascontiguousarray(np.asarray(result).transpose(2, 1, 0).reshape(1, SEQ, D))
```

```python
import numpy as np
import concourse.bass as bass
from concourse import mybir
from contextlib import ExitStack

F32 = mybir.dt.float32
F32R = mybir.dt.float32r
I32 = mybir.dt.int32
ALU = mybir.AluOpType
ACT = mybir.ActivationFunctionType
AX = mybir.AxisListType

P = 128
D = 1024
KD = D // P
SEQ = 512
META = 16
T = META + SEQ
EPS = 1e-6
GRID_W, GRID_R = 64, 8
NA_H, DH = 8, 64
GLA_H, DK, DV, CHUNK = 4, 64, 128, 64
NCHUNK = SEQ // CHUNK + 1
RANK = 16
DFF = 2816
JF = DFF // P
CONVF = 3
CONV_CH, CONV_W = 512, 31
NMOD = 6
FT0 = 12
FT = T - FT0
TOPK = 128
TAKEN = -3e38
RING = 3
BLK = 8
ADA_RING = 4

VECS = [("mix_pre", 8), ("na_gain", 4), ("gate_bias", 4), ("gla_gain", 1), ("mix_post", 8),
        ("ffn_pre", 8), ("cw", 44 * CONVF), ("cb", 44), ("ffn_post", 8),
        ("mix2", 8), ("w_dw", 4 * CONV_W), ("b_dw", 4), ("ln_g", 4), ("ln_b", 4), ("ffn2", 8),
        ("b_ada", 48), ("final", 8), ("c", 8), ("eps", 1)]
VCOL = {}
_at = 0
for _n, _w in VECS:
    VCOL[_n] = _at
    _at += _w
NVEC = _at

UNITS = [("z", 1), ("q_gl", 2), ("k_gl", 2), ("v_gl", 4), ("q_na", 4), ("k_na", 4), ("v_na", 4),
         ("g_gl", 4), ("w_o", 8), ("ffn_in", 2 * JF), ("ffn_out", 24),
         ("u2", 8), ("qi2", 4), ("ki2", 1), ("wi2", 1), ("q2", 4), ("k2", 4), ("v2", 4),
         ("ga2", 8), ("gb2", 8), ("proj2", 8), ("out2", 8), ("ffn_in2", 2 * JF), ("ffn_out2", 24)]
U0 = {}
_at = 0
for _n, _w in UNITS:
    U0[_n] = _at
    _at += _w
NUNIT = _at

T0 = {}
_at = 0
for _n, _w in UNITS:
    T0[_n] = _at
    _at += {"ffn_out": 8, "ffn_out2": 8, "proj2": 16}.get(_n, _w)


def na_window(a):
    lo, hi = max(0, 16 * (a - 1)), min(GRID_W, 16 * (a + 2))
    return lo, hi - lo


def chunk_place(c):
    if c == 0:
        return 4, 0, META, 0
    return (c - 1) // 2, CHUNK * ((c - 1) % 2), CHUNK, META + CHUNK * (c - 1)


def build(nc, wstream, ada, hT, vecs, consts, masks, scanm, bias, up, out):
    ctx = ExitStack()
    with ctx:

        def sb(name, shape, at, dt=F32):
            return nc.alloc_sbuf_tensor_at(name, shape, dt, offset=at)

        class Signals(dict):
            def __missing__(self, name):
                self[name] = ctx.enter_context(nc.semaphore(name))
                return self[name]

        s = Signals()

        at = 16512
        h = sb("h", [P, KD, T], at); at += KD * T * 4
        U_AT = at
        uhi = sb("uhi", [P, KD, T], at, F32R); at += KD * T * 4
        ulo = sb("ulo", [P, KD, T], at, F32R); at += KD * T * 4
        raw = sb("raw", [P, RING, BLK * P], at); at += RING * BLK * P * 4
        whi = sb("whi", [P, RING, BLK * P], at, F32R); at += RING * BLK * P * 4
        wlo = sb("wlo", [P, RING, BLK * P], at, F32R); at += RING * BLK * P * 4
        vec = sb("vec", [P, NVEC], at); at += -(-4 * NVEC // 64) * 64
        ident = sb("ident", [P, P], at); at += 512
        ones = sb("ones", [P, P], at); at += 512
        one_col = sb("one_col", [P, 1], at); at += 64
        small = sb("small", [P, 160], at); at += 640
        A0 = -(-at // 64) * 64

        def arena(offset):
            return A0 + offset

        def v(name, k=0, n=1):
            return vec[:, VCOL[name] + k:VCOL[name] + k + n]

        csilu = small[:, 0:8]
        mod = small[:, 8:56]
        gm2 = small[:, 56:64]
        gf2 = small[:, 64:72]
        mx = small[:, 72:80]
        nmx = small[:, 80:88]
        rs = small[:, 88:96]
        rinv = small[:, 96:104]
        na_ssum = small[:, 104:106]
        na_rstd = small[:, 106:108]
        top8 = small[:, 112:120]
        row_sum = small[:, 120:136].rearrange("p (b h) -> p b h", b=2)

        o = 0
        qna = sb("qna", [P, 4, T], arena(o)); o += 8448
        kna = sb("kna", [P, 4, T], arena(o)); o += 8448
        vna = sb("vna", [P, 5, 512], arena(o)); o += 10240
        vglT = sb("vglT", [P, 4, T], arena(o - 10240))
        vgl = sb("vgl", [P, 5, 512], arena(o)); o += 10240
        sg = sb("sg", [P, 4, T], arena(o)); o += 8448
        biasn = sb("biasn", [P, NA_H, 48 * 8], arena(o)); o += 12288
        KEND = o
        kend = sb("kend", [P, 4, T], arena(o)); o += 8448
        QDEC = o
        qdec = sb("qdec", [P, 4, T], arena(o)); o += 8448
        KINV = o
        kinv = sb("kinv", [P, 4, T], arena(o)); o += 8448
        QGL = o
        qgl = sb("qgl", [P, 2, T], arena(o)); o += 4224
        kgl = sb("kgl", [P, 2, T], arena(o)); o += 4224
        TX = o
        tx = sb("tx", [P, 2, T], arena(o)); o += 4224
        TE = o
        te = sb("te", [P, 2, T], arena(o)); o += 4224
        scan_keep = sb("scan_keep", [P, 2, T], arena(o)); o += 4224
        zT = sb("zT", [32, T], arena(o)); o += 2112
        upt = sb("upt", [32, 512], arena(o)); o += 2048
        dec = sb("dec", [P, 4, NCHUNK], arena(o)); o += 192
        gmask = sb("gmask", [P, 2, P], arena(o), I32); o += 1024
        wmask = sb("wmask", [P, 4, 48], arena(o)); o += 768
        sq1 = sb("sq1", [P, 2, T], arena(KEND))
        ub1 = sb("ub1", [P, 2, T], arena(KEND + 4224))
        rstd1 = sb("rstd1", [P, T], arena(QDEC))
        kendT = sb("kendT", [P, 5, 512], U_AT)
        S = sb("S", [P, 2, NCHUNK, 2, DV], U_AT + 10240)
        Amat = sb("Amat", [P, 2, 512], U_AT + 28672)
        oT = sb("oT", [P, 4, T], arena(KEND))
        onaT = sb("onaT", [P, 4, T], arena(QDEC))
        gsq = sb("gsq", [P, GLA_H, T], U_AT)
        grs = sb("grs", [P, GLA_H, T], arena(KINV))
        sc = sb("sc", [P, 3, 2, 400], arena(QGL))
        vT = sb("vT", [P, 4, T], arena(TX))
        pt = sb("pt", [P, 2, 2, 512], arena(QGL + 9600))
        otok = sb("otok", [P, 2, 512], arena(QGL + 17792))
        osq = sb("osq", [P, 512], arena(QGL + 21888))
        yhi = sb("yhi", [P, JF, SEQ], arena(0), F32R)
        ylo = sb("ylo", [P, JF, SEQ], arena(45056), F32R)
        FB = 90112
        av = sb("av", [P, 3, FT + 4], arena(FB))
        ag = sb("ag", [P, 3, FT + 4], arena(FB + 6240))
        tv = sb("tv", [P, 3, SEQ], arena(FB + 12480))
        tg = sb("tg", [P, 3, SEQ], arena(FB + 18624))
        yf = sb("yf", [P, 3, SEQ], arena(FB + 24768))
        m1 = sb("m1", [P, KD, FT], arena(0))
        sq2 = sb("sq2", [P, 2, T], arena(FB))
        ub2 = sb("ub2", [P, 2, T], arena(FB + 4224))
        rstd2 = sb("rstd2", [P, T], arena(FB + 8448))
        m2 = sb("m2", [P, KD, SEQ], U_AT)
        ada_in = sb("ada_in", [P, ADA_RING, 1024], U_AT + 16384)
        ada_acc = sb("ada_acc", [P, NMOD * 1024], arena(FB))
        sq3 = sb("sq3", [P, 2, SEQ], arena(FB + 24768))
        rstd3 = sb("rstd3", [P, SEQ], arena(FB + 28864))
        ub3 = sb("ub3", [P, 2, SEQ], arena(0))

        z2 = sb("z2", [P, 4, CONV_W - 1 + SEQ], arena(0))
        ch = sb("ch", [P, 4, SEQ], arena(0), F32R)
        cacc = sb("cacc", [P, 4, SEQ], arena(8704))
        cl = sb("cl", [P, 4, SEQ], arena(8704), F32R)
        sgm = sb("sgm", [P, 2, SEQ], arena(16896))
        rt = sb("rt", [P, 2, SEQ], arena(16896))
        q2 = sb("q2_", [P, 4, SEQ], arena(20992))
        k2 = sb("k2_", [P, 4, SEQ], arena(29184))
        qi2 = sb("qi2_", [P, 4, SEQ], arena(37376))
        ki2 = sb("ki2_", [P, SEQ], arena(45568))
        v2 = sb("v2_", [P, 4, 512], arena(47616))
        mh = sb("mh", [P, KD, SEQ], arena(20992), F32R)
        ml = sb("ml", [P, KD, SEQ], arena(72320), F32R)
        yab = sb("yab", [P, 4, SEQ], arena(47616))
        wi2 = sb("wi2_", [P, 4, 8], arena(55808))
        sga = sb("sga", [P, KD, SEQ], arena(55936))
        sgb = [sb("sgb0", [P, 4, SEQ], arena(37376)), sb("sgb1", [P, 4, SEQ], arena(109696))]
        scb = sb("scb", [P, 1152], arena(72320))
        S2 = sb("S2", [P, 3, SEQ], arena(76928))
        pt2 = sb("pt2", [P, 2, SEQ], arena(83072))
        otok2 = sb("otok2", [P, 512], arena(87168))
        sq4 = sb("sq4", [P, 2, T], arena(76928))
        ub4 = sb("ub4", [P, 2, T], arena(81152))
        rstd4 = sb("rstd4", [P, T], arena(85376))
        dtab = sb("dtab", [P, 896], arena(89216))
        caus = sb("caus", [P, P], arena(92800))
        ah = sb("ah", [P, 4, SEQ], arena(93312), F32R)
        al = sb("al", [P, 4, SEQ], arena(101504), F32R)
        v2T = sb("v2T", [P, 4, SEQ], arena(93312))
        wi2T = sb("wi2T", [8, SEQ], arena(101504))
        lnt = sb("lnt", [P, 2, SEQ], arena(109696))
        lnr = sb("lnr", [P, SEQ], arena(113792))
        res = sb("res", [P, KD, SEQ], U_AT)

        G = ctx.enter_context(nc.psum_tensor("G", [P, 2, 2, 512], F32))
        B4 = ctx.enter_context(nc.psum_tensor("B4", [P, 4, 512], F32))

        def norm_halves(W):
            return (1, W) if W <= 512 else (2, W // 2)

        ROWS4 = [(0, META + SEQ // 2), (META + SEQ // 2, SEQ // 2)]

        NORMS = {"mix_pre": (0, T), "mix_post": (1, FT), "ffn_pre": (2, FT), "ffn_post": (3, SEQ),
                 "mix2": (4, SEQ), "ffn2": (5, SEQ), "final": (6, SEQ)}
        ADDED = ("mix_post", "ffn_post", "ffn2", "final")
        SPLITS = {"mix_pre": 0, "mix": 1, "ffn_pre": 2, "mix2": 3, "ffn2": 4}

        GLA_FIRST = (4, 5, 6, 7, 0, 1, 2, 3)

        def unadded(norm):
            return sum(1 for n, (r, _w) in NORMS.items() if n not in ADDED and r < NORMS[norm][0])

        def scratch(norm):
            return {"mix_pre": (sq1, ub1, rstd1), "ffn_post": (sq3, ub3, rstd3),
                    "mix2": (sq4, ub4, rstd4)}.get(norm, (sq2, ub2, rstd2))

        block = ctx.enter_context(nc.Block())

        @block.sync
        def _(sp):
            for k in range(KD):
                sp.dma_start(h[:, k, :], hT[:, k, :]).then_inc(s[f"h_in{k % 2}"], 16)
            sp.dma_start(vec[:, :], vecs).then_inc(s["vec_in"], 16)
            sp.dma_start(ones[:, :], consts[:, P:2 * P]).then_inc(s["ones_in"], 16)

            def load_unit(n, i, wait):
                if wait is not None:
                    sp.wait_ge(s["unit_split"], wait)
                sp.dma_start(raw[:, i, :], wstream[bass.ds(n, 1), :, :].rearrange("a p n -> p (a n)"))\
                    .then_inc(s[f"unit_in{i}"], 16)

            for n in range(RING):
                load_unit(n, n, None)
            sp.dma_start(ident[:, :], consts[:, 0:P]).then_inc(s["ident_in"], 16)
            sp.dma_start(scan_keep[:, :, :], scanm).then_inc(s["gla_in"], 16)
            sp.dma_start(upt[:, :], up).then_inc(s["up_in"], 16)
            sp.dma_start(gmask[:, :, :], masks).then_inc(s["gmask_in"], 16)
            sp.dma_start(biasn[:, :, :], bias).then_inc(s["bias_in"], 16)
            sp.dma_start(wmask[:, :, :], consts[:, 2 * P:2 * P + 192].rearrange("p (a w) -> p a w", a=4))\
                .then_inc(s["wmask_in"], 16)
            with sp.Fori(1, NUNIT // RING) as i:
                for r in range(RING):
                    load_unit(RING * i + r, r, RING * i + r - (RING - 1))
            for n in range(NUNIT // RING * RING, NUNIT):
                load_unit(n, n % RING, n - (RING - 1))
            for k in range(KD):
                sp.wait_ge(s["res_done"], k + 1)
                sp.dma_start(out[:, k, :], res[:, k, :]).then_inc(s["stored"], 16)
            sp.wait_ge(s["stored"], 16 * KD)


        @block.gpsimd
        def _(pool):
            pool.memset(one_col[:, :], 1.0).then_inc(s["one_col"], 1)
            pool.wait_ge(s["one_col"], 1)

            def split_unit(n, i, arrived):
                pool.wait_ge(s[f"unit_in{i}"], arrived)
                pool.tensor_tensor(whi[:, i, :], raw[:, i, :], one_col[:, 0:1].broadcast_to([P, BLK * P]),
                                   ALU.mult).then_inc(s["unit_hi"], 1)
                pool.wait_ge(s["unit_hi"], n + 1)
                pool.tensor_tensor(wlo[:, i, :], raw[:, i, :], whi[:, i, :].bitcast(F32), ALU.subtract)\
                    .then_inc(s["unit_split"], 1)

            for n in range(RING):
                split_unit(n, n, 16)
            with pool.Fori(1, NUNIT // RING) as i:
                for r in range(RING):
                    pool.wait_ge(s["unit_used"], RING * i + r - (RING - 1))
                    split_unit(RING * i + r, r, 16 * i + 16)
            for n in range(NUNIT // RING * RING, NUNIT):
                pool.wait_ge(s["unit_used"], n - (RING - 1))
                split_unit(n, n % RING, 16 * (n // RING) + 16)

        @block.tensor
        def _(pe):
            def sums(norm):
                r, W = NORMS[norm]
                nh, hw = norm_halves(W)
                if norm in ADDED:
                    pe.wait_ge(s["sq_added"], (KD - 1) * (ADDED.index(norm) + 1))
                    for x in range(nh):
                        last = pe.matmul(B4[:, x, 0:hw], ones[:, :], scratch(norm)[2][:, x * hw:(x + 1) * hw],
                                         start=True, stop=True)
                    last.then_inc(s["ss_ps"], 1)
                    return
                for k in range(KD):
                    pe.wait_ge(s["sq_done"], KD * r + k + 1)
                    for x in range(nh):
                        last = pe.matmul(B4[:, x, 0:hw], ones[:, :], scratch(norm)[0][:, k % 2, x * hw:(x + 1) * hw],
                                         start=(k == 0), stop=(k == KD - 1))
                    last.then_inc(s["sq_used"], 1)

            def split_ready(group, k):
                pe.wait_ge(s["ulo_done"], KD * SPLITS[group] + k + 1)

            def unit_ready(n):
                pe.wait_ge(s["unit_split"], n + 1)

            def tile_free(t, at_least=2):
                pe.wait_ge(s["evac_done"], t - 1)

            def product(dst, slot, blocks, hi, lo, off, W, first=True, last=True, ready=None, halves=None):
                nh, hw = norm_halves(W)
                halves = halves or [(x * hw, hw) for x in range(nh)]
                for i, (b, k) in enumerate(blocks):
                    if ready:
                        ready(k)
                    for j, (w, u) in enumerate(((whi, hi), (whi, lo), (wlo, hi))):
                        for x, (x0, xw) in enumerate(halves):
                            ins = pe.matmul(dst[:, x, 0:xw], w[:, slot, b * P:(b + 1) * P],
                                            u[:, k, off + x0:off + x0 + xw],
                                            start=(first and i == 0 and j == 0),
                                            stop=(last and i == len(blocks) - 1 and j == 2))
                return ins

            def fm_tile(n, t, off=0, W=T, group=None, halves=None, order=range(KD)):
                unit_ready(n)
                if t >= 2:
                    tile_free(t)
                product(G[:, t % 2], n % RING, [(k, k) for k in order], uhi, ulo, off, W,
                        ready=(lambda k: split_ready(group, order.index(k))) if group else None, halves=halves)\
                    .then_inc(s["unit_used"], 1)

            pe.wait_ge(s["ones_in"], 16)
            sums("mix_pre")
            for name in ("z", "q_gl", "k_gl"):
                for i in range(dict(UNITS)[name]):
                    fm_tile(U0[name] + i, T0[name] + i, group="mix_pre" if name == "z" else None)
            pe.wait_ge(s["up_in"], 16)
            pe.wait_ge(s["evac_done"], T0["z"] + 1)
            def gate_logits(j):
                if j >= 2:
                    pe.wait_ge(s["gate_x"], j - 1)
                for x in range(2):
                    last = pe.matmul(B4[:, 2 * (j % 2) + x, 0:T // 2], upt[:, j * P:(j + 1) * P],
                                     zT[:, x * (T // 2):(x + 1) * (T // 2)], start=True, stop=True)
                last.then_inc(s["gate_ps"], 1)

            gate_logits(0)
            gate_logits(1)

            def by_token(sig, src, i, bank):
                n, t0 = (P, META + P * i) if i < 4 else (META, 0)
                for f in range(4):
                    last = pe.transpose(B4[0:n, bank, f * P:(f + 1) * P], src[:, f, t0:t0 + n], ident[:, :])
                last.then_inc(s[sig], 1)

            for i in range(4):
                fm_tile(U0["v_gl"] + i, T0["v_gl"] + i)
                if i < 2:
                    gate_logits(i + 2)
            for i in range(4):
                fm_tile(U0["q_na"] + i, T0["q_na"] + i, halves=ROWS4)
            pe.wait_ge(s["gate_x"], 4)
            pe.wait_ge(s["ident_in"], 16)
            for i in range(4):
                fm_tile(U0["k_na"] + i, T0["k_na"] + i, halves=ROWS4)
                by_token("vgl_ps", vglT, i, i)
            for i in range(4):
                fm_tile(U0["v_na"] + i, T0["v_na"] + i, halves=ROWS4)
                if i == 0:
                    pe.wait_ge(s["vgl_done"], 1)
                    by_token("vgl_ps", vglT, 4, 0)
            for i in range(4):
                fm_tile(U0["g_gl"] + i, T0["g_gl"] + i)

            pe.wait_ge(s["evac_done"], T0["v_na"] + 4)
            for i in range(5):
                pe.wait_ge(s["vgl_done"], 5)
                if i >= 4:
                    pe.wait_ge(s["by_token_done"], i - 3)
                by_token("by_token_ps", vT, i, i % 4)

            pe.wait_ge(s["kend_done"], 4)
            for i in range(5):
                pe.wait_ge(s["by_token_done"], i + 2)
                by_token("by_token_ps", kend, i, (i + 5) % 4)
            for i in range(NCHUNK - 1):
                for d, c in ((0, i), (1, NCHUNK - 1 - i)):
                    tile, p0, n, _t = chunk_place(c)
                    bank = 2 * (i % 2) + d
                    if i >= 2:
                        pe.wait_ge(s["state_done"], 4 * (i - 1))
                    else:
                        pe.wait_ge(s["by_token_done"], 10)
                    for hh in range(GLA_H):
                        hp, par = hh // 2, hh % 2
                        last = pe.matmul(B4[par * DK:(par + 1) * DK, bank, hp * DV:(hp + 1) * DV],
                                         kendT[p0:p0 + n, tile, (2 * d + hp) * P + par * DK:(2 * d + hp) * P + (par + 1) * DK],
                                         vgl[p0:p0 + n, tile, hh * DV:(hh + 1) * DV], start=True, stop=True)
                    last.then_inc(s["ds_ps"], 1)
            def gla_scores(i):
                n, t0 = (P, META + P * i) if i < 4 else (META, 0)
                if i >= 2:
                    pe.wait_ge(s["amat_done"], i - 1)
                for par in range(2):
                    bank = 2 * (i % 2) + par
                    for d in range(2):
                        for hp in range(2):
                            last = pe.matmul(B4[0:n, bank, (2 * d + hp) * P:(2 * d + hp) * P + n],
                                             kinv[par * DK:(par + 1) * DK, 2 * d + hp, t0:t0 + n],
                                             qdec[par * DK:(par + 1) * DK, 2 * d + hp, t0:t0 + n],
                                             start=True, stop=True)
                last.then_inc(s["a_ps"], 1)

            def gla_values(i):
                n = P if i < 4 else META
                pe.wait_ge(s["amat_done"], i + 1)
                if i >= 2:
                    pe.wait_ge(s["ogl_done"], i - 1)
                if i == 0:
                    pe.wait_ge(s["evac_done"], T0["g_gl"] + 4)
                chunks = (2 * i + 1, 2 * i + 2) if i < 4 else (0,)
                for par in range(2):
                    for hp in range(2):
                        hh = 2 * hp + par
                        pe.matmul(G[:, i % 2, par, hp * P:hp * P + n], vgl[0:n, i, hh * DV:(hh + 1) * DV],
                                  Amat[0:n, i % 2, (2 * par + hp) * P:(2 * par + hp) * P + n],
                                  start=True, stop=False)
                        for x, c in enumerate(chunks):
                            cn, ct = chunk_place(c)[2:]
                            for d in range(2):
                                last = pe.matmul(G[:, i % 2, par, hp * P + x * CHUNK:hp * P + x * CHUNK + cn],
                                                 S[par * DK:(par + 1) * DK, d, c, hp, :],
                                                 qdec[par * DK:(par + 1) * DK, 2 * d + hp, ct:ct + cn],
                                                 start=False, stop=(d == 1 and x == len(chunks) - 1))
                last.then_inc(s["ogl_ps"], 1)

            pe.wait_ge(s["state_done"], 4 * (NCHUNK - 1))
            gla_scores(0)
            for i in range(5):
                if i < 4:
                    gla_scores(i + 1)
                gla_values(i)
            pe.wait_ge(s["ogl_done"], 5)
            pe.wait_ge(s["amat_done"], 5)
            for hh in range(GLA_H):
                pe.wait_ge(s["gsq_done"], hh + 1)
                for x in range(2):
                    bank = B4[:, 2 * (hh % 2) + x, 0:T // 2] if hh < 2 else G[:, hh % 2, x, 0:T // 2]
                    last = pe.matmul(bank, ones[:, :], gsq[:, hh, x * (T // 2):(x + 1) * (T // 2)],
                                     start=True, stop=True)
                last.then_inc(s["gss_ps"], 1)

            def na_scores(st):
                a, hp = st // 4, st % 4
                c0, W = na_window(a)
                if st >= 2:
                    pe.wait_ge(s["na_s"], st - 1)
                else:
                    pe.wait_ge(s["gln_done"], st + 1)
                for par in range(2):
                    bank = 2 * (st % 2) + par
                    q = qna[par * DH:(par + 1) * DH, hp, META + P * a:META + P * (a + 1)]
                    pe.matmul(B4[:, bank, 0:8 * W], q,
                              kna[par * DH:(par + 1) * DH, hp, META + 8 * c0:META + 8 * (c0 + W)],
                              start=True, stop=True)
                    last = pe.matmul(B4[:, bank, 8 * W:8 * W + META], q, kna[par * DH:(par + 1) * DH, hp, 0:META],
                                     start=True, stop=True)
                last.then_inc(s["na_s_ps"], 1)

            def na_transposes(st):
                nb = na_window(st // 4)[1] // 16
                W = 16 * nb
                if st >= 1:
                    pe.wait_ge(s["na_pt0"], st)
                    pe.wait_ge(s["na_pt1"], st)
                for par in range(2):
                    pe.wait_ge(s["na_p"], 2 * st + par + 1)
                    for b in range(nb):
                        pe.transpose(G[:, 0, par, b * P:(b + 1) * P], sc[:, st % 3, par, b * P:(b + 1) * P], ident[:, :])
                    pe.transpose(G[0:META, 0, par, 384:512], sc[:, st % 3, par, 8 * W:8 * W + META], ident[:, :])\
                        .then_inc(s["na_t_ps"], 1)

            def na_values(st):
                a, hp = st // 4, st % 4
                c0, W = na_window(a)
                nb = W // 16
                for par in range(2):
                    hh = 2 * hp + par
                    pe.wait_ge(s["na_pt1" if par else "na_pt0"], st + 1)
                    if st % 4 == 0 and par == 0 and a >= 2:
                        pe.wait_ge(s["na_evac"], a - 1)
                    for b in range(nb):
                        pe.matmul(G[:, 1, a % 2, hh * DH:(hh + 1) * DH], pt[:, st % 2, par, b * P:(b + 1) * P],
                                  vna[:, c0 // 16 + b, hh * DH:(hh + 1) * DH], start=(b == 0), stop=False)
                    pe.matmul(G[:, 1, a % 2, hh * DH:(hh + 1) * DH], pt[0:META, st % 2, par, 384:512],
                              vna[0:META, 4, hh * DH:(hh + 1) * DH], start=False, stop=True)\
                        .then_inc(s["na_o_ps"], 1)

            def na_turn(a, n=P):
                bank = G[:, 1, a % 2] if a < 3 else B4[:, 3 if a == 3 else 0]
                pe.wait_ge(s["na_otok"], a + 1)
                for f in range(4):
                    last = pe.transpose(bank[:, f * P:f * P + n], otok[0:n, a % 2, f * P:(f + 1) * P], ident[0:n, 0:n])
                last.then_inc(s["na_turned"], 1)

            for st in range(21):
                if st < 16:
                    na_scores(st)
                if st == 1:
                    pe.wait_ge(s["gln_done"], 4)
                if 1 <= st <= 16:
                    na_transposes(st - 1)
                if 2 <= st <= 17:
                    na_values(st - 2)
                if st >= 8 and st % 4 == 0:
                    na_turn(st // 4 - 2)
                if st == 16:
                    pe.wait_ge(s["na_s"], 15)
                    for par in range(2):
                        for hp in range(4):
                            last = pe.matmul(B4[0:META, par, hp * META:(hp + 1) * META],
                                             qna[par * DH:(par + 1) * DH, hp, 0:META],
                                             kna[par * DH:(par + 1) * DH, hp, 0:META], start=True, stop=True)
                    last.then_inc(s["meta_s_ps"], 1)
                if st == 17:
                    pe.wait_ge(s["meta_e"], 1)
                    pe.wait_ge(s["na_s"], 16)
                    for hh in range(NA_H):
                        last = pe.transpose(B4[0:META, 2, hh * META:(hh + 1) * META],
                                            sc[0:META, 1, 0, hh * META:(hh + 1) * META], ident[0:META, 0:META])
                    last.then_inc(s["meta_t_ps"], 1)
                if st == 18:
                    pe.wait_ge(s["meta_pt"], 1)
                    pe.wait_ge(s["na_evac"], 3)
                    for hh in range(NA_H):
                        i = 4 * (hh % 2) + hh // 2
                        last = pe.matmul(G[0:META, 1, 0, hh * DH:(hh + 1) * DH], pt[0:META, 0, 0, i * META:(i + 1) * META],
                                         vna[0:META, 4, hh * DH:(hh + 1) * DH], start=True, stop=True)
                    last.then_inc(s["na_o_ps"], 1)
            na_turn(4, META)

            for i in range(8):
                fm_tile(U0["w_o"] + i, T0["w_o"] + i, FT0, FT, group="mix" if i == 0 else None, order=GLA_FIRST)
            sums("mix_post")
            sums("ffn_pre")

            def ffn_pair(name, p, x, group=None, W=FT):
                for half in range(2):
                    n = U0[name] + 2 * p + half
                    t = T0[name] + 2 * p + half
                    pe.wait_ge(s["unit_split"], n + 1)
                    pe.wait_ge(s["evac_done"], t - 1)
                    product(G[:, (T0[name] + half) % 2], (U0[name] + 2 * x + half) % RING, [(k, k) for k in range(KD)],
                            uhi, ulo, 0, W,
                            ready=(lambda k: split_ready(group, k)) if group and half == 0 else None)\
                        .then_inc(s["unit_used"], 1)

            def ffn_in(name, group, W):
                for p in range(4):
                    ffn_pair(name, p, p, group if p == 0 else None, W)
                with pe.Fori(0, (JF - 4) // 3) as i:
                    for r in range(3):
                        ffn_pair(name, 3 * i + 4 + r, 4 + r, None, W)

            def ffn_out(name):
                pe.wait_ge(s["ylow_done"], JF * (1 if name == "ffn_out" else 2))
                with pe.Fori(0, KD // 2) as i:
                    for r in range(2):
                        for x in range(3):
                            pe.wait_ge(s["unit_split"], 6 * i + (U0[name] + 3 * r + x + 1))
                            if x == 0:
                                pe.wait_ge(s["evac_done"], 2 * i + (T0[name] + r - 1))
                            ks = range(BLK * x, min(BLK * (x + 1), JF))
                            product(G[:, (T0[name] + r) % 2], (U0[name] + 3 * r + x) % RING,
                                    [(k - BLK * x, k) for k in ks], yhi, ylo, 0, SEQ, first=(x == 0), last=(x == 2))\
                                .then_inc(s["unit_used"], 1)

            ffn_in("ffn_in", "ffn_pre", FT)
            ffn_out("ffn_out")
            sums("ffn_post")
            pe.wait_ge(s["ada_used"], NMOD * KD)
            pe.wait_ge(s["rstd_done"], NORMS["ffn_post"][0] + 1)
            for m in range(NMOD * KD):
                last = pe.matmul(B4[:, 3, m:m + 1], ada_acc[:, m * P:(m + 1) * P], ones[:, 0:1], start=True, stop=True)
            last.then_inc(s["mod_ps"], 1)

            sums("mix2")
            for i in range(8):
                fm_tile(U0["u2"] + i, T0["u2"] + i, 0, SEQ, group="mix2" if i == 0 else None)
            for i in range(4):
                fm_tile(U0["qi2"] + i, T0["qi2"] + i, 0, SEQ)
            fm_tile(U0["ki2"], T0["ki2"], 0, SEQ)

            fm_tile(U0["wi2"], T0["wi2"], 0, SEQ)
            for name in ("q2", "k2", "v2"):
                for i in range(4):
                    fm_tile(U0[name] + i, T0[name] + i, 0, SEQ)
                    if name == "q2" and i == 1:
                        for f in range(4):
                            last = pe.transpose(B4[:, 0, 8 * f:8 * f + 8], wi2T[:, f * P:(f + 1) * P], ident[0:8, 0:8])
                        last.then_inc(s["wi2_ps"], 1)

            def gate_tile(name, i):
                fm_tile(U0[name] + i, T0[name] + i, 0, SEQ)

            gate_tile("ga2", 0)
            pe.wait_ge(s["wi2_done"], 1)
            pe.wait_ge(s["evac_done"], T0["v2"] + 4)
            for i in range(4):
                for f in range(4):
                    last = pe.transpose(B4[:, i, f * P:(f + 1) * P], v2T[:, f, i * P:(i + 1) * P], ident[:, :])
                last.then_inc(s["v2_ps"], 1)

            for e in range(24):
                b, j = 1 + e // 8, e % 8
                par = j % 2
                if e < 4:
                    pe.wait_ge(s["v2_done"], e + 1)
                else:
                    pe.wait_ge(s["relu_done"], e - 3)
                pe.matmul(B4[:, e % 4, 0:P * (b + 1)], qi2[par * 64:(par + 1) * 64, j // 2, P * b:P * (b + 1)],
                          ki2[par * 64:(par + 1) * 64, 0:P * (b + 1)], start=True, stop=True)\
                    .then_inc(s["idx_ps"], 1)
                if e % 6 == 5:
                    gate_tile("ga2", e // 6 + 1)

            pe.wait_ge(s["relu_done"], 24)
            for j in range(4):
                pe.wait_ge(s["conv31_done"], j + 1)
                last = pe.matmul(B4[:, 0, :], ones[:, :], cacc[:, j, :], start=(j == 0), stop=(j == 3))
            last.then_inc(s["ln_ps"], 1)
            gate_tile("ga2", 5)
            for j in range(4):
                pe.wait_ge(s["lnsq_done"], j + 1)
                last = pe.matmul(B4[:, 1, :], ones[:, :], lnt[:, j % 2, :], start=(j == 0), stop=(j == 3))
                last.then_inc(s["lnsq_used"], 1)
            for i in range(6, 8):
                gate_tile("ga2", i)

            def scores2(q):
                b, hh = q // 8, q % 8
                par = hh % 2
                if q >= 2:
                    pe.wait_ge(s["s2_read"], q - 1)
                elif q == 0:
                    pe.wait_ge(s["ln_read"], 1)
                    pe.wait_ge(s["lnv_read"], 1)
                pe.matmul(B4[:, q % 2, 0:P * (b + 1)], q2[par * 64:(par + 1) * 64, hh // 2, P * b:P * (b + 1)],
                          k2[par * 64:(par + 1) * 64, hh // 2, 0:P * (b + 1)], start=True, stop=True)\
                    .then_inc(s["s2_ps"], 1)

            def transposes2(q):
                b = q // 8
                pe.wait_ge(s["p2_done"], q + 1)
                if q >= 2:
                    pe.wait_ge(s["pt2_done"], q - 1)
                for c in range(b + 1):
                    last = pe.transpose(G[:, q % 2, 1, c * P:(c + 1) * P], S2[:, q % 3, c * P:(c + 1) * P], ident[:, :])
                last.then_inc(s["t2_ps"], 1)

            def values2(q):
                b, hh = q // 8, q % 8
                pe.wait_ge(s["pt2_done"], q + 1)
                if hh == 0 and b >= 2:
                    pe.wait_ge(s["al_done"], 4 * (b - 1))
                for c in range(b + 1):
                    last = pe.matmul(B4[:, 2 + b % 2, hh * 64:(hh + 1) * 64], pt2[:, q % 2, c * P:(c + 1) * P],
                                     v2[:, c, hh * 64:(hh + 1) * 64], start=(c == 0), stop=(c == b))
                last.then_inc(s["o2_ps"], 1)

            def turn2(b):
                pe.wait_ge(s["otok2_done"], b + 1)
                for f in range(4):
                    last = pe.transpose(B4[:, 2 + b % 2, f * P:(f + 1) * P], otok2[:, f * P:(f + 1) * P], ident[:, :])
                last.then_inc(s["turned2"], 1)

            for q in range(37):
                if q < 32:
                    scores2(q)
                    if q % 4 == 1:
                        gate_tile("gb2", q // 4)
                if 1 <= q <= 32:
                    transposes2(q - 1)
                if 2 <= q <= 33:
                    values2(q - 2)
                if q >= 12 and q % 8 == 4:
                    turn2(q // 8 - 1)

            for i in range(8):
                n, hi, lo = U0["proj2"] + i, (ah, ch)[i % 2], (al, cl)[i % 2]
                unit_ready(n)
                if i == 0:
                    pe.wait_ge(s["al_done"], 16)
                    pe.wait_ge(s["evac_done"], T0["proj2"])
                if i == 1:
                    pe.wait_ge(s["cl_done"], 4)
                for ct in range(2):
                    t = T0["proj2"] + 2 * i + ct
                    pe.wait_ge(s["evac_done"], t - 3)
                    last = product(G[:, t % 2, (t // 2) % 2:(t // 2) % 2 + 1], n % RING, [(4 * ct + k, k) for k in range(4)],
                                   hi, lo, 0, SEQ)
                last.then_inc(s["unit_used"], 1)
            for i in range(8):
                n, t = U0["out2"] + i, T0["out2"] + i
                unit_ready(n)
                tile_free(t)
                if i < 2:
                    pe.wait_ge(s["evac_done"], T0["out2"])
                product(G[:, t % 2], n % RING, [(k, k) for k in range(KD)], mh, ml, 0, SEQ,
                        ready=(lambda k: pe.wait_ge(s["ml_done"], k + 1)) if i == 0 else None)\
                    .then_inc(s["unit_used"], 1)
            sums("ffn2")
            ffn_in("ffn_in2", "ffn2", SEQ)
            ffn_out("ffn_out2")
            sums("final")

        @block.scalar
        def _(act):
            def ln_and_exp():
                nc.scalar.preload_act_table_set("natural_log_exp_and_others")

            def squares(norm, src, ready):
                ln_and_exp()
                for k in range(KD):
                    ready(k)
                    square(norm, k, src(k))

            def square(norm, k, src):
                r, W = NORMS[norm]
                if k >= 2:
                    if norm in ADDED:
                        act.wait_ge(s["sq_added"], (KD - 1) * ADDED.index(norm) + k - 1)
                    else:
                        act.wait_ge(s["sq_used"], KD * unadded(norm) + k - 1)
                act.activation(scratch(norm)[0][:, k % 2, 0:W], src, ACT.Square).then_inc(s["sq_done"], 1)

            def root(norm):
                r, W = NORMS[norm]
                nh, hw = norm_halves(W)
                rstd = scratch(norm)[2]
                if norm in ADDED:
                    act.wait_ge(s["ss_ps"], ADDED.index(norm) + 1)
                else:
                    act.wait_ge(s["sq_used"], KD * (unadded(norm) + 1))
                act.activation(rstd[:, 0:W].rearrange("p (x w) -> p x w", x=nh), B4[:, 0:nh, 0:hw], ACT.Ln,
                               bias=v("eps"), scale=1.0 / D).then_inc(s["ln_done"], 1)
                act.wait_ge(s["ln_done"], r + 1)
                act.activation(rstd[:, 0:W], rstd[:, 0:W], ACT.Exp, scale=-0.5).then_inc(s["rstd_done"], 1)

            def high(group, norm, off, shift=None):
                W = NORMS[norm][1]
                for k in range(KD):
                    act.wait_ge(s["u_done"], KD * {"mix_pre": 0, "ffn_pre": 1, "mix2": 2, "ffn2": 3}[norm] + k + 1)
                    if shift is None:
                        ins = act.activation(uhi[:, k, off:off + W], scratch(norm)[1][:, k % 2, 0:W], ACT.Copy)
                    else:
                        ins = act.activation(uhi[:, k, off:off + W], scratch(norm)[1][:, k % 2, 0:W], ACT.Identity,
                                             bias=shift(k))
                    ins.then_inc(s["uhi_done"], 1)

            def tile_ready(n):
                act.wait_ge(s["unit_used"], n + 1)

            def evac(name, i, dst, func=ACT.Copy, rows=P, W=T, **kw):
                n, t = U0[name] + i, T0[name] + i
                nh, hw = norm_halves(W)
                tile_ready(n)
                act.activation(dst.rearrange("p (x w) -> p x w", x=nh), G[0:rows, t % 2, 0:nh, 0:hw], func, **kw)\
                    .then_inc(s["evac_done"], 1)

            def h_here(k):
                act.wait_ge(s[f"h_in{k % 2}"], 16 * (k // 2) + 16)
            act.wait_ge(s["vec_in"], 16)
            act.activation(csilu, v("c", 0, 8), ACT.Silu).then_inc(s["csilu"], 1)
            squares("mix_pre", lambda k: h[:, k, :], h_here)
            root("mix_pre")
            high("mix_pre", "mix_pre", 0)
            evac("z", 0, zT[:, :], rows=32)
            for i in range(2):
                evac("q_gl", i, qgl[:, i, :])
            for i in range(2):
                evac("k_gl", i, kgl[:, i, :])

            def gate(j):
                b = j % 2
                act.wait_ge(s["gate_x"], j + 1)
                act.activation(te[:, b, :], tx[:, b, :], ACT.Abs).then_inc(s["act_step"], 1)
                act.wait_ge(s["act_step"], 2 * j + 1)
                act.activation(te[:, b, :], te[:, b, :], ACT.Exp, scale=-1.0).then_inc(s["act_step"], 1)
                act.wait_ge(s["act_step"], 2 * j + 2)
                act.activation(te[:, b, :], te[:, b, :], ACT.Ln, bias=1.0).then_inc(s["gate_ln"], 1)
                act.wait_ge(s["gate_b"], 2 * j + 1)
                act.activation(te[:, b, :], kend[:, j, :], ACT.Exp, scale=1.0 / 16).then_inc(s["gate_eb"], 1)
                ends = (META - 1, META + CHUNK - 1) if j < 2 else (0, META)
                act.activation(dec[:, j, 0:1], kend[:, j, ends[0]:ends[0] + 1], ACT.Exp, scale=1.0 / 16)
                act.activation(dec[:, j, 1:NCHUNK], kend[:, j, ends[1]:ends[1] + CHUNK * (NCHUNK - 2) + 1:CHUNK], ACT.Exp,
                               scale=1.0 / 16)
                act.wait_ge(s["gate_used"], 2 * j + 1)
                act.activation(te[:, b, :], kend[:, j, :], ACT.Exp, scale=-1.0 / 16).then_inc(s["gate_eb"], 1)
                act.wait_ge(s["gate_b"], 2 * j + 2)
                act.activation(tx[:, b, :], tx[:, b, :], ACT.Exp, scale=1.0 / 16).then_inc(s["gate_ed"], 1)

            ln_and_exp()
            for i in range(4):
                gate(i)
                evac("v_gl", i, vglT[:, i, :])
            def evac_columns(name, i, dst):
                t = T0[name] + i
                tile_ready(U0[name] + i)
                to = dst[:, META:T].rearrange("p (c r) -> p r c", r=GRID_R)
                act.activation(dst[:, 0:META], G[:, t % 2, 0, 0:META], ACT.Copy)
                act.activation(to[:, 0:4, :], G[:, t % 2, 0, META:META + 256].rearrange("p (r c) -> p r c", r=4), ACT.Copy)
                act.activation(to[:, 4:8, :], G[:, t % 2, 1, 0:256].rearrange("p (r c) -> p r c", r=4), ACT.Copy)\
                    .then_inc(s["evac_done"], 1)

            def vgl_evac(i):
                n = P if i < 4 else META
                act.wait_ge(s["vgl_ps"], i + 1)
                act.activation(vgl[0:n, i, :], B4[0:n, i % 4, :], ACT.Copy).then_inc(s["vgl_done"], 1)

            for i in range(4):
                evac_columns("q_na", i, qna[:, i, :])
            for i in range(4):
                evac_columns("k_na", i, kna[:, i, :])
                vgl_evac(i)
            act.wait_ge(s["kend_done"], 4)
            for i in range(4):
                evac_columns("v_na", i, vT[:, i, :])
                if i == 0:
                    vgl_evac(4)
            for i in range(4):
                evac("g_gl", i, sg[:, i, :], ACT.Silu)

            for i in range(5):
                n = P if i < 4 else META
                act.wait_ge(s["by_token_ps"], i + 1)
                act.activation(vna[0:n, i, :], B4[0:n, i % 4, :], ACT.Copy).then_inc(s["by_token_done"], 1)

            ln_and_exp()
            for i in range(5):
                n = P if i < 4 else META
                act.wait_ge(s["by_token_ps"], i + 6)
                if i == 0:
                    act.wait_ge(s["unit_used"], U0["g_gl"] + 4)
                act.activation(kendT[0:n, i, :], B4[0:n, (i + 5) % 4, :], ACT.Copy).then_inc(s["by_token_done"], 1)
            for i in range(5):
                n, t0 = (P, META + P * i) if i < 4 else (META, 0)
                act.wait_ge(s["ogl_ps"], i + 1)
                for par in range(2):
                    ins = act.activation(oT[:, par:4:2, t0:t0 + n],
                                         G[:, i % 2, par, 0:2 * P].rearrange("p (a n) -> p a n", a=2)[:, :, 0:n], ACT.Copy)
                ins.then_inc(s["ogl_done"], 1)
            act.wait_ge(s["ogl_done"], 5)
            for hh in range(GLA_H):
                act.activation(gsq[:, hh, :], oT[:, hh, :], ACT.Square).then_inc(s["gsq_done"], 1)
            for hh in range(GLA_H):
                act.wait_ge(s["gss_ps"], hh + 1)
                src = B4[:, 2 * (hh % 2):2 * (hh % 2) + 2, 0:T // 2] if hh < 2 else G[:, hh % 2, :, 0:T // 2]
                act.activation(grs[:, hh, :].rearrange("p (x w) -> p x w", x=2), src, ACT.Ln,
                               bias=v("eps"), scale=1.0 / DV).then_inc(s["gln_done"], 1)
            act.wait_ge(s["gln_done"], 4)
            act.activation(grs[:, :, :], grs[:, :, :], ACT.Exp, scale=-0.5).then_inc(s["grs_done"], 1)

            def na_exp(st):
                a = st // 4
                W = na_window(a)[1]
                act.wait_ge(s["na_nmx"], st + 1)
                if st % 4 == 0 and a >= 2:
                    act.wait_ge(s["na_rinv"], a - 1)
                for par in range(2):
                    hh = 2 * (st % 4) + par
                    act.activation(sc[:, st % 3, par, 0:8 * W + META], sc[:, st % 3, par, 0:8 * W + META], ACT.Exp,
                                   bias=nmx[:, 2 * (st % 3) + par:2 * (st % 3) + par + 1],
                                   accum_out=row_sum[:, a % 2, hh:hh + 1]).then_inc(s["na_p"], 1)

            def na_turned(a, n=P):
                act.wait_ge(s["na_turned"], a + 1)
                bank = G[:, 1, a % 2] if a < 3 else B4[:, 3 if a == 3 else 0]
                for f in range(4):
                    if a < 4:
                        dst = onaT[:, f, META:T].rearrange("p (r c) -> p c r", r=GRID_R)[:, 16 * a:16 * a + 16, :]
                        src = bank[:, f * P:(f + 1) * P].rearrange("p (c r) -> p c r", r=GRID_R)
                    else:
                        dst, src = onaT[:, f, 0:META], bank[:, f * P:f * P + n]
                    ins = act.activation(dst, src, ACT.Copy, scale=v("na_gain", f))
                ins.then_inc(s["na_evac"], 1)

            def na_root(a, n=P):
                act.wait_ge(s["na_o_scaled"], a + 1)
                if a >= 2:
                    act.wait_ge(s["na_otok"], a - 1)
                if a >= 1:
                    act.wait_ge(s["na_ss"], a)
                act.activation(osq[0:n], otok[0:n, a % 2, :], ACT.Square, accum_out=na_ssum[0:n, a % 2:a % 2 + 1]).then_inc(s["na_ss"], 1)
                act.wait_ge(s["na_ss"], a + 1)
                act.activation(na_rstd[0:n, a % 2:a % 2 + 1], na_ssum[0:n, a % 2:a % 2 + 1], ACT.Ln, bias=vec[0:n, VCOL["eps"]:VCOL["eps"] + 1],
                               scale=1.0 / 512).then_inc(s["na_ln"], 1)
                act.wait_ge(s["na_ln"], a + 1)
                act.activation(na_rstd[0:n, a % 2:a % 2 + 1], na_rstd[0:n, a % 2:a % 2 + 1], ACT.Exp, scale=-0.5).then_inc(s["na_rstd"], 1)

            def na_pt_evac(st):
                nb = na_window(st // 4)[1] // 16
                act.wait_ge(s["na_t_ps"], 2 * st + 1)
                if st >= 2:
                    act.wait_ge(s["na_o_ps"], 2 * st - 3)
                act.activation(pt[:, st % 2, 0, 0:nb * P], G[:, 0, 0, 0:nb * P], ACT.Copy)
                act.activation(pt[0:META, st % 2, 0, 384:512], G[0:META, 0, 0, 384:512], ACT.Copy).then_inc(s["na_pt0"], 1)

            for st in range(21):
                if 1 <= st <= 16:
                    na_pt_evac(st - 1)
                if st < 16:
                    na_exp(st)
                if 6 <= st <= 18 and st % 4 == 2:
                    na_root(st // 4 - 1)
                if st == 16:
                    act.wait_ge(s["meta_s"], 1)
                    act.activation(sc[0:META, 1, 0, 0:P], sc[0:META, 1, 0, 0:P], ACT.Exp).then_inc(s["meta_e"], 1)
                if st == 17:
                    act.wait_ge(s["meta_t_ps"], 1)
                    act.activation(pt[0:META, 0, 0, 0:P], B4[0:META, 2, 0:P], ACT.Copy).then_inc(s["meta_pt"], 1)
                if st == 19:
                    na_root(4, META)
                if st >= 8 and st % 4 == 0:
                    na_turned(st // 4 - 2)
                if st == 12:
                    for k in range(4):
                        act.wait_ge(s["ogl_out"], k + 1)
                        act.activation(uhi[:, 4 + k, :], oT[:, k, :], ACT.Copy).then_inc(s["uhi_done"], 1)
            na_turned(4, META)
            act.wait_ge(s["na_evac"], 5)
            for k in range(4):
                act.activation(uhi[:, k, :], onaT[:, k, :], ACT.Copy).then_inc(s["uhi_done"], 1)
            ln_and_exp()
            for i in range(8):
                t = T0["w_o"] + i
                evac("w_o", i, m1[:, i, :], W=FT)
                act.wait_ge(s["evac_done"], t + 1)
                square("mix_post", i, m1[:, i, :])
            root("mix_post")
            squares("ffn_pre", lambda k: h[:, k, FT0:T], lambda k: act.wait_ge(s["h_done"], k + 1))
            root("ffn_pre")
            high("ffn_pre", "ffn_pre", 0)

            def ffn_evac(name, p, x, half, dst, func=ACT.Copy, W=FT):
                act.wait_ge(s["unit_used"], U0[name] + 2 * p + (half + 1))
                nh, hw = norm_halves(W)
                act.activation(dst.rearrange("p (x w) -> p x w", x=nh), G[:, (T0[name] + half) % 2, 0:nh, 0:hw], func)\
                    .then_inc(s["evac_done"], 1)

            def ffn_act(p, x, early):
                if not early:
                    act.wait_ge(s["conv_done"], 2 * p - 5)
                ffn_evac("ffn_in", p, x, 0, av[:, x, 0:FT])
                if not early:
                    act.wait_ge(s["conv_done"], 2 * p - 4)
                ffn_evac("ffn_in", p, x, 1, ag[:, x, 0:FT])
                act.wait_ge(s["conv_done"], 2 * p + 2)
                act.activation(tg[:, x, :], tg[:, x, :], ACT.Gelu_apprx_tanh).then_inc(s["gelu_done"], 1)
                ffn_high(p, x, 0)

            def ffn_high(p, x, before):
                act.wait_ge(s["yf_done"], p + (before + 1))
                act.wait_ge(s["yf_done"], 1)
                act.activation(yhi[:, bass.ds(p, 1), :].rearrange("p a n -> p (a n)"), yf[:, x, :], ACT.Copy)\
                    .then_inc(s["yhi_done"], 1)

            for p in range(4):
                ffn_act(p, p % 3, p < 3)
            with act.Fori(0, (JF - 4) // 3) as i:
                for r in range(3):
                    ffn_act(3 * i + 4 + r, (4 + r) % 3, False)
            ln_and_exp()
            for c in range(KD):
                t = T0["ffn_out"] + c
                for m in range(NMOD * c, NMOD * (c + 1)):
                    if m >= ADA_RING:
                        act.wait_ge(s["ada_used"], m - ADA_RING + 1)
                    act.dma_start(ada_in[:, m % ADA_RING, :], ada[m, :, :]).then_inc(s[f"ada_in{m % ADA_RING}"], 16)
                act.wait_ge(s["unit_used"], U0["ffn_out"] + 3 * c + 3)
                act.activation(m2[:, c, :], G[:, t % 2, 0, :], ACT.Copy).then_inc(s["evac_done"], 1)
                act.wait_ge(s["evac_done"], t + 1)
                square("ffn_post", c, m2[:, c, :])
            root("ffn_post")
            act.wait_ge(s["mod_ps"], 1)
            act.activation(mod, B4[:, 3, 0:NMOD * KD], ACT.Copy).then_inc(s["mod_done"], 1)

            squares("mix2", lambda k: h[:, k, META:T], lambda k: act.wait_ge(s["h_done"], KD + k + 1))
            act.dma_start(dtab[:, :], consts[:, 576:576 + 896]).then_inc(s["dtab_in"], 16)
            act.dma_start(caus[:, :], consts[:, 448:576]).then_inc(s["caus_in"], 16)
            root("mix2")
            act.wait_ge(s["modv_done"], 1)
            high("mix2", "mix2", 0, lambda k: mod[:, k:k + 1])
            for j in range(4):
                evac("u2", 2 * j, z2[:, j, CONV_W - 1:CONV_W - 1 + SEQ], W=SEQ)
                if j >= 2:
                    act.wait_ge(s["z_done"], j - 1)
                evac("u2", 2 * j + 1, sgm[:, j % 2, :], ACT.Sigmoid, W=SEQ)
            for i in range(4):
                evac("qi2", i, qi2[:, i, :], W=SEQ)
            evac("ki2", 0, ki2[:, :], W=SEQ)
            evac("wi2", 0, wi2T[:, :], rows=8, W=SEQ)
            for i in range(4):
                evac("q2", i, q2[:, i, :], W=SEQ)
                if i == 1:
                    act.wait_ge(s["wi2_ps"], 1)
                    act.activation(wi2[:, :, :], B4[:, 0, 0:32].rearrange("p (a n) -> p a n", a=4), ACT.Copy,
                                   scale=8 ** -0.5).then_inc(s["wi2_done"], 1)
            for i in range(4):
                evac("k2", i, k2[:, i, :], W=SEQ)
            for i in range(4):
                evac("v2", i, v2T[:, i, :], W=SEQ)
            def gate_evac(i):
                evac("ga2", i, sga[:, i, :], W=SEQ)

            gate_evac(0)
            for i in range(4):
                act.wait_ge(s["v2_ps"], i + 1)
                act.activation(v2[:, i, :], B4[:, i, :], ACT.Copy).then_inc(s["v2_done"], 1)
            act.wait_ge(s["z_done"], 4)
            for e in range(24):
                b = 1 + e // 8
                act.wait_ge(s["idx_ps"], e + 1)
                if e >= 2:
                    act.wait_ge(s["idx_acc"], e - 1)
                act.activation(sgm[:, e % 2, 0:P * (b + 1)], B4[:, e % 4, 0:P * (b + 1)], ACT.Relu, scale=64 ** -0.5)\
                    .then_inc(s["relu_done"], 1)
                if e % 6 == 5:
                    gate_evac(e // 6 + 1)
            for j in range(4):
                act.wait_ge(s["lnc_done"], j + 1)
                if j >= 2:
                    act.wait_ge(s["lnsq_used"], j - 1)
                act.activation(lnt[:, j % 2, :], cacc[:, j, :], ACT.Square).then_inc(s["lnsq_done"], 1)
            gate_evac(5)
            act.wait_ge(s["lnsq_used"], 4)
            act.activation(lnr[:, :], B4[:, 1, :], ACT.Ln, bias=v("eps"), scale=1.0 / CONV_CH).then_inc(s["lnv_read"], 1)
            act.wait_ge(s["lnv_read"], 1)
            act.activation(lnr[:, :], lnr[:, :], ACT.Exp, scale=-0.5).then_inc(s["lnr_done"], 1)
            for j in range(4):
                act.wait_ge(s["lnx_done"], j + 1)
                if j >= 2:
                    act.wait_ge(s["cl_done"], j - 1)
                act.activation(lnt[:, j % 2, :], cacc[:, j, :], ACT.Silu, bias=v("ln_b", j)).then_inc(s["silu_done"], 1)
                act.wait_ge(s["silu_done"], j + 1)
                act.activation(ch[:, j, :], lnt[:, j % 2, :], ACT.Copy).then_inc(s["ch_done"], 1)
            for i in range(6, 8):
                gate_evac(i)
            act.wait_ge(s["evac_done"], T0["ga2"] + 8)
            act.activation(sga[:, :, :], sga[:, :, :], ACT.Sigmoid).then_inc(s["sga_done"], 1)

            def exp2(q):
                b, hh = q // 8, q % 8
                act.wait_ge(s["nmx2"], q + 1)
                if hh == 0 and b >= 2:
                    act.wait_ge(s["rinv2"], b - 1)
                act.activation(S2[:, q % 3, 0:P * (b + 1)], S2[:, q % 3, 0:P * (b + 1)], ACT.Exp,
                               bias=nmx[:, q % 3:q % 3 + 1], accum_out=row_sum[:, b % 2, hh:hh + 1]).then_inc(s["p2_done"], 1)

            def pt2_evac(q):
                b = q // 8
                act.wait_ge(s["t2_ps"], q + 1)
                if q >= 2:
                    act.wait_ge(s["o2_ps"], q - 1)
                act.activation(pt2[:, q % 2, 0:P * (b + 1)], G[:, q % 2, 1, 0:P * (b + 1)], ACT.Copy)\
                    .then_inc(s["pt2_done"], 1)

            for q in range(37):
                if q < 32 and q % 4 == 1:
                    i = q // 4
                    if i == 4:
                        act.wait_ge(s["cl_done"], 4)
                    evac("gb2", i, sgb[i // 4][:, i % 4, :], W=SEQ)
                if 1 <= q <= 32:
                    pt2_evac(q - 1)
                if q < 32:
                    exp2(q)
                if q >= 12 and q % 8 == 4:
                    b = q // 8 - 1
                    act.wait_ge(s["turned2"], b + 1)
                    for f in range(4):
                        act.activation(ah[:, f, P * b:P * (b + 1)], B4[:, 2 + b % 2, f * P:(f + 1) * P], ACT.Copy)\
                            .then_inc(s["ah_done"], 1)
            act.wait_ge(s["evac_done"], T0["gb2"] + 8)
            for half in sgb:
                act.activation(half[:, :, :], half[:, :, :], ACT.Sigmoid).then_inc(s["sgb_done"], 1)
            for i in range(4):
                for br in range(2):
                    tile_ready(U0["proj2"] + 2 * i + br)
                    if i >= 1:
                        act.wait_ge(s["ml_done"], 2 * i)
                    for ct in range(2):
                        t = T0["proj2"] + 4 * i + 2 * br + ct
                        act.activation(yab[:, 2 * br + ct, :], G[:, t % 2, (t // 2) % 2, :], ACT.Copy)\
                            .then_inc(s["evac_done"], 1)
                for ct in range(2):
                    c = 2 * i + ct
                    act.wait_ge(s["mrg_done"], c + 1)
                    act.activation(mh[:, c, :], yab[:, ct, :], ACT.Copy).then_inc(s["mh_done"], 1)

            def residual_tiles(name, per, scale, before, rt, norm):
                ln_and_exp()
                for c in range(KD):
                    t = T0[name] + c
                    act.wait_ge(s["unit_used"], U0[name] + per * (c + 1))
                    if c >= 2:
                        act.wait_ge(s["h_done"], before + c - 1)
                    act.activation(rt[:, c % 2, :], G[:, t % 2, 0, :], ACT.Copy, scale=scale(c)).then_inc(s["evac_done"], 1)
                    if c >= 1:
                        act.wait_ge(s["h_done"], before + c)
                        square(norm, c - 1, h[:, c - 1, META:T])
                act.wait_ge(s["h_done"], before + KD)
                square(norm, KD - 1, h[:, KD - 1, META:T])

            residual_tiles("out2", 1, lambda c: mod[:, 16 + c:17 + c], 2 * KD, rt, "ffn2")
            root("ffn2")
            high("ffn2", "ffn2", 0, lambda k: mod[:, 24 + k:25 + k])

            def ffn2_act(p, x, early):
                if not early:
                    act.wait_ge(s["yf_done"], p + (JF - 2))
                ffn_evac("ffn_in2", p, x, 0, tv[:, x, :], ACT.Silu, W=SEQ)
                ffn_evac("ffn_in2", p, x, 1, tg[:, x, :], W=SEQ)
                ffn_high(p, x, JF)

            for p in range(4):
                ffn2_act(p, p % 3, p < 3)
            with act.Fori(0, (JF - 4) // 3) as i:
                for r in range(3):
                    ffn2_act(3 * i + 4 + r, (4 + r) % 3, False)
            residual_tiles("ffn_out2", 3, lambda c: mod[:, 40 + c:41 + c], 3 * KD, tv, "final")
            root("final")

        @block.vector
        def _(dve):
            step = [0]

            def link(ins):
                step[0] += 1
                ins.then_inc(s["dve_step"], 1)
                dve.wait_ge(s["dve_step"], step[0])

            def normalise(norm, group, off, hoff, gain, shift=None):
                r, W = NORMS[norm]
                base = KD * SPLITS[group]
                ub, rstd = scratch(norm)[1], scratch(norm)[2]
                dve.wait_ge(s["rstd_done"], r + 1)
                for k in range(KD + 1):
                    if k < KD:
                        if k >= 2:
                            dve.wait_ge(s["ulo_done"], base + k - 1)
                        dve.scalar_tensor_tensor(ub[:, k % 2, 0:W], h[:, k, hoff:hoff + W], gain(k), rstd[:, 0:W],
                                                 ALU.mult, ALU.mult).then_inc(s["u_done"], 1)
                    if k >= 1:
                        q = k - 1
                        dve.wait_ge(s["uhi_done"], base + q + 1)
                        if shift is None:
                            ins = dve.tensor_tensor(ulo[:, q, off:off + W], ub[:, q % 2, 0:W],
                                                    uhi[:, q, off:off + W].bitcast(F32), ALU.subtract)
                        else:
                            ins = dve.scalar_tensor_tensor(ulo[:, q, off:off + W], ub[:, q % 2, 0:W], shift(q),
                                                           uhi[:, q, off:off + W].bitcast(F32), ALU.add, ALU.subtract)
                        ins.then_inc(s["ulo_done"], 1)
                dve.wait_ge(s["ulo_done"], base + KD)

            def add_square(norm, k):
                r, W = NORMS[norm]
                sq, _ub, acc = scratch(norm)
                before = (KD - 1) * ADDED.index(norm)
                dve.wait_ge(s["sq_done"], KD * r + k + 1)
                if k >= 2:
                    dve.wait_ge(s["sq_added"], before + k - 1)
                dve.tensor_tensor(acc[:, 0:W], sq[:, 0, 0:W] if k == 1 else acc[:, 0:W], sq[:, k % 2, 0:W], ALU.add)\
                   .then_inc(s["sq_added"], 1)

            def add_normed(norm, m, gain, hoff, count):
                r, W = NORMS[norm]
                ub, rstd = scratch(norm)[1], scratch(norm)[2]
                dve.wait_ge(s["rstd_done"], r + 1)
                for k in range(KD + 1):
                    if k < KD:
                        if k >= 2:
                            dve.wait_ge(s["h_done"], count + k - 1)
                        dve.scalar_tensor_tensor(ub[:, k % 2, 0:W], m[:, k, 0:W], gain(k), rstd[:, 0:W],
                                                 ALU.mult, ALU.mult).then_inc(s["normed"], 1)
                    if k >= 1:
                        q = k - 1
                        dve.wait_ge(s["normed"], count + q + 1)
                        dve.tensor_tensor(h[:, q, hoff:hoff + W], h[:, q, hoff:hoff + W], ub[:, q % 2, 0:W], ALU.add)\
                           .then_inc(s["h_done"], 1)

            normalise("mix_pre", "mix_pre", 0, 0, lambda k: v("mix_pre", k))

            dve.wait_ge(s["gla_in"], 16)
            for j in range(4):
                b, hp, fwd = j % 2, j % 2, j < 2
                dve.wait_ge(s["gate_ps"], j + 1)
                dve.tensor_scalar(tx[:, b, :].rearrange("p (x w) -> p x w", x=2), B4[:, 2 * b:2 * b + 2, 0:T // 2],
                                  v("gate_bias", j), None, ALU.add).then_inc(s["gate_x"], 1)
                dve.wait_ge(s["gate_ln"], j + 1)
                link(dve.scalar_tensor_tensor(tx[:, b, :], tx[:, b, :], 0.0, te[:, b, :], ALU.min, ALU.subtract))
                flip = slice(None) if fwd else slice(None, None, -1)
                dve.tensor_tensor_scan(kend[:, j, flip], scan_keep[:, j // 2, flip], tx[:, b, flip], 0.0,
                                       ALU.mult, ALU.add).then_inc(s["gate_b"], 1)
                if j == 0:
                    dve.wait_ge(s["evac_done"], T0["k_gl"] + 2)
                dve.wait_ge(s["gate_eb"], 2 * j + 1)
                dve.scalar_tensor_tensor(qdec[:, j, :], qgl[:, hp, :], DK ** -0.5, te[:, b, :], ALU.mult, ALU.mult)\
                   .then_inc(s["gate_used"], 1)
                dve.wait_ge(s["gate_b"], 2 * j + 1)
                e0, e1 = (META - 1, CHUNK - 1) if fwd else (0, 0)
                body = kend[:, j, META:T].rearrange("p (c n) -> p c n", n=CHUNK)
                dve.tensor_tensor(tx[:, b, META:T].rearrange("p (c n) -> p c n", n=CHUNK),
                                  body[:, :, e1:e1 + 1].broadcast_to([P, NCHUNK - 1, CHUNK]), body, ALU.subtract)
                dve.tensor_tensor(tx[:, b, 0:META], kend[:, j, e0:e0 + 1].broadcast_to([P, META]), kend[:, j, 0:META],
                                  ALU.subtract).then_inc(s["gate_b"], 1)
                dve.wait_ge(s["gate_eb"], 2 * j + 2)
                dve.tensor_tensor(kinv[:, j, :], kgl[:, hp, :], te[:, b, :], ALU.mult).then_inc(s["gate_used"], 1)
                dve.wait_ge(s["gate_ed"], j + 1)
                dve.tensor_tensor(kend[:, j, :], kgl[:, hp, :], tx[:, b, :], ALU.mult).then_inc(s["kend_done"], 1)

            dve.wait_ge(s["unit_used"], U0["g_gl"] + 4)
            dve.memset(S[:, 0, 0, :, :], 0.0)
            link(dve.memset(S[:, 1, NCHUNK - 1, :, :], 0.0))
            for i in range(NCHUNK - 1):
                for d, c in ((0, i), (1, NCHUNK - 1 - i)):
                    to = c + 1 if d == 0 else c - 1
                    dve.wait_ge(s["ds_ps"], 2 * i + d + 1)
                    if i >= 1:
                        dve.wait_ge(s["state_done"], 4 * i)
                    for hp in range(2):
                        dve.scalar_tensor_tensor(S[:, d, to, hp, :], S[:, d, c, hp, :], dec[:, 2 * d + hp, c:c + 1],
                                                 B4[:, 2 * (i % 2) + d, hp * DV:(hp + 1) * DV], ALU.mult, ALU.add)\
                           .then_inc(s["state_done"], 1)
            dve.wait_ge(s["gmask_in"], 16)
            link(dve.memset(Amat[:, :, :], 0.0))
            for i in range(5):
                n = P if i < 4 else META
                dve.wait_ge(s["a_ps"], i + 1)
                if i >= 2:
                    dve.wait_ge(s["ogl_ps"], i - 1)
                for par in range(2):
                    for d in range(2):
                        if d == 1:
                            link(last)
                        last = dve.copy_predicated(
                            Amat[0:n, i % 2, 256 * par:256 * par + 256].rearrange("p (a c) -> p a c", a=2)[:, :, 0:n],
                            gmask[0:n, d, 0:n].unsqueeze(1).broadcast_to([n, 2, n]),
                            B4[0:n, 2 * (i % 2) + par, 256 * d:256 * d + 256].rearrange("p (a c) -> p a c", a=2)[:, :, 0:n])
                last.then_inc(s["amat_done"], 1)
            def gla_out():
                dve.wait_ge(s["evac_done"], T0["g_gl"] + 4)
                dve.wait_ge(s["grs_done"], 1)
                for hh in range(GLA_H):
                    link(dve.scalar_tensor_tensor(oT[:, hh, :], oT[:, hh, :], v("gla_gain"), grs[:, hh, :],
                                                  ALU.mult, ALU.mult))
                    dve.tensor_tensor(oT[:, hh, :], oT[:, hh, :], sg[:, hh, :], ALU.mult).then_inc(s["ogl_out"], 1)

            dve.wait_ge(s["bias_in"], 16)
            dve.wait_ge(s["wmask_in"], 16)

            def na_soft(st):
                a, hp = st // 4, st % 4
                c0, W = na_window(a)
                w0 = c0 - 16 * (a - 1)
                b = st % 3
                bank = 2 * (st % 2)
                dve.wait_ge(s["na_s_ps"], st + 1)
                if st >= 3:
                    dve.wait_ge(s["na_t_ps"], 2 * (st - 2))
                dve.scalar_tensor_tensor(sc[:, b, :, 0:8 * W], B4[:, bank:bank + 2, 0:8 * W], DH ** -0.5,
                                         biasn[:, 2 * hp:2 * hp + 2, 8 * w0:8 * (w0 + W)], ALU.mult, ALU.add)
                dve.tensor_scalar(sc[:, b, :, 8 * W:8 * W + META], B4[:, bank:bank + 2, 8 * W:8 * W + META],
                                  DH ** -0.5, None, ALU.mult).then_inc(s["na_s"], 1)
                dve.wait_ge(s["na_s"], st + 1)
                for par in range(2):
                    x = sc[:, b, par, 0:8 * W].rearrange("p (w r) -> p w r", r=8)
                    last = dve.tensor_tensor(x, x, wmask[:, a, 0:W].unsqueeze(2).broadcast_to([P, W, 8]), ALU.add)
                link(last)
                link(dve.tensor_reduce(mx[:, 0:2], sc[:, b, :, 0:8 * W + META], AX.X, ALU.max))
                dve.tensor_scalar(nmx[:, 2 * b:2 * b + 2], mx[:, 0:2], -1.0, None, ALU.mult).then_inc(s["na_nmx"], 1)

            def na_pt_copy(st):
                nb = na_window(st // 4)[1] // 16
                dve.wait_ge(s["na_t_ps"], 2 * st + 2)
                if st >= 2:
                    dve.wait_ge(s["na_o_ps"], 2 * st - 2)
                dve.tensor_copy(pt[:, st % 2, 1, 0:nb * P], G[:, 0, 1, 0:nb * P])
                dve.tensor_copy(pt[0:META, st % 2, 1, 384:512], G[0:META, 0, 1, 384:512]).then_inc(s["na_pt1"], 1)

            def na_divide(a, n=P):
                if a < 4:
                    dve.wait_ge(s["na_p"], 8 * (a + 1))
                dve.reciprocal(rinv[0:n], row_sum[0:n, a % 2, :]).then_inc(s["na_rinv"], 1)
                dve.wait_ge(s["na_rinv"], a + 1)
                dve.wait_ge(s["na_o_ps"], 8 * (a + 1) if a < 4 else 33)
                if a >= 2:
                    dve.wait_ge(s["na_turned"], a - 1)
                dve.tensor_tensor(otok[0:n, a % 2, :].rearrange("p (h e) -> p h e", h=NA_H),
                                  G[0:n, 1, a % 2, :].rearrange("p (h e) -> p h e", h=NA_H),
                                  rinv[0:n].unsqueeze(2).broadcast_to([n, NA_H, DH]), ALU.mult)\
                   .then_inc(s["na_o_scaled"], 1)

            def na_norm(a, n=P):
                dve.wait_ge(s["na_rstd"], a + 1)
                dve.tensor_scalar(otok[0:n, a % 2, :], otok[0:n, a % 2, :], na_rstd[0:n, a % 2:a % 2 + 1], None, ALU.mult).then_inc(s["na_otok"], 1)

            def split_mix(src, first):
                for q in range(first, first + 4):
                    k = GLA_FIRST[q]
                    dve.wait_ge(s["uhi_done"], KD * SPLITS["mix"] + q + 1)
                    dve.tensor_tensor(ulo[:, k, :], src[:, k % 4, :], uhi[:, k, :].bitcast(F32), ALU.subtract)\
                       .then_inc(s["ulo_done"], 1)

            for st in range(20):
                if st < 16:
                    na_soft(st)
                if 1 <= st <= 16:
                    na_pt_copy(st - 1)
                if st == 1:
                    gla_out()
                if 6 <= st <= 18 and st % 4 == 2:
                    na_divide(st // 4 - 1)
                if st >= 7 and st % 4 == 3:
                    na_norm(st // 4 - 1)
                if st == 12:
                    split_mix(oT, 0)
                if st == 16:
                    dve.wait_ge(s["meta_s_ps"], 1)
                    ms = sc[0:META, 1, 0, 0:P].rearrange("p (h k) -> p h k", h=NA_H)
                    link(dve.tensor_scalar(sc[0:META, 1, 0, 0:P].rearrange("p (a n) -> p a n", a=2), B4[0:META, 0:2, 0:64],
                                           DH ** -0.5, None, ALU.mult))
                    link(dve.tensor_reduce(mx[0:META], ms, AX.X, ALU.max))
                    dve.tensor_tensor(ms, ms, mx[0:META].unsqueeze(2).broadcast_to([META, NA_H, META]), ALU.subtract)\
                       .then_inc(s["meta_s"], 1)
                if st == 18:
                    dve.wait_ge(s["meta_e"], 1)
                    link(dve.tensor_reduce(row_sum[0:META, 0, :].rearrange("p (b a) -> p a b", a=2),
                                           ms.rearrange("p (a b) k -> p a b k", a=2), AX.X, ALU.add))
                    na_divide(4, META)
            na_norm(4, META)
            split_mix(onaT, 4)
            for k in range(1, KD):
                add_square("mix_post", k)
            add_normed("mix_post", m1, lambda k: v("mix_post", k), FT0, 0)
            normalise("ffn_pre", "ffn_pre", 0, FT0, lambda k: v("ffn_pre", k))

            dve.memset(av[:, :, FT:FT + 1], 0.0)
            link(dve.memset(ag[:, :, FT:FT + 1], 0.0))

            def conv3(p, x, half, early):
                src, dst = ((av, tv), (ag, tg))[half]
                w = lambda k: vec[:, bass.ds(VCOL["cw"] + 44 * k + half + 2 * p, 1)]
                taps = [src[:, x, META - FT0 - 1 + k:META - FT0 - 1 + k + SEQ] for k in range(3)]
                dve.wait_ge(s["evac_done"], 2 * p + (T0["ffn_in"] + half + 1))
                if not early:
                    dve.wait_ge(s["ylow_done"], p - 2)
                dve.tensor_scalar(dst[:, x, :], taps[0], w(0), vec[:, bass.ds(VCOL["cb"] + half + 2 * p, 1)],
                                  ALU.mult, ALU.add).then_inc(s["conv_step"], 1)
                dve.wait_ge(s["conv_step"], 4 * p + (2 * half + 1))
                dve.scalar_tensor_tensor(dst[:, x, :], taps[1], w(1), dst[:, x, :], ALU.mult, ALU.add)\
                   .then_inc(s["conv_step"], 1)
                dve.wait_ge(s["conv_step"], 4 * p + (2 * half + 2))
                dve.scalar_tensor_tensor(dst[:, x, :], taps[2], w(2), dst[:, x, :], ALU.mult, ALU.add)\
                   .then_inc(s["conv_done"], 1)

            def gated(p, x, before):
                dve.tensor_tensor(yf[:, x, :], tv[:, x, :], tg[:, x, :], ALU.mult).then_inc(s["yf_done"], 1)
                dve.wait_ge(s["yhi_done"], p + (before + 1))
                dve.tensor_tensor(ylo[:, bass.ds(p, 1), :].rearrange("p a n -> p (a n)"), yf[:, x, :],
                                  yhi[:, bass.ds(p, 1), :].rearrange("p a n -> p (a n)").bitcast(F32), ALU.subtract)\
                   .then_inc(s["ylow_done"], 1)

            def ffn_dve(p, x, early):
                conv3(p, x, 0, early)
                conv3(p, x, 1, early)
                dve.wait_ge(s["gelu_done"], p + 1)
                gated(p, x, 0)

            for p in range(4):
                ffn_dve(p, p % 3, p < 3)
            with dve.Fori(0, (JF - 4) // 3) as i:
                for r in range(3):
                    ffn_dve(3 * i + 4 + r, (4 + r) % 3, False)
            dve.wait_ge(s["ylow_done"], JF)
            dve.wait_ge(s["csilu"], 1)
            for m in range(NMOD * KD):
                k, part = m // NMOD, m % NMOD
                acc = ada_acc[:, 1024 * part:1024 * (part + 1)]
                dve.wait_ge(s[f"ada_in{m % ADA_RING}"], 16 * (m // ADA_RING) + 16)
                if k == 0:
                    ins = dve.tensor_scalar(acc, ada_in[:, m % ADA_RING, :], csilu[:, k:k + 1], None, ALU.mult)
                else:
                    dve.wait_ge(s["ada_used"], m - NMOD + 1)
                    ins = dve.scalar_tensor_tensor(acc, ada_in[:, m % ADA_RING, :], csilu[:, k:k + 1], acc,
                                                   ALU.mult, ALU.add)
                ins.then_inc(s["ada_used"], 1)
                if m % NMOD == NMOD - 1 and k >= 1:
                    add_square("ffn_post", k)
            add_normed("ffn_post", m2, lambda k: v("ffn_post", k), META, KD)

            dve.wait_ge(s["mod_done"], 1)
            link(dve.tensor_tensor(mod, mod, v("b_ada", 0, 48), ALU.add))
            dve.scalar_tensor_tensor(gm2, mod[:, 8:16], 1.0, v("mix2", 0, 8), ALU.add, ALU.mult)
            dve.scalar_tensor_tensor(gf2, mod[:, 32:40], 1.0, v("ffn2", 0, 8), ALU.add, ALU.mult).then_inc(s["modv_done"], 1)
            dve.wait_ge(s["modv_done"], 1)
            normalise("mix2", "mix2", 0, META, lambda k: gm2[:, k:k + 1], lambda k: mod[:, k:k + 1])
            link(dve.memset(z2[:, :, 0:CONV_W - 1], 0.0))
            for j in range(4):
                dve.wait_ge(s["evac_done"], T0["u2"] + 2 * j + 2)
                x = z2[:, j, CONV_W - 1:CONV_W - 1 + SEQ]
                dve.tensor_tensor(x, x, sgm[:, j % 2, :], ALU.mult).then_inc(s["z_done"], 1)
            dve.wait_ge(s["z_done"], 4)
            for j in range(4):
                dve.tensor_scalar(cacc[:, j, :], z2[:, j, 0:SEQ], v("w_dw", j), v("b_dw", j), ALU.mult, ALU.add)\
                   .then_inc(s["tap_done"], 1)
            with dve.Fori(1, CONV_W - 1) as k:
                for j in range(4):
                    dve.wait_ge(s["tap_done"], 4 * k + (j - 3))
                    dve.scalar_tensor_tensor(cacc[:, j, :], z2[:, j, bass.ds(k, SEQ)],
                                             vec[:, bass.ds(VCOL["w_dw"] + j + 4 * k, 1)], cacc[:, j, :],
                                             ALU.mult, ALU.add).then_inc(s["tap_done"], 1)
            for j in range(4):
                k = CONV_W - 1
                dve.wait_ge(s["tap_done"], 4 * k + (j - 3))
                dve.scalar_tensor_tensor(cacc[:, j, :], z2[:, j, k:k + SEQ], v("w_dw", 4 * k + j), cacc[:, j, :],
                                         ALU.mult, ALU.add).then_inc(s["conv31_done"], 1)

            def scx(b):
                first = (0, 0, 256, 640)[b]
                return scb[:, first:first + P * (b + 1)]

            dve.wait_ge(s["wi2_done"], 1)
            e = 0
            for b in range(1, 4):
                for j in range(8):
                    dve.wait_ge(s["relu_done"], e + 1)
                    r = sgm[:, e % 2, 0:P * (b + 1)]
                    w = wi2[:, b, j:j + 1]
                    if j == 0:
                        ins = dve.tensor_scalar(scx(b), r, w, None, ALU.mult)
                    else:
                        ins = dve.scalar_tensor_tensor(scx(b), r, w, scx(b), ALU.mult, ALU.add)
                    ins.then_inc(s["idx_acc"], 1)
                    e += 1
                    dve.wait_ge(s["idx_acc"], e)
            dve.wait_ge(s["ln_ps"], 1)
            for j in range(4):
                dve.scalar_tensor_tensor(cacc[:, j, :], B4[:, 0, :], -1.0 / CONV_CH, cacc[:, j, :], ALU.mult, ALU.add)\
                   .then_inc(s["lnc_done"], 1)
            dve.wait_ge(s["lnc_done"], 4)
            dve.memset(mx[:, 0:1], 0.0).then_inc(s["ln_read"], 1)
            dve.wait_ge(s["lnr_done"], 1)
            for j in range(4):
                dve.scalar_tensor_tensor(cacc[:, j, :], cacc[:, j, :], v("ln_g", j), lnr[:, :], ALU.mult, ALU.mult)\
                   .then_inc(s["lnx_done"], 1)
            for j in range(4):
                dve.wait_ge(s["ch_done"], j + 1)
                dve.tensor_tensor(cl[:, j, :], lnt[:, j % 2, :], ch[:, j, :].bitcast(F32), ALU.subtract)\
                   .then_inc(s["cl_done"], 1)

            dve.wait_ge(s["caus_in"], 16)
            dve.wait_ge(s["dtab_in"], 16)

            def select(b, part):
                x = scx(b)
                if part == 0:
                    diag = x[:, P * b:P * (b + 1)]
                    link(dve.tensor_tensor(diag, diag, caus[:, :], ALU.add))
                for _ in range(TOPK // 64):
                    link(dve.max(top8, x))
                    link(dve.match_replace(x, top8, x, TAKEN))
                if part == 7:
                    link(dve.tensor_scalar(x, x, TAKEN / 2, -1e30, ALU.is_gt, ALU.mult))

            def soft2(q):
                b, hh = q // 8, q % 8
                W = P * (b + 1)
                dve.wait_ge(s["s2_ps"], q + 1)
                if q >= 3:
                    dve.wait_ge(s["t2_ps"], q - 2)
                x = S2[:, q % 3, 0:W]
                link(dve.scalar_tensor_tensor(x, dtab[:, 384 - P * b:384 - P * b + W], 2.0 ** -(hh + 1),
                                              scx(b) if b else caus[:, :], ALU.mult, ALU.add))
                dve.scalar_tensor_tensor(x, B4[:, q % 2, 0:W], 64 ** -0.5, x, ALU.mult, ALU.add).then_inc(s["s2_read"], 1)
                dve.wait_ge(s["s2_read"], q + 1)
                link(dve.tensor_reduce(mx[:, 0:1], x, AX.X, ALU.max))
                dve.tensor_scalar(nmx[:, q % 3:q % 3 + 1], mx[:, 0:1], -1.0, None, ALU.mult).then_inc(s["nmx2"], 1)
                dve.wait_ge(s["nmx2"], q + 1)

            for q in range(37):
                if q < 32:
                    soft2(q)
                    if q < 24:
                        select(q // 8 + 1, q % 8)
                if q >= 10 and q % 8 == 2:
                    b = q // 8 - 1
                    dve.wait_ge(s["p2_done"], 8 * b + 8)
                    dve.reciprocal(rinv, row_sum[:, b % 2, :]).then_inc(s["rinv2"], 1)
                    dve.wait_ge(s["rinv2"], b + 1)
                    dve.wait_ge(s["o2_ps"], 8 * b + 8)
                    dve.tensor_tensor(otok2[:, :].rearrange("p (h e) -> p h e", h=8),
                                      B4[:, 2 + b % 2, :].rearrange("p (h e) -> p h e", h=8),
                                      rinv.unsqueeze(2).broadcast_to([P, 8, 64]), ALU.mult).then_inc(s["otok2_done"], 1)
                if q >= 12 and q % 8 == 4:
                    b = q // 8 - 1
                    dve.wait_ge(s["ah_done"], 4 * b + 4)
                    for f in range(4):
                        dve.tensor_tensor(al[:, f, P * b:P * (b + 1)], B4[:, 2 + b % 2, f * P:(f + 1) * P],
                                          ah[:, f, P * b:P * (b + 1)].bitcast(F32), ALU.subtract).then_inc(s["al_done"], 1)

            dve.wait_ge(s["sga_done"], 1)
            for i in range(4):
                dve.wait_ge(s["evac_done"], T0["proj2"] + 4 * (i + 1))
                dve.wait_ge(s["sgb_done"], i // 2 + 1)
                for ct in range(2):
                    c = 2 * i + ct
                    dve.tensor_tensor(yab[:, ct, :], yab[:, ct, :], sga[:, c, :], ALU.mult)
                    link(dve.tensor_tensor(yab[:, 2 + ct, :], yab[:, 2 + ct, :], sgb[c // 4][:, c % 4, :], ALU.mult))
                    dve.tensor_tensor(yab[:, ct, :], yab[:, ct, :], yab[:, 2 + ct, :], ALU.add).then_inc(s["mrg_done"], 1)
                for ct in range(2):
                    c = 2 * i + ct
                    dve.wait_ge(s["mh_done"], c + 1)
                    dve.tensor_tensor(ml[:, c, :], yab[:, ct, :], mh[:, c, :].bitcast(F32), ALU.subtract)\
                       .then_inc(s["ml_done"], 1)

            def add_residual(name, rt, norm):
                for c in range(KD):
                    dve.wait_ge(s["evac_done"], T0[name] + c + 1)
                    dve.tensor_tensor(h[:, c, META:T], h[:, c, META:T], rt[:, c % 2, :], ALU.add).then_inc(s["h_done"], 1)
                    if c >= 2:
                        add_square(norm, c - 1)
                add_square(norm, KD - 1)

            add_residual("out2", rt, "ffn2")
            normalise("ffn2", "ffn2", 0, META, lambda k: gf2[:, k:k + 1], lambda k: mod[:, 24 + k:25 + k])

            def ffn2_dve(p, x):
                dve.wait_ge(s["evac_done"], 2 * p + (T0["ffn_in2"] + 2))
                gated(p, x, JF)

            for p in range(4):
                ffn2_dve(p, p % 3)
            with dve.Fori(0, (JF - 4) // 3) as i:
                for r in range(3):
                    ffn2_dve(3 * i + 4 + r, (4 + r) % 3)
            add_residual("ffn_out2", tv, "final")
            dve.wait_ge(s["rstd_done"], 7)
            for k in range(KD):
                dve.scalar_tensor_tensor(res[:, k, :], h[:, k, META:T], v("final", k), rstd2[:, 0:SEQ], ALU.mult, ALU.mult)\
                   .then_inc(s["res_done"], 1)


def _columns(w, cols):
    cols = list(cols)
    units = []
    for i in range(0, len(cols), P):
        c = cols[i:i + P]
        u = np.zeros((P, KD, P), np.float32)
        u[:, :, :len(c)] = w[:, c].reshape(KD, P, len(c)).transpose(1, 0, 2)
        units.append(u.reshape(P, KD * P))
    return units


def _deep(w):
    units = []
    for c in range(KD):
        b = np.zeros((24, P, P), np.float32)
        b[:JF] = w[:, c * P:(c + 1) * P].reshape(JF, P, P)
        units += list(b.reshape(3, BLK, P, P).transpose(0, 2, 1, 3).reshape(3, P, BLK * P))
    return units


def _shallow(w, i):
    return w[:, 256 * i:256 * (i + 1)].reshape(4, P, 2, P).transpose(1, 2, 0, 3).reshape(P, BLK * P)


def layout(x):
    f = {k: np.asarray(a) for k, a in x.items()}
    w1, w2 = f["w_in"][0], f["w_in_2"][0]
    o = np.cumsum([0, 512, 512, 512, 256, 256, 512, 512, 32])
    r = lambda a, n=None: range(o[a], o[a + 1])
    stream = _columns(w1, r(7)) + _columns(w1, r(3)) + _columns(w1, r(4)) + _columns(w1, r(5))
    stream += _columns(w1, r(0)) + _columns(w1, r(1)) + _columns(w1, r(2)) + _columns(w1, r(6))
    stream += _columns(f["w_o"][0], range(D))
    ffn = [c for j in range(JF) for half in (0, DFF) for c in range(half + P * j, half + P * (j + 1))]
    stream += _columns(f["w_ffn_in"][0], ffn) + _deep(f["w_ffn_out"][0])
    q2, k2, v2, qi, ki, wi, u2, ga, gb = np.cumsum([0, 512, 512, 512, 512, 64, 8, 1024, 1024])
    span = lambda a, n: range(a, a + n)
    stream += _columns(w2, [c for j in range(4) for half in (0, CONV_CH) for c in span(u2 + half + P * j, P)])
    stream += _columns(w2, span(qi, 512)) + _columns(w2, list(span(ki, 64)) * 2) + _columns(w2, span(wi, 8))
    stream += _columns(w2, span(q2, 512)) + _columns(w2, span(k2, 512)) + _columns(w2, span(v2, 512))
    stream += _columns(w2, span(ga, 1024)) + _columns(w2, span(gb, 1024))
    for i in range(4):
        stream += [_shallow(f["w_attn_proj_2"][0], i), _shallow(f["w_conv_proj_2"][0], i)]
    stream += _columns(f["w_out_2"][0], range(D))
    stream += _columns(f["w_ffn_in_2"][0], ffn) + _deep(f["w_ffn_out_2"][0])
    stream = np.stack(stream[:NUNIT])

    h = np.concatenate([f["meta_tokens"], f["x"][0]], axis=0)
    h = np.ascontiguousarray(h.T.reshape(KD, P, T).transpose(1, 0, 2))
    col = lambda a: np.asarray(a).reshape(-1, P).T
    vecs = {"mix_pre": f["norm_mix_pre"], "na_gain": f["na_out_gain"],
            "gate_bias": np.concatenate([f["gla_gate_bias_fwd"], f["gla_gate_bias_bwd"]], 1),
            "gla_gain": f["gla_out_gain"], "mix_post": f["norm_mix_post"], "ffn_pre": f["norm_ffn_pre"],
            "cw": f["ffn_conv_w"], "cb": f["ffn_conv_b"], "ffn_post": f["norm_ffn_post"],
            "mix2": f["norm_mix_g_2"], "w_dw": f["w_dw_2"], "b_dw": f["b_dw_2"], "ln_g": f["conv_ln_g_2"],
            "ln_b": f["conv_ln_b_2"], "ffn2": f["norm_ffn_g_2"], "b_ada": f["b_ada_2"],
            "final": f["norm_final_g_2"], "c": f["c_2"], "eps": np.full((1, P), EPS, np.float32)}
    pairs = lambda a: np.asarray(a).reshape(-1, 2, JF, P).transpose(0, 2, 1, 3)
    vecs["cw"], vecs["cb"] = pairs(vecs["cw"]), pairs(vecs["cb"])
    vecs = np.ascontiguousarray(np.concatenate([col(vecs[n]) for n, _ in VECS], 1))
    assert vecs.shape[1] == NVEC

    p = np.arange(P)
    ident = np.eye(P, dtype=np.float32)
    onesm = np.ones((P, P), np.float32)
    wmask = np.zeros((P, 4, 48), np.float32)
    for a in range(4):
        lo, W = na_window(a)
        c, key = 16 * a + p // 8, lo + np.arange(W)
        first = np.clip(c - 8, 0, GRID_W - 16)
        seen = (key[None] >= first[:, None]) & (key[None] < first[:, None] + 16)
        wmask[:, a, :W] = np.where(seen, 0.0, -1e30)
    causal = np.where(p[None] <= p[:, None], 0.0, -1e30).astype(np.float32)
    dist = (np.arange(896)[None] - 384 - p[:, None]).astype(np.float32)
    consts = np.ascontiguousarray(np.concatenate([ident, onesm, wmask.reshape(P, -1), causal, dist], 1))
    same = (p[:, None] // CHUNK) == (p[None] // CHUNK)
    masks = np.stack([same & (p[:, None] <= p[None]), same & (p[:, None] > p[None])], 1).astype(np.int32)
    keep = np.ones((P, 2, T), np.float32)
    keep[:, 0, META::CHUNK] = 0.0
    keep[:, 1, META - 1::CHUNK] = 0.0

    rpb = np.zeros((NA_H, 15, 64), np.float32)
    rpb[:, :, 16:47] = f["na_rel_bias"][0]
    bias = np.zeros((P, NA_H, 48, 8), np.float32)
    for q in range(P):
        bias[q] = rpb[:, 7 - q % 8:15 - q % 8, 15 - q // 8:63 - q // 8].transpose(0, 2, 1)
    bias = bias.reshape(P, NA_H, 384)
    up = np.zeros((32, 512), np.float32)
    up[:RANK, :256] = f["gla_gate_up_fwd"][0]
    up[RANK:, 256:] = f["gla_gate_up_bwd"][0]
    ada = np.ascontiguousarray(f["w_ada_2"][0].reshape(KD, P, NMOD, D).transpose(0, 2, 1, 3).reshape(-1, P, D))
    return {"wstream": stream, "ada": ada, "hT": h, "vecs": vecs, "consts": consts, "masks": masks,
            "scanm": keep, "bias": bias, "up": up}


def kernel(**inputs):
    import concourse.bacc as bacc
    from concourse.bass_utils import run_bass_kernel_spmd

    arrays = layout(inputs)
    nc = bacc.Bacc("TRN2", target_bir_lowering=False, num_devices=1)
    aps = {n: nc.dram_tensor(n, a.shape, mybir.dt.from_np(a.dtype), kind="ExternalInput").ap()
           for n, a in arrays.items()}
    out = nc.dram_tensor("out", (P, KD, SEQ), F32, kind="ExternalOutput").ap()
    build(nc, out=out, **aps)
    result = run_bass_kernel_spmd(nc, [arrays], core_ids=[0]).results[0]["out"]
    return np.ascontiguousarray(np.asarray(result).transpose(2, 1, 0).reshape(1, SEQ, D))
```
